# Optimizing a Trainium2 kernel written in Bass

```python
import jax, jax.numpy as jnp
from jax import lax
import numpy as np

D_MODEL = 1024
BATCH = 1
SEQ = 1024
DEPTH = 1
DEC_BATCH = 8
DEC_SEQ = 8
PAST_LEN = 256
PAGE_SIZE = 128

H_FOX = 8
DH_FOX = 64
FOX_BLOCK = 128
FOX_BIAS_CENTER = 2.0
H_GLA = 4
DK_GLA = 64
DV_GLA = 128
GLA_GATE_RANK = 16
GLA_TAU = 16.0
GLA_CHUNK = 64
N_MEM = 256
H_MEM = 4
DH_MEM = D_MODEL // H_MEM
N_KEYS = 128
N_EXPERTS = N_KEYS * N_KEYS
H_PEER = 8
D_KEY = 256
PEER_TOPK = 16
PEER_BLOCK = 256

EPS = 1e-6
NEG_INF = -1e30
FOX_W = H_FOX * DH_FOX
GLA_KW = H_GLA * DK_GLA
GLA_VW = H_GLA * DV_GLA
MIX_W = FOX_W + GLA_VW
IN_SIZES = (FOX_W, FOX_W, FOX_W, H_FOX, GLA_KW, GLA_KW, GLA_VW, GLA_GATE_RANK, GLA_VW)
D_IN = sum(IN_SIZES)

kernel_name = 'hybrid_fox_gla_peer_decoder_step'

def rmsnorm(x, g):
    xf = x.astype(jnp.float32)
    y = xf * lax.rsqrt(jnp.mean(xf * xf, axis=-1, keepdims=True) + EPS)
    return (y * g.astype(jnp.float32)).astype(x.dtype)

def mixer_inputs(h, w_in, b_fox_f, w_gla_gate2, b_gla_gate):
    B, L, _ = h.shape
    splits = [int(s) for s in np.cumsum(IN_SIZES)[:-1]]
    fq, fk, fv, ff, gq, gk, gv, gg, gr = jnp.split(h @ w_in, splits, axis=-1)
    fq = fq.reshape(B, L, H_FOX, DH_FOX)
    fk = fk.reshape(B, L, H_FOX, DH_FOX)
    fv = fv.reshape(B, L, H_FOX, DH_FOX)
    logf = jax.nn.log_sigmoid((ff + b_fox_f).astype(jnp.float32))
    gq = gq.reshape(B, L, H_GLA, DK_GLA) * (DK_GLA ** -0.5)
    gk = gk.reshape(B, L, H_GLA, DK_GLA)
    gv = gv.reshape(B, L, H_GLA, DV_GLA)
    z = (gg @ w_gla_gate2 + b_gla_gate).astype(jnp.float32)
    log_a = (jax.nn.log_sigmoid(z) / GLA_TAU).reshape(B, L, H_GLA, DK_GLA)
    return fq, fk, fv, logf, gq, gk, gv, log_a, gr

def fox_prompt(q, k, v, logf):
    B, L, H, Dh = q.shape
    scale = Dh ** -0.5
    c_t = jnp.cumsum(logf, axis=1).transpose(0, 2, 1)
    nb = L // FOX_BLOCK
    qb = q.reshape(B, nb, FOX_BLOCK, H, Dh).transpose(1, 0, 2, 3, 4)
    cb = c_t.reshape(B, H, nb, FOX_BLOCK).transpose(2, 0, 1, 3)
    starts = jnp.arange(nb, dtype=jnp.int32) * FOX_BLOCK
    k_pos = jnp.arange(L, dtype=jnp.int32)

    def block(args):
        qi, ci, s0 = args
        s = jnp.einsum('bqhd,bkhd->bhqk', qi, k).astype(jnp.float32) * scale
        s = s + ci[..., :, None] - c_t[:, :, None, :]
        q_pos = s0 + jnp.arange(FOX_BLOCK, dtype=jnp.int32)
        s = jnp.where(k_pos[None, :] <= q_pos[:, None], s, NEG_INF)
        p = jax.nn.softmax(s, axis=-1).astype(v.dtype)
        return jnp.einsum('bhqk,bkhd->bqhd', p, v)

    o = lax.map(block, (qb, cb, starts))
    return o.transpose(1, 0, 2, 3, 4).reshape(B, L, H * Dh)

def fox_sample(q, k, v, logf, k_past, v_past, logf_past):
    B, L, H, Dh = q.shape
    P = k_past.shape[1]
    scale = Dh ** -0.5
    c_past = jnp.cumsum(logf_past.astype(jnp.float32), axis=1).transpose(0, 2, 1)
    c_new = c_past[:, :, -1:] + jnp.cumsum(logf, axis=1).transpose(0, 2, 1)
    s_past = jnp.einsum('bqhd,bkhd->bhqk', q, k_past).astype(jnp.float32) * scale
    s_past = s_past + c_new[..., :, None] - c_past[:, :, None, :]
    s_new = jnp.einsum('bqhd,bkhd->bhqk', q, k).astype(jnp.float32) * scale
    s_new = s_new + c_new[..., :, None] - c_new[:, :, None, :]
    s_new = jnp.where(jnp.tril(jnp.ones((L, L), dtype=bool)), s_new, NEG_INF)
    p = jax.nn.softmax(jnp.concatenate([s_past, s_new], axis=-1), axis=-1).astype(v.dtype)
    o = jnp.einsum('bhqk,bkhd->bqhd', p[..., :P], v_past) + jnp.einsum('bhqk,bkhd->bqhd', p[..., P:], v)
    return o.reshape(B, L, H * Dh)

def gla_chunk_size(L):
    return GLA_CHUNK if L % GLA_CHUNK == 0 else L

def gla_chunked(q, k, v, log_a, s0, chunk):
    B, L, H, dk = q.shape
    dv = v.shape[-1]
    n = L // chunk

    def blk(t):
        return t.astype(jnp.float32).reshape(B, n, chunk, H, t.shape[-1]).transpose(0, 3, 1, 2, 4)

    q, k, v, la = blk(q), blk(k), blk(v), blk(log_a)
    b = jnp.cumsum(la, axis=3)
    b_last = b[:, :, :, -1:, :]
    q_dec = q * jnp.exp(b)
    att = jnp.einsum('bhncd,bhnsd->bhncs', q_dec, k * jnp.exp(-b))
    att = jnp.where(jnp.tril(jnp.ones((chunk, chunk), dtype=bool)), att, 0.0)
    o_intra = jnp.einsum('bhncs,bhnse->bhnce', att, v)
    chunk_kv = jnp.einsum('bhnsd,bhnse->nbhde', k * jnp.exp(b_last - b), v)
    decay = jnp.exp(b_last[:, :, :, 0, :]).transpose(2, 0, 1, 3)

    def step(S, inp):
        dec, kv = inp
        return dec[..., None] * S + kv, S

    s_final, s_prev = lax.scan(step, s0.astype(jnp.float32), (decay, chunk_kv))
    o_inter = jnp.einsum('bhncd,nbhde->bhnce', q_dec, s_prev)
    o = (o_intra + o_inter).transpose(0, 2, 3, 1, 4).reshape(B, L, H, dv)
    return o, s_final

def mix_out(fox_o, gla_o, gr, g_gla_out, w_out):
    B, L = fox_o.shape[:2]
    gla_n = rmsnorm(gla_o, g_gla_out.reshape(H_GLA, DV_GLA)).reshape(B, L, GLA_VW)
    gla_n = gla_n * jax.nn.silu(gr.astype(jnp.float32))
    merged = jnp.concatenate([fox_o, gla_n.astype(fox_o.dtype)], axis=-1)
    return merged @ w_out

def memory_kv(mem, g_mem, w_mem_k, w_mem_v):
    B, M, _ = mem.shape
    m = rmsnorm(mem, g_mem)
    return (m @ w_mem_k).reshape(B, M, H_MEM, DH_MEM), (m @ w_mem_v).reshape(B, M, H_MEM, DH_MEM)

def cross_attn(h, mk, mv, w_q, w_o):
    B, L, _ = h.shape
    q = (h @ w_q).reshape(B, L, H_MEM, DH_MEM)
    s = jnp.einsum('blhd,bmhd->bhlm', q, mk).astype(jnp.float32) * (DH_MEM ** -0.5)
    p = jax.nn.softmax(s, axis=-1).astype(mv.dtype)
    o = jnp.einsum('bhlm,bmhd->blhd', p, mv).reshape(B, L, H_MEM * DH_MEM)
    return o @ w_o

def peer_ffn(h, w_q, subkeys, u, v):
    shp = h.shape
    hf = h.reshape(-1, shp[-1])
    T = hf.shape[0]
    pad = (-T) % PEER_BLOCK
    hp = jnp.pad(hf, ((0, pad), (0, 0))).reshape(-1, PEER_BLOCK, shp[-1])

    def block(hb):
        q = (hb @ w_q).reshape(PEER_BLOCK, H_PEER, 2, D_KEY // 2)
        s1 = jnp.einsum('thd,kd->thk', q[:, :, 0], subkeys[0]).astype(jnp.float32)
        s2 = jnp.einsum('thd,kd->thk', q[:, :, 1], subkeys[1]).astype(jnp.float32)
        v1, i1 = lax.top_k(s1, PEER_TOPK)
        v2, i2 = lax.top_k(s2, PEER_TOPK)
        cand = (v1[..., :, None] + v2[..., None, :]).reshape(PEER_BLOCK, H_PEER, PEER_TOPK * PEER_TOPK)
        sc, ci = lax.top_k(cand, PEER_TOPK)
        e = (jnp.take_along_axis(i1, ci // PEER_TOPK, axis=-1) * N_KEYS
             + jnp.take_along_axis(i2, ci % PEER_TOPK, axis=-1))
        g = jax.nn.softmax(sc, axis=-1)
        a = jax.nn.gelu(jnp.einsum('thkd,td->thk', u[e], hb).astype(jnp.float32))
        w = (g * a).astype(hb.dtype)
        return jnp.einsum('thk,thkd->td', w, v[e])

    out = lax.map(block, hp).reshape(-1, shp[-1])[:T]
    return out.reshape(shp)

def setup_inputs(seed: int = 0) -> dict:
    key = jax.random.key(seed)
    ks = iter(jax.random.split(key, 32))

    def nrm(shape, scale):
        return jax.random.normal(next(ks), shape, jnp.float32) * scale

    def gain(shape):
        return 1.0 + nrm(shape, 0.02)

    n_pages = PAST_LEN // PAGE_SIZE
    n_pool = (DEC_BATCH * n_pages * 5) // 4
    x_prompt = nrm((BATCH, SEQ, D_MODEL), 1.0)
    x_sample = nrm((DEC_BATCH, DEC_SEQ, D_MODEL), 1.0)
    cache_fox_k = nrm((DEPTH, n_pool, PAGE_SIZE, H_FOX, DH_FOX), 1.0)
    cache_fox_v = nrm((DEPTH, n_pool, PAGE_SIZE, H_FOX, DH_FOX), 1.0)
    cache_fox_logf = jax.nn.log_sigmoid(FOX_BIAS_CENTER + nrm((DEPTH, n_pool, PAGE_SIZE, H_FOX), 1.0))
    state_gla = nrm((DEPTH, DEC_BATCH, H_GLA, DK_GLA, DV_GLA), 1.0)
    cache_mem_k = nrm((DEPTH, DEC_BATCH, N_MEM, H_MEM, DH_MEM), 1.0)
    cache_mem_v = nrm((DEPTH, DEC_BATCH, N_MEM, H_MEM, DH_MEM), 1.0)
    page_table = jax.random.permutation(next(ks), n_pool)[:DEC_BATCH * n_pages]
    page_table = page_table.reshape(DEC_BATCH, n_pages).astype(jnp.int32)
    mem_prompt = nrm((BATCH, N_MEM, D_MODEL), 1.0)
    return {
        'x_prompt': x_prompt,
        'x_sample': x_sample,
        'cache_fox_k': cache_fox_k,
        'cache_fox_v': cache_fox_v,
        'cache_fox_logf': cache_fox_logf,
        'state_gla': state_gla,
        'cache_mem_k': cache_mem_k,
        'cache_mem_v': cache_mem_v,
        'page_table': page_table,
        'mem_prompt': mem_prompt,
        'g_mix': gain((DEPTH, D_MODEL)),
        'w_in': nrm((DEPTH, D_MODEL, D_IN), D_MODEL ** -0.5),
        'b_fox_f': FOX_BIAS_CENTER + nrm((DEPTH, H_FOX), 0.1),
        'w_gla_gate2': nrm((DEPTH, GLA_GATE_RANK, GLA_KW), GLA_GATE_RANK ** -0.5),
        'b_gla_gate': nrm((DEPTH, GLA_KW), 0.1),
        'g_gla_out': gain((DEPTH, GLA_VW)),
        'w_out': nrm((DEPTH, MIX_W, D_MODEL), MIX_W ** -0.5),
        'g_cross': gain((DEPTH, D_MODEL)),
        'g_mem': gain((DEPTH, D_MODEL)),
        'w_mem_k': nrm((DEPTH, D_MODEL, H_MEM * DH_MEM), D_MODEL ** -0.5),
        'w_mem_v': nrm((DEPTH, D_MODEL, H_MEM * DH_MEM), D_MODEL ** -0.5),
        'w_cross_q': nrm((DEPTH, D_MODEL, H_MEM * DH_MEM), D_MODEL ** -0.5),
        'w_cross_o': nrm((DEPTH, H_MEM * DH_MEM, D_MODEL), D_MODEL ** -0.5),
        'g_ffn': gain((DEPTH, D_MODEL)),
        'peer_w_q': nrm((DEPTH, D_MODEL, H_PEER * D_KEY), D_MODEL ** -0.5),
        'peer_subkeys': nrm((DEPTH, 2, N_KEYS, D_KEY // 2), (D_KEY // 2) ** -0.5),
        'peer_u': nrm((DEPTH, N_EXPERTS, D_MODEL), D_MODEL ** -0.5),
        'peer_v': nrm((DEPTH, N_EXPERTS, D_MODEL), D_MODEL ** -0.5),
        'g_final': gain((D_MODEL,)),
    }

def reference(x_prompt, x_sample, cache_fox_k, cache_fox_v, cache_fox_logf, state_gla,
              cache_mem_k, cache_mem_v, page_table, mem_prompt, g_mix, w_in, b_fox_f,
              w_gla_gate2, b_gla_gate, g_gla_out, w_out, g_cross, g_mem, w_mem_k, w_mem_v,
              w_cross_q, w_cross_o, g_ffn, peer_w_q, peer_subkeys, peer_u, peer_v, g_final):
    xp, xs = x_prompt, x_sample
    Bp, Lp = xp.shape[:2]
    Bs, Ls = xs.shape[:2]
    fk_p, fv_p, fl_p, gs_p, mk_p, mv_p = [], [], [], [], [], []
    fk_s, fv_s, fl_s, gs_s = [], [], [], []
    for l in range(DEPTH):
        h = rmsnorm(xp, g_mix[l])
        fq, fk, fv, logf, gq, gk, gv, log_a, gr = mixer_inputs(h, w_in[l], b_fox_f[l], w_gla_gate2[l], b_gla_gate[l])
        fox_o = fox_prompt(fq, fk, fv, logf)
        s0 = jnp.zeros((Bp, H_GLA, DK_GLA, DV_GLA), jnp.float32)
        gla_o, s_fin = gla_chunked(gq, gk, gv, log_a, s0, gla_chunk_size(Lp))
        xp = xp + mix_out(fox_o, gla_o, gr, g_gla_out[l], w_out[l])
        mk, mv = memory_kv(mem_prompt, g_mem[l], w_mem_k[l], w_mem_v[l])
        xp = xp + cross_attn(rmsnorm(xp, g_cross[l]), mk, mv, w_cross_q[l], w_cross_o[l])
        xp = xp + peer_ffn(rmsnorm(xp, g_ffn[l]), peer_w_q[l], peer_subkeys[l], peer_u[l], peer_v[l])
        fk_p.append(fk)
        fv_p.append(fv)
        fl_p.append(logf)
        gs_p.append(s_fin)
        mk_p.append(mk)
        mv_p.append(mv)
        h = rmsnorm(xs, g_mix[l])
        fq, fk, fv, logf, gq, gk, gv, log_a, gr = mixer_inputs(h, w_in[l], b_fox_f[l], w_gla_gate2[l], b_gla_gate[l])
        k_past = cache_fox_k[l][page_table].reshape(Bs, -1, H_FOX, DH_FOX)
        v_past = cache_fox_v[l][page_table].reshape(Bs, -1, H_FOX, DH_FOX)
        lf_past = cache_fox_logf[l][page_table].reshape(Bs, -1, H_FOX)
        fox_o = fox_sample(fq, fk, fv, logf, k_past, v_past, lf_past)
        gla_o, s_new = gla_chunked(gq, gk, gv, log_a, state_gla[l], gla_chunk_size(Ls))
        xs = xs + mix_out(fox_o, gla_o, gr, g_gla_out[l], w_out[l])
        xs = xs + cross_attn(rmsnorm(xs, g_cross[l]), cache_mem_k[l], cache_mem_v[l], w_cross_q[l], w_cross_o[l])
        xs = xs + peer_ffn(rmsnorm(xs, g_ffn[l]), peer_w_q[l], peer_subkeys[l], peer_u[l], peer_v[l])
        fk_s.append(fk)
        fv_s.append(fv)
        fl_s.append(logf)
        gs_s.append(s_new)
    y_prompt = rmsnorm(xp, g_final)
    y_sample = rmsnorm(xs, g_final)
    return (y_prompt, y_sample,
            jnp.stack(fk_p, axis=0), jnp.stack(fv_p, axis=0), jnp.stack(fl_p, axis=0),
            jnp.stack(gs_p, axis=0), jnp.stack(mk_p, axis=0), jnp.stack(mv_p, axis=0),
            jnp.stack(fk_s, axis=0), jnp.stack(fv_s, axis=0), jnp.stack(fl_s, axis=0),
            jnp.stack(gs_s, axis=0))


_drawn_inputs = setup_inputs


def setup_inputs(seed=0):
    import zlib

    import numpy as np

    out = dict(_drawn_inputs(seed))
    spreads = {}
    factors = {'g_gla_out': 7.485,
     'g_cross': 8.0,
     'g_mem': 2.905,
     'g_ffn': 8.0,
     'peer_w_q': 4.213,
     'peer_subkeys': 4.204,
     'peer_u': 4.668,
     'peer_v': 4.195,
     'g_final': 2.736}
    for name, (base, spread) in spreads.items():
        noise = np.random.default_rng([zlib.crc32(name.encode()), seed]).standard_normal(out[name].shape)
        drawn = base * np.exp(spread * noise) if base else spread * noise
        out[name] = __import__('jax').numpy.asarray(drawn.astype(out[name].dtype))
    for name, factor in factors.items():
        out[name] = (out[name] * factor).astype(out[name].dtype)
    return out
```

```python
from contextlib import ExitStack

import numpy as np

import concourse.bass as bass
from concourse import mybir

F32 = mybir.dt.float32
I32 = mybir.dt.int32
U32 = mybir.dt.uint32
BF16 = mybir.dt.bfloat16
ACT = mybir.ActivationFunctionType
ALU = mybir.AluOpType
AX = mybir.AxisListType

P = 128
D = 1024
KC = D // P
SEQ = 1024
TILES = SEQ // P
DEC_BATCH, DEC_SEQ = 8, 8
RS = DEC_BATCH * DEC_SEQ
N_PAGES = 2
H_FOX, DH = 8, 64
DA = DH + 2
H_GLA, DK, DV = 4, 64, 128
CHUNK = 64
NCH = P // CHUNK
RANK = 16
TAU = 16.0
N_MEM = 256
MC = N_MEM // P
H_MEM, DH_MEM = 4, 256
N_KEYS = 128
H_PEER = 8
TOPK = 16
SLOTS = H_PEER * TOPK
EPS = 1e-6
NEG = -1e30
LOWEST = -3.0e38
GKW = H_GLA * DK
NLS = H_FOX + GKW
OFF_FQ, OFF_FK, OFF_FV, OFF_FF = 0, 512, 1024, 1536
OFF_GQK, OFF_GV, OFF_GG, OFF_GR, D_IN = 1544, 2056, 2568, 2584, 3096
W = 512
GROUP = 8
UB = 4
VB = 4
WB = 2

MM_SETUP = [f"mem{m}{w}{c}" for w in "kv" for c in range(2) for m in range(MC)]
MM_PROMPT = ["fq", "fk", "fv", "gqk", "gv", "gr", "small", "gate", "cum", "cumg", "fo", "go",
             "cq0", "cq1", "cu0", "cu1", "pq0", "pq1", "pq2", "pq3"]
TP_SETUP = [f"mx{m}{c}" for m in range(MC) for c in range(2)] + [f"mk{m}{c}" for c in range(2) for m in range(MC)]
TP_PROMPT = (["x0", "x1", "q0", "q1", "k0", "k1", "gq", "gk"] + [f"P{h}{c}" for h in range(H_FOX) for c in range(2)]
             + ["m0", "m1", "h0", "h1", "p0", "p1", "f0", "f1"])
SC_PROMPT = ["gg"] + [f"s{h}" for h in range(H_FOX)] + ["gatt", "gkv", "wout", "xs", "wo", "ps0", "ps1"]
MM_SAMPLE = ["fq", "fk", "fv", "gqk", "gv", "gr", "small", "gate", "cpast", "cum", "cumg", "go", "fo",
             "cq0", "cq1", "cs", "cu0", "cu1", "pq0", "pq1", "pq2", "pq3"]
TP_SAMPLE = (["x0", "x1", "q0", "q1", "k0", "k1", "gq", "gk", "got"] + [f"S{i}" for i in range(4)]
             + [f"P{i}" for i in range(4)] + ["Pn", "fot", "m0", "m1", "h0", "h1", "c0", "c1", "p0", "p1", "f0", "f1"])
SC_SAMPLE = ["gg", "gatt"] + [f"kv{b}" for b in range(DEC_BATCH)] + ["past", "new", "wout", "wo", "ps0", "ps1"]


class Banks:

    def __init__(self, nc, ctx, name, depth, width, setup, prompt, sample):
        self.full = ctx.enter_context(nc.semaphore(f"{name}_full"))
        self.free = ctx.enter_context(nc.semaphore(f"{name}_free"))
        self.bank = [ctx.enter_context(nc.psum_tensor(f"{name}{i}", [P, width], F32)) for i in range(depth)]
        self.depth = depth
        self.plans = {"setup": setup, "prompt": prompt, "sample": sample}
        assert len(setup) % depth == 0 and len(prompt) % depth == 0

    def number(self, at, name):
        plan, t = at
        k = self.plans[plan].index(name)
        if plan == "setup":
            return k
        return len(self.plans["setup"]) + t * len(self.plans["prompt"]) + k

    def ap(self, at, name):
        return self.bank[self.plans[at[0]].index(name) % self.depth]

    def turn(self, at, name):
        return self.number(at, name) + 1

    def filled(self, at, name):
        return self.number(at, name) + 1

    def taken(self, at, name):
        return self.number(at, name) + 1 + self.depth


def build(nc, ins, outs):
    (x_all, page_table, past_kt, past_v, past_lf, state_in, smem_kt, smem_v, mem_prompt, g_cols, w_in, bias_ls, w_gate2,
     w_out, w_mem_k, w_mem_v, w_cross_q, w_cross_o, g_ffn, peer_w_q, subkeys_t, peer_u, peer_v, g_final) = (
        ins[n] for n in ("x_all page_table past_kt past_v past_lf state_in smem_kt smem_v mem_prompt g_cols w_in bias_ls "
                         "w_gate2 w_out w_mem_k w_mem_v w_cross_q w_cross_o g_ffn peer_w_q subkeys_t peer_u peer_v "
                         "g_final").split())
    with ExitStack() as ctx:
        def sb(name, shape, dt=F32):
            return ctx.enter_context(nc.sbuf_tensor(name, shape, dt))

        def sem(name):
            return ctx.enter_context(nc.semaphore(name))

        MM = Banks(nc, ctx, "mm", 2, 512, MM_SETUP, MM_PROMPT, MM_SAMPLE)
        TP = Banks(nc, ctx, "tp", 2, 512, TP_SETUP, TP_PROMPT, TP_SAMPLE)
        SC = Banks(nc, ctx, "sc", 1, 1024, [], SC_PROMPT, SC_SAMPLE)
        acc = ctx.enter_context(nc.psum_tensor("acc", [P, D], F32))

        kt_all = sb("kt_all", [P, H_FOX, SEQ])
        v_all = sb("v_all", [P, TILES, H_FOX * DH])
        mem_kt = sb("mem_kt", [P, KC, N_MEM])
        mem_v = sb("mem_v", [P, MC, D])
        state = sb("state", [DK, H_GLA, DV])
        carry = sb("carry", [P, H_FOX])
        ident = sb("ident", [P, P])
        causal = sb("causal", [P, 2 * SEQ - P], BF16)
        upper = sb("upper", [P, P])
        ones = sb("ones", [P, P])
        blk_up = sb("blk_up", [P, P])
        blk_one = sb("blk_one", [P, P])
        blk_ind = sb("blk_ind", [P, NCH])
        iota_k = sb("iota_k", [P, TOPK])
        eps_col = sb("eps_col", [P, 1])
        gains_t = sb("gains_t", [P, 3 * KC + H_GLA])
        g_ffn_bc = sb("g_ffn_bc", [P, D])
        g_fin_bc = sb("g_fin_bc", [P, D])
        bias_bc = sb("bias_bc", [P, NLS])
        gate2 = sb("gate2", [RANK, GKW])
        w_small = sb("w_small", [P, KC, H_FOX + RANK])
        same_up = sb("same_up", [RS, RS])
        same_one = sb("same_one", [RS, RS])
        same_ind = sb("same_ind", [RS, DEC_BATCH])
        same_low = sb("same_low", [RS, RS])
        same_mask = sb("same_mask", [RS, RS])
        row_no = sb("row_no", [P, 1])
        pages = sb("pages", [P, DEC_BATCH * N_PAGES], I32)
        page_rows = sb("page_rows", [P, DEC_BATCH * N_PAGES], I32)
        page_cols = sb("page_cols", [P, DEC_BATCH * N_PAGES], I32)
        lf_past = sb("lf_past", [P, DEC_BATCH, N_PAGES, H_FOX])
        c_past = sb("c_past", [P, N_PAGES, DEC_BATCH, H_FOX])
        c_last = sb("c_last", [RS, DEC_BATCH, H_FOX])
        c_rows = sb("c_rows", [RS, H_FOX])
        decay_s = sb("decay_s", [DK, H_GLA * DEC_BATCH])
        sub_t = sb("sub_t", [P, 2, N_KEYS])
        w_ring = sb("w_ring", [P, WB, KC, W])
        u_ring = sb("u_ring", [P, UB, D])
        v_ring = sb("v_ring", [P, VB, D])
        xr = sb("xr", [P, D])
        xs = sb("xs", [P, D])
        h_t = sb("h_t", [P, KC, P])
        hb = sb("hb", [P, D])
        q_aug = sb("q_aug", [P, H_FOX, DA])
        k_aug = sb("k_aug", [P, H_FOX, DA])
        gqk = sb("gqk", [P, 2 * GKW])
        gv = sb("gv", [P, H_GLA * DV])
        silu_r = sb("silu_r", [P, H_GLA * DV])
        gg = sb("gg", [P, RANK])
        gg_t = sb("gg_t", [RANK, P])
        lf = sb("lf", [P, NLS])
        cums = sb("cums", [P, 2 * H_FOX])
        gb = sb("gb", [P, GKW])
        q_dec = sb("q_dec", [P, GKW])
        k_neg = sb("k_neg", [P, GKW])
        k_dl = sb("k_dl", [P, GKW])
        decay = sb("decay", [DK, H_GLA * NCH])
        att_t = sb("att_t", [P, H_GLA, P])
        stats = sb("stats", [P, 64])
        work = sb("work", [P, 5120])
        gates = sb("gates", [P, SLOTS])
        experts = sb("experts", [P, SLOTS], I32)
        stage = sb("stage", [P, 2, GROUP], I32)
        dots = sb("dots", [P, 2, GROUP])
        gelu = sb("gelu", [P, 2, GROUP])
        wts = sb("wts", [P, 2, GROUP])
        gsum = sb("gsum", [P, H_PEER])
        ginv = sb("ginv", [P, H_PEER])

        g_mix_c, g_cross_c, g_mem_c = (gains_t[:, i * KC:(i + 1) * KC] for i in range(3))
        g_gla_c = gains_t[:, 3 * KC:3 * KC + H_GLA]
        SSQ, STD, RSTD, FMAX, FSUM, FINV, GSS, GSTD, GINV, CMAX, CSUM, CINV = (
            0, 1, 2, 8, 16, 24, 32, 36, 40, 44, 48, 52)
        probs = [work[:, i * D:(i + 1) * D] for i in range(2)]
        p_t = work[:, 2 * D:3 * D].rearrange("p (j q) -> p j q", j=KC)
        c_qt = work[:, 3 * D:4 * D].rearrange("p (j q) -> p j q", j=KC)
        pq_t = work[:, 3 * D:5 * D].rearrange("p (j q) -> p j q", j=2 * H_PEER)
        mem_t = work[:, 0:2 * D].rearrange("p (j m) -> p j m", j=KC)
        mem_k_rows = work[:, 2 * D:4 * D].rearrange("p (m c n) -> p m c n", m=MC, c=2)
        zz, zl = xs[:, 0:NLS], xs[:, NLS:2 * NLS]
        state1 = work[0:DK, D:D + W].rearrange("p (h v) -> p h v", h=H_GLA)
        diag = work[:, 0:D].rearrange("p (s q) -> p s q", s=GROUP)
        mask = h_t[:, 0:4, :].rearrange("p a b -> p (a b)").bitcast(BF16)
        q_t = work[0:DA, 3 * D:4 * D].rearrange("p (h q) -> p h q", h=H_FOX)
        qd_t = work[0:DK, 4 * D:4 * D + W].rearrange("p (h q) -> p h q", h=H_GLA)
        kn_t = work[0:DK, 4 * D + W:5 * D].rearrange("p (h q) -> p h q", h=H_GLA)
        lists = lambda a, shape: a.rearrange("p (a b) -> p a b", a=shape[0])
        vals = lists(gqk[:, 0:256], (2 * H_PEER, TOPK))
        indf = lists(gqk[:, 256:512], (2 * H_PEER, TOPK))
        half_f = lists(gv[:, 0:256], (2, SLOTS))
        picked = lists(gv[:, 256:512], (2, SLOTS))
        inds = lists(silu_r[:, 0:256].bitcast(U32), (2 * H_PEER, TOPK))
        best = lists(silu_r[:, 256:384], (H_PEER, TOPK))
        besti = lists(silu_r[:, 384:512].bitcast(U32), (H_PEER, TOPK))
        half_i = lists(gb[:, :].bitcast(U32), (2, SLOTS))
        mem_rows = [v_all[:, 2 * m:2 * m + 2, :].rearrange("p c n -> p (c n)") for m in range(MC)]
        states_s = v_all[0:DK].rearrange("p t n -> p (t n)").rearrange("p (s v) -> p s v", v=DV)
        big = kt_all[:].rearrange("p h k -> p (h k)")
        past_values = big.rearrange("p (n c) -> p n c", c=H_FOX * DH)
        past_keys = [u_ring[0:DH, i, :].rearrange("p (h k) -> p h k", h=H_FOX) for i in range(UB)]
        s_mem_k = [big[:, i * 2 * D:(i + 1) * 2 * D].rearrange("p (j m) -> p j m", j=KC) for i in range(2)]
        s_mem_v = [big[:, (2 + i) * 2 * D:(3 + i) * 2 * D].rearrange("p (m n) -> p m n", m=MC) for i in range(2)]
        flat_v = v_ring[0:RS].rearrange("p s n -> p (s n)")
        k_masked = flat_v[:, 0:DEC_BATCH * GKW].rearrange("p (b n) -> p b n", b=DEC_BATCH)
        NK_S = N_PAGES * P + RS
        s_rows = flat_v[:, 0:H_FOX * NK_S].rearrange("p (h k) -> p h k", h=H_FOX)
        past_scores = work[:, 0:D].rearrange("p (s q) -> p s q", q=RS)
        past_p_t = past_scores
        k_new_t = work[0:DA, D:2 * D].rearrange("p (h q) -> p h q", h=H_FOX)
        go_t = work[:, 2 * D:2 * D + H_GLA * RS].rearrange("p (h q) -> p h q", q=RS)
        new_p_t = work[0:RS, 2 * D:2 * D + W].rearrange("p (h q) -> p h q", q=RS)
        cs_t = work[:, 2 * D:2 * D + W].rearrange("p (s q) -> p s q", q=RS)
        v_new = work[0:RS, 2 * D + W:3 * D]
        fo_t = work[0:DH, 3 * D:3 * D + W].rearrange("p (h q) -> p h q", q=RS)
        rest = work[:, 0:D].rearrange("p (j q) -> p j q", j=KC)
        cand = work[:, D:3 * D]
        cand2 = work[:, 3 * D:5 * D]

        names = ("page_idx c_sub s_sub s_exp fo_norm k_masked past_q new_kt smk_used smv_used past_kept mask preset made copied consts mem_ss mem_xs std_x xs_x zmin lnz lf gdiff aug_cols q_dec gexpl k_dl fox_sub fox_exp "
                 "finv gstd merged std_2 xs_2 c_exp p_norm std_3 hb_rows gate_sub gate_exp experts staged gelu "
                 "wts diag acc_set state1 u_free v_free acc_free std_y y_rows").split()
        done = {n: sem(n) for n in names}
        land = {n: sem("landed_" + n) for n in "x mem page gains ffn fin bias gate2 small sub past_kt0 past_kt1 past_v past_lf s_state smk0 smk1 smv0 smv1".split()}
        w_land = [sem(f"w_land{i}") for i in range(WB)]
        u_land = [sem(f"u_land{i}") for i in range(UB)]
        v_land = [sem(f"v_land{i}") for i in range(VB)]
        land_s = {n: sem("landed_" + n) for n in ("state_s", "lf_past", "pages", "values_past")}
        key_land = [sem(f"key_land{i}") for i in range(UB)]
        smk_land = [sem(f"smk_land{i}") for i in range(2)]
        smv_land = [sem(f"smv_land{i}") for i in range(2)]
        out_sem = {n: sem("stored_" + n) for n in "fk fv lf y gs mk0 mk1 mv0 mv1".split()}

        def apart(eng):
            eng.sem_inc(done["copied"], 1)

        block = ctx.enter_context(nc.Block())

        chunks = ([(w_in, o) for o in (OFF_FQ, OFF_FK, OFF_FV, OFF_GQK, OFF_GV, OFF_GR)]
                  + [(w, o) for w in (w_out, w_cross_q, w_cross_o) for o in (0, W)]
                  + [(peer_w_q, i * W) for i in range(4)])
        NCHUNK = len(chunks)
        mem_chunks = [(w_mem_k, 0), (w_mem_k, W), (w_mem_v, 0), (w_mem_v, W)]
        NMEMC = len(mem_chunks)
        chunk_user = ([(MM, n) for n in ("fq", "fk", "fv", "gqk", "gv", "gr")] + [(SC, "wout")] * 2
                      + [(MM, "cq0"), (MM, "cq1")] + [(SC, "wo")] * 2 + [(MM, f"pq{i}") for i in range(4)])
        c_in, c_out, c_cq, c_co, c_pq = 0, 6, 8, 10, 12
        assert NCHUNK % WB == 0 and NMEMC % WB == 0

        @block.sync
        def _(sp):
            def load_chunk(which, n):
                src, off = which
                sp.dma_start(w_ring[:, n % WB], src.rearrange("(c p) n -> p c n", p=P)[:, :, off:off + W]
                             ).then_inc(w_land[n % WB], 16)

            def mem_load(b, which):
                if b >= 2:
                    sp.wait_ge(done["smk_used"] if which == "k" else done["smv_used"], b - 1)
                if which == "k":
                    sp.dma_start(s_mem_k[b % 2], smem_kt[b * D:(b + 1) * D, :].rearrange("(c p) m -> p c m", p=P)).then_inc(smk_land[b % 2], 16)
                else:
                    sp.dma_start(s_mem_v[b % 2], smem_v[b * N_MEM:(b + 1) * N_MEM, :].rearrange("(m p) n -> p m n", p=P)).then_inc(smv_land[b % 2], 16)

            def tile_loads(at, last):
                t = at[1]
                for k in range(NCHUNK):
                    if last and k == c_out:
                        sp.wait_ge(MM.full, MM.number(at, "fo") + 1)
                        for b in range(2):
                            mem_load(b, "k")
                            mem_load(b, "v")
                    if last and k == c_co:
                        for which in "kv":
                            for b in range(2, DEC_BATCH):
                                mem_load(b, which)
                    if not (last and k + WB >= NCHUNK):
                        bank, name = chunk_user[k]
                        sp.wait_ge(bank.full, bank.number(at, name) + 1)
                        load_chunk(chunks[(k + WB) % NCHUNK], k + WB)
                    if k == NCHUNK - 1 and not last:
                        sp.wait_ge(done["acc_set"], t + 1)
                        sp.dma_start(xr[:], x_all[bass.ds(t * P + P, P), :]).then_inc(land["x"], 16)
                if not last:
                    apart(sp)

            sp.dma_start(v_all[:, 0:2, :], mem_prompt[0:P, :].rearrange("p (c n) -> p c n", c=2)).then_inc(land["mem"], 16)
            load_chunk(mem_chunks[0], 0)
            load_chunk(mem_chunks[1], 1)
            sp.dma_start(gains_t[:], g_cols).then_inc(land["gains"], 16)
            sp.dma_start(sub_t[:], subkeys_t).then_inc(land["sub"], 16)
            sp.dma_start(g_ffn_bc[:], g_ffn.partition_broadcast(P)).then_inc(land["ffn"], 16)
            sp.dma_start(g_fin_bc[:], g_final.partition_broadcast(P)).then_inc(land["fin"], 16)
            sp.dma_start(bias_bc[:], bias_ls.partition_broadcast(P)).then_inc(land["bias"], 16)
            sp.dma_start(pages[:], page_table.partition_broadcast(P)).then_inc(land_s["pages"], 16)
            sp.dma_start(gate2[:], w_gate2).then_inc(land["gate2"], 16)
            w_rows = w_in.rearrange("(c p) n -> p c n", p=P)
            sp.dma_start(w_small[:, :, 0:H_FOX], w_rows[:, :, OFF_FF:OFF_FF + H_FOX]).then_inc(land["small"], 16)
            sp.dma_start(w_small[:, :, H_FOX:], w_rows[:, :, OFF_GG:OFF_GG + RANK]).then_inc(land["small"], 16)
            sp.dma_start(xr[:], x_all[0:P, :]).then_inc(land["x"], 16)
            sp.dma_start(v_all[:, 2:4, :], mem_prompt[P:2 * P, :].rearrange("p (c n) -> p c n", c=2)).then_inc(land["mem"], 16)
            for k in range(NMEMC):
                sp.wait_ge(MM.full, MC * (k + 1))
                load_chunk((mem_chunks + chunks)[k + WB], k + WB)
            with sp.Fori(0, TILES) as t:
                tile_loads(("prompt", t), False)
            sp.dma_start(states_s, state_in.rearrange("(s d) v -> d s v", d=DK)).then_inc(land_s["state_s"], 16)
            tile_loads(("sample", TILES), True)

        @block.tensor
        def _(pe):
            def transposes(at, name, src, rows, cols, n, pitch=P):
                bank = TP.ap(at, name)
                if cols == DK:
                    apart(pe)
                for j in range(n):
                    ins = nc.tensor.transpose(bank[0:cols, j * pitch:j * pitch + rows], src(j), ident[0:rows, 0:rows])
                return ins

            def rows_times(bank, lhs, k, rows):
                for c in range(KC):
                    ins = nc.tensor.matmul(bank, lhs[:, c, 0:rows], w_ring[:, k % WB, c, :], start=(c == 0), stop=(c == KC - 1))
                return ins

            def chunk_times(bank, rhs, k, rows):
                for f in range(W // P):
                    for c in range(KC):
                        ins = nc.tensor.matmul(bank[:, f * P:f * P + rows], w_ring[:, k % WB, c, f * P:(f + 1) * P],
                                               rhs[:, c, 0:rows], start=(c == 0), stop=(c == KC - 1))
                return ins

            at = ("setup", 0)
            pe.wait_ge(done["consts"], 1)
            pe.sem_inc(done["v_free"], VB)
            for m in range(MC):
                pe.wait_ge(done["mem_xs"], m + 1)
                for c in range(2):
                    pe.wait_ge(TP.free, TP.turn(at, f"mx{m}{c}"))
                    transposes(at, f"mx{m}{c}", lambda j: hb[:, (4 * c + j) * P:(4 * c + j + 1) * P], P, P, 4).then_inc(TP.full, 1)
            pe.wait_ge(TP.free, TP.taken(at, "mx11"))
            for k, wv in enumerate("kkvv"):
                pe.wait_ge(w_land[k % WB], 16 * (k // WB + 1))
                for m in range(MC):
                    name = f"mem{m}{wv}{k % 2}"
                    pe.wait_ge(MM.free, MM.turn(at, name))
                    bank = MM.ap(at, name)
                    for c in range(KC):
                        ins = nc.tensor.matmul(bank[:, :], mem_t[:, c, m * P:(m + 1) * P], w_ring[:, k % WB, c, :],
                                               start=(c == 0), stop=(c == KC - 1))
                    ins.then_inc(MM.full, 1)
                    if wv == "k":
                        pe.wait_ge(MM.free, MM.taken(at, name))
                        pe.wait_ge(TP.free, TP.turn(at, f"mk{m}{k % 2}"))
                        transposes(at, f"mk{m}{k % 2}", lambda j: mem_k_rows[:, m, k % 2, j * P:(j + 1) * P], P, P, 4).then_inc(TP.full, 1)

            def loads(t, k):
                return (NMEMC // WB + t * (NCHUNK // WB) + k // WB + 1) * 16

            def front(at, t, rows):
                pe.wait_ge(done["xs_x"], t + 1)
                for c in range(2):
                    pe.wait_ge(TP.free, TP.turn(at, f"x{c}"))
                    transposes(at, f"x{c}", lambda j: xs[0:rows, (4 * c + j) * P:(4 * c + j + 1) * P], rows, P, 4).then_inc(TP.full, 1)
                pe.wait_ge(TP.free, TP.taken(at, "x1"))
                for k, name in enumerate(MM_PROMPT[:6]):
                    pe.wait_ge(MM.free, MM.turn(at, name))
                    pe.wait_ge(w_land[k % WB], loads(t, k))
                    rows_times(MM.ap(at, name)[0:rows, :], h_t, k, rows).then_inc(MM.full, 1)
                pe.wait_ge(MM.free, MM.turn(at, "small"))
                bank = MM.ap(at, "small")
                for c in range(KC):
                    ins = nc.tensor.matmul(bank[0:rows, 0:H_FOX + RANK], h_t[:, c, 0:rows], w_small[:, c, :],
                                           start=(c == 0), stop=(c == KC - 1))
                ins.then_inc(MM.full, 1)
                pe.wait_ge(MM.free, MM.taken(at, "small"))
                pe.wait_ge(SC.free, SC.turn(at, "gg"))
                bank = SC.ap(at, "gg")
                nc.tensor.transpose(bank[0:RANK, 0:rows], gg[0:rows, :], ident[0:rows, 0:rows]).then_inc(SC.full, 1)
                pe.wait_ge(SC.free, SC.taken(at, "gg"))
                pe.wait_ge(MM.free, MM.turn(at, "gate"))
                bank = MM.ap(at, "gate")
                nc.tensor.matmul(bank[0:rows, 0:GKW], gg_t[:, 0:rows], gate2[:, :], start=True, stop=True).then_inc(MM.full, 1)

            def turn_heads(at, t, rows):
                pe.wait_ge(done["aug_cols"], t + 1)
                for name, src in (("q", q_aug), ("k", k_aug)):
                    for c in range(2):
                        pe.wait_ge(TP.free, TP.turn(at, f"{name}{c}"))
                        transposes(at, f"{name}{c}", lambda j: src[0:rows, 4 * c + j, :], rows, DA, 4).then_inc(TP.full, 1)
                pe.wait_ge(done["q_dec"], t + 1)
                for name, src in (("gq", q_dec), ("gk", k_neg)):
                    pe.wait_ge(TP.free, TP.turn(at, name))
                    transposes(at, name, lambda j: src[0:rows, j * DK:(j + 1) * DK], rows, DK, 4).then_inc(TP.full, 1)

            def peer_scores(at, t, rows):
                pe.wait_ge(done["hb_rows"], t + 1)
                pe.wait_ge(TP.free, TP.turn(at, "f0"))
                transposes(at, "f0", lambda j: hb[0:rows, (0 + j) * P:(0 + j + 1) * P], rows, P, 4).then_inc(TP.full, 1)
                pe.wait_ge(TP.free, TP.turn(at, "f1"))
                transposes(at, "f1", lambda j: hb[0:rows, (4 + j) * P:(4 + j + 1) * P], rows, P, 4).then_inc(TP.full, 1)
                pe.wait_ge(TP.free, TP.taken(at, "f1"))
                for i in range(4):
                    pe.wait_ge(MM.free, MM.turn(at, f"pq{i}"))
                    pe.wait_ge(w_land[(c_pq + i) % WB], loads(t, c_pq + i))
                    chunk_times(MM.ap(at, f"pq{i}"), h_t, c_pq + i, rows).then_inc(MM.full, 1)
                pe.wait_ge(MM.free, MM.taken(at, "pq3"))
                for i in range(2):
                    pe.wait_ge(SC.free, SC.turn(at, f"ps{i}"))
                    bank = SC.ap(at, f"ps{i}")
                    for j in range(8):
                        hh = 8 * i + j
                        ins = nc.tensor.matmul(bank[0:rows, j * P:(j + 1) * P], pq_t[:, hh, 0:rows], sub_t[:, hh % 2, :],
                                               start=True, stop=True)
                    ins.then_inc(SC.full, 1)

            def peer_sum(t, rows):
                pe.wait_ge(done["acc_free"], t + 1)
                for c in range(2):
                    ins = nc.tensor.matmul(acc[0:P, c * W:(c + 1) * W], ident[0:rows, :], xr[0:rows, c * W:(c + 1) * W],
                                           start=True, stop=True, skip_group_check=True)
                ins.then_inc(done["acc_set"], 1)
                with pe.Fori(0, SLOTS // (2 * GROUP)) as it:
                    for g in range(2):
                        for s in range(GROUP):
                            n = g * GROUP + s
                            if s == 0:
                                pe.wait_ge(done["diag"], (t * 8 + it) * 2 + g + 1)
                            pe.wait_ge(v_land[n % VB], ((t * 8 + it) * (2 * GROUP // VB) + n // VB + 1) * 16)
                            for c in range(2):
                                ins = nc.tensor.matmul(acc[0:P, c * W:(c + 1) * W], diag[0:rows, s, :],
                                                       v_ring[0:rows, n % VB, c * W:(c + 1) * W],
                                                       start=False, stop=True, skip_group_check=True)
                            ins.then_inc(done["v_free"], 1)

            def prompt_tile(t):
                at = ("prompt", t)
                front(at, t, P)
                pe.wait_ge(done["lf"], t + 1)
                pe.wait_ge(MM.free, MM.turn(at, "cum"))
                bank = MM.ap(at, "cum")
                nc.tensor.matmul(bank[:, 0:H_FOX], upper[:, :], lf[:, 0:H_FOX], start=True, stop=True)
                nc.tensor.matmul(bank[:, H_FOX:2 * H_FOX], ones[:, :], lf[:, 0:H_FOX], start=True, stop=True)
                nc.tensor.matmul(bank[:, 2 * H_FOX:2 * H_FOX + GKW], blk_up[:, :], lf[:, H_FOX:NLS],
                                 start=True, stop=True).then_inc(MM.full, 1)
                pe.wait_ge(MM.free, MM.turn(at, "cumg"))
                bank = MM.ap(at, "cumg")
                nc.tensor.matmul(bank[:, 0:GKW], blk_one[:, :], lf[:, H_FOX:NLS], start=True, stop=True)
                for h in range(H_GLA):
                    ins = nc.tensor.matmul(bank[0:DK, GKW + NCH * h:GKW + NCH * (h + 1)],
                                           lf[:, H_FOX + h * DK:H_FOX + (h + 1) * DK], blk_ind[:, :], start=True, stop=True)
                ins.then_inc(MM.full, 1)
                turn_heads(at, t, P)
                pe.wait_ge(TP.free, TP.taken(at, "gk"))

                def scores(h):
                    pe.wait_ge(SC.free, SC.turn(at, f"s{h}"))
                    bank = SC.ap(at, f"s{h}")
                    for c in range(2):
                        ins = nc.tensor.matmul(bank[:, c * W:(c + 1) * W], q_t[:, h, :], kt_all[0:DA, h, c * W:(c + 1) * W],
                                               start=True, stop=True)
                    ins.then_inc(SC.full, 1)

                scores(0)
                pe.wait_ge(MM.free, MM.turn(at, "fo"))
                fo = MM.ap(at, "fo")
                for h in range(H_FOX):
                    if h + 1 < H_FOX:
                        scores(h + 1)
                    pe.wait_ge(done["fox_exp"], t * H_FOX + h + 1)
                    for c in range(2):
                        pe.wait_ge(TP.free, TP.turn(at, f"P{h}{c}"))
                        transposes(at, f"P{h}{c}", lambda j: probs[h % 2][:, (4 * c + j) * P:(4 * c + j + 1) * P], P, P, 4).then_inc(TP.full, 1)
                    pe.wait_ge(TP.free, TP.taken(at, f"P{h}1"))
                    for j in range(TILES):
                        ins = nc.tensor.matmul(fo[:, h * DH:(h + 1) * DH], p_t[:, j, :], v_all[:, j, h * DH:(h + 1) * DH],
                                               start=(j == 0), stop=(j == TILES - 1))
                ins.then_inc(MM.full, 1)
                pe.wait_ge(SC.free, SC.turn(at, "gatt"))
                bank = SC.ap(at, "gatt")
                for h in range(H_GLA):
                    ins = nc.tensor.matmul(bank[:, h * P:(h + 1) * P], kn_t[:, h, :], qd_t[:, h, :], start=True, stop=True)
                ins.then_inc(SC.full, 1)
                pe.wait_ge(SC.free, SC.turn(at, "gkv"))
                bank = SC.ap(at, "gkv")
                pe.wait_ge(done["k_dl"], t + 1)
                apart(pe)
                for ch in range(NCH):
                    r = slice(ch * CHUNK, (ch + 1) * CHUNK)
                    for h in range(H_GLA):
                        ins = nc.tensor.matmul(bank[0:DK, (ch * H_GLA + h) * DV:(ch * H_GLA + h + 1) * DV],
                                               k_dl[r, h * DK:(h + 1) * DK], gv[r, h * DV:(h + 1) * DV], start=True, stop=True)
                ins.then_inc(SC.full, 1)
                pe.wait_ge(MM.free, MM.turn(at, "go"))
                bank = MM.ap(at, "go")
                pe.wait_ge(done["state1"], t + 1)
                for h in range(H_GLA):
                    o = bank[:, h * DV:(h + 1) * DV]
                    nc.tensor.matmul(o, att_t[:, h, :], gv[:, h * DV:(h + 1) * DV], start=True, stop=False, skip_group_check=True)
                    for ch in range(NCH):
                        r = slice(ch * CHUNK, (ch + 1) * CHUNK)
                        ins = nc.tensor.matmul(bank[r, h * DV:(h + 1) * DV], qd_t[:, h, r], (state, state1)[ch][:, h, :],
                                               start=False, stop=True, skip_group_check=True)
                ins.then_inc(MM.full, 1)
                pe.wait_ge(done["merged"], t + 1)
                pe.wait_ge(TP.free, TP.turn(at, "m0"))
                transposes(at, "m0", lambda j: hb[0:P, (0 + j) * P:(0 + j + 1) * P], P, P, 4).then_inc(TP.full, 1)
                pe.wait_ge(TP.free, TP.turn(at, "m1"))
                transposes(at, "m1", lambda j: hb[0:P, (4 + j) * P:(4 + j + 1) * P], P, P, 4).then_inc(TP.full, 1)
                pe.wait_ge(TP.free, TP.taken(at, "m1"))
                pe.wait_ge(SC.free, SC.turn(at, "wout"))
                pe.wait_ge(w_land[c_out % WB], loads(t, c_out))
                rows_times(SC.ap(at, "wout")[0:P, 0:W], h_t, c_out, P)
                pe.wait_ge(w_land[(c_out + 1) % WB], loads(t, c_out + 1))
                rows_times(SC.ap(at, "wout")[0:P, W:D], h_t, c_out + 1, P).then_inc(SC.full, 1)
                pe.wait_ge(done["xs_2"], t + 1)
                pe.wait_ge(TP.free, TP.turn(at, "h0"))
                transposes(at, "h0", lambda j: xs[0:P, (0 + j) * P:(0 + j + 1) * P], P, P, 4).then_inc(TP.full, 1)
                pe.wait_ge(TP.free, TP.turn(at, "h1"))
                transposes(at, "h1", lambda j: xs[0:P, (4 + j) * P:(4 + j + 1) * P], P, P, 4).then_inc(TP.full, 1)
                pe.wait_ge(TP.free, TP.taken(at, "h1"))
                pe.wait_ge(MM.free, MM.turn(at, "cq0"))
                pe.wait_ge(w_land[(c_cq) % WB], loads(t, c_cq))
                chunk_times(MM.ap(at, "cq0"), h_t, c_cq, P).then_inc(MM.full, 1)
                pe.wait_ge(MM.free, MM.turn(at, "cq1"))
                pe.wait_ge(w_land[(c_cq + 1) % WB], loads(t, c_cq + 1))
                chunk_times(MM.ap(at, "cq1"), h_t, c_cq + 1, P).then_inc(MM.full, 1)
                pe.wait_ge(MM.free, MM.taken(at, "cq1"))
                pe.wait_ge(SC.free, SC.turn(at, "xs"))
                bank = SC.ap(at, "xs")
                for h in range(H_MEM):
                    for c in range(2):
                        ins = nc.tensor.matmul(bank[:, h * N_MEM:(h + 1) * N_MEM], c_qt[:, 2 * h + c, :], mem_kt[:, 2 * h + c, :],
                                               start=(c == 0), stop=(c == 1))
                ins.then_inc(SC.full, 1)
                pe.wait_ge(done["p_norm"], t + 1)
                pe.wait_ge(TP.free, TP.turn(at, "p0"))
                transposes(at, "p0", lambda j: probs[0][0:P, (0 + j) * P:(0 + j + 1) * P], P, P, 4).then_inc(TP.full, 1)
                pe.wait_ge(TP.free, TP.turn(at, "p1"))
                transposes(at, "p1", lambda j: probs[0][0:P, (4 + j) * P:(4 + j + 1) * P], P, P, 4).then_inc(TP.full, 1)
                pe.wait_ge(TP.free, TP.taken(at, "p1"))
                for i in range(2):
                    pe.wait_ge(MM.free, MM.turn(at, f"cu{i}"))
                    bank = MM.ap(at, f"cu{i}")
                    for j in range(4):
                        d = 4 * i + j
                        for m in range(MC):
                            ins = nc.tensor.matmul(bank[:, j * P:(j + 1) * P], mem_v[:, m, d * P:(d + 1) * P],
                                                   p_t[:, 2 * (d // 2) + m, :], start=(m == 0), stop=(m == MC - 1))
                    ins.then_inc(MM.full, 1)
                pe.wait_ge(MM.free, MM.taken(at, "cu1"))
                pe.wait_ge(SC.free, SC.turn(at, "wo"))
                pe.wait_ge(w_land[c_co % WB], loads(t, c_co))
                rows_times(SC.ap(at, "wo")[0:P, 0:W], h_t, c_co, P)
                pe.wait_ge(w_land[(c_co + 1) % WB], loads(t, c_co + 1))
                rows_times(SC.ap(at, "wo")[0:P, W:D], h_t, c_co + 1, P).then_inc(SC.full, 1)
                peer_scores(at, t, P)
                peer_sum(t, P)

            with pe.Fori(0, TILES) as t:
                prompt_tile(t)

            def sample_tile(t):
                at = ("sample", t)
                rows = RS
                seq = [slice(b * DEC_SEQ, (b + 1) * DEC_SEQ) for b in range(DEC_BATCH)]
                front(at, t, rows)
                pe.wait_ge(land_s["lf_past"], 16 * DEC_BATCH * N_PAGES)
                pe.wait_ge(MM.free, MM.turn(at, "cpast"))
                bank = MM.ap(at, "cpast")
                n = DEC_BATCH * H_FOX
                first, second = lf_past[:, :, 0, :], lf_past[:, :, 1, :]
                nc.tensor.matmul(bank[:, 0:n], upper[:, :], first, start=True, stop=True)
                nc.tensor.matmul(bank[:, n:2 * n], upper[:, :], second, start=True, stop=False)
                nc.tensor.matmul(bank[:, n:2 * n], ones[:, :], first, start=False, stop=True)
                nc.tensor.matmul(bank[0:rows, 2 * n:3 * n], ones[:, 0:rows], first, start=True, stop=False)
                nc.tensor.matmul(bank[0:rows, 2 * n:3 * n], ones[:, 0:rows], second, start=False, stop=True).then_inc(MM.full, 1)
                pe.wait_ge(done["lf"], t + 1)
                pe.wait_ge(MM.free, MM.turn(at, "cum"))
                bank = MM.ap(at, "cum")
                nc.tensor.matmul(bank[0:rows, 0:H_FOX], same_up[:, :], lf[0:rows, 0:H_FOX], start=True, stop=True)
                nc.tensor.matmul(bank[0:rows, 2 * H_FOX:2 * H_FOX + GKW], same_up[:, :], lf[0:rows, H_FOX:NLS],
                                 start=True, stop=True).then_inc(MM.full, 1)
                pe.wait_ge(MM.free, MM.turn(at, "cumg"))
                bank = MM.ap(at, "cumg")
                nc.tensor.matmul(bank[0:rows, 0:GKW], same_one[:, :], lf[0:rows, H_FOX:NLS], start=True, stop=True)
                for h in range(H_GLA):
                    ins = nc.tensor.matmul(bank[0:DK, GKW + DEC_BATCH * h:GKW + DEC_BATCH * (h + 1)],
                                           lf[0:rows, H_FOX + h * DK:H_FOX + (h + 1) * DK], same_ind[:, :], start=True, stop=True)
                ins.then_inc(MM.full, 1)
                turn_heads(at, t, rows)
                pe.wait_ge(TP.free, TP.taken(at, "gk"))
                pe.wait_ge(SC.free, SC.turn(at, "gatt"))
                bank = SC.ap(at, "gatt")
                for h in range(H_GLA):
                    ins = nc.tensor.matmul(bank[0:rows, h * P:h * P + rows], kn_t[:, h, 0:rows], qd_t[:, h, 0:rows], start=True, stop=True)
                ins.then_inc(SC.full, 1)
                pe.wait_ge(MM.free, MM.turn(at, "go"))
                bank = MM.ap(at, "go")
                pe.wait_ge(SC.free, SC.taken(at, "gatt"))
                pe.wait_ge(land_s["state_s"], 16)
                for h in range(H_GLA):
                    nc.tensor.matmul(bank[:, h * rows:(h + 1) * rows], gv[0:rows, h * DV:(h + 1) * DV], att_t[0:rows, h, 0:rows],
                                     start=True, stop=False, skip_group_check=True)
                    for b in range(DEC_BATCH):
                        ins = nc.tensor.matmul(bank[:, h * rows + b * DEC_SEQ:h * rows + (b + 1) * DEC_SEQ], states_s[:, b * H_GLA + h, :],
                                               qd_t[:, h, seq[b]], start=False, stop=True, skip_group_check=True)
                ins.then_inc(MM.full, 1)
                pe.wait_ge(done["k_masked"], 1)
                for b in range(DEC_BATCH):
                    pe.wait_ge(SC.free, SC.turn(at, f"kv{b}"))
                    bank = SC.ap(at, f"kv{b}")
                    for h in range(H_GLA):
                        ins = nc.tensor.matmul(bank[0:DK, h * DV:(h + 1) * DV], k_masked[:, b, h * DK:(h + 1) * DK],
                                               gv[0:rows, h * DV:(h + 1) * DV], start=True, stop=True)
                    ins.then_inc(SC.full, 1)
                pe.wait_ge(MM.free, MM.taken(at, "go"))
                pe.wait_ge(TP.free, TP.turn(at, "got"))
                transposes(at, "got", lambda j: go_t[:, j, :], P, rows, 4).then_inc(TP.full, 1)
                pe.wait_ge(SC.free, SC.turn(at, "past"))
                bank = SC.ap(at, "past")
                for b in range(DEC_BATCH):
                    for page in range(N_PAGES):
                        n = b * N_PAGES + page
                        pe.wait_ge(key_land[n % UB], 16 * (n // UB + 1))
                        for h in range(H_FOX):
                            c = (page * H_FOX + h) * rows + b * DEC_SEQ
                            ins = nc.tensor.matmul(bank[:, c:c + DEC_SEQ], past_keys[n % UB][:, h, :], q_t[0:DH, h, seq[b]],
                                                   start=True, stop=True)
                        if n == DEC_BATCH * N_PAGES - 1:
                            ins.then_inc(SC.full, 1)
                        else:
                            ins.then_inc(done["past_kept"], 1)
                pe.wait_ge(SC.free, SC.turn(at, "new"))
                bank = SC.ap(at, "new")
                for h in range(H_FOX):
                    ins = nc.tensor.matmul(bank[0:rows, h * rows:(h + 1) * rows], q_t[:, h, 0:rows], k_new_t[:, h, 0:rows], start=True, stop=True)
                ins.then_inc(SC.full, 1)
                for i in range(4):
                    pe.wait_ge(TP.free, TP.turn(at, f"S{i}"))
                    transposes(at, f"S{i}", lambda j: past_scores[:, 4 * i + j, :], P, rows, 4).then_inc(TP.full, 1)
                pe.wait_ge(done["s_exp"], 1)
                for i in range(4):
                    pe.wait_ge(TP.free, TP.turn(at, f"P{i}"))
                    transposes(at, f"P{i}", lambda j: s_rows[:, 4 * (i % 2) + j, (i // 2) * P:(i // 2 + 1) * P], rows, P, 4).then_inc(TP.full, 1)
                pe.wait_ge(TP.free, TP.turn(at, "Pn"))
                transposes(at, "Pn", lambda j: s_rows[:, j, N_PAGES * P:], rows, rows, 8, pitch=rows).then_inc(TP.full, 1)
                pe.wait_ge(TP.free, TP.taken(at, "Pn"))
                pe.wait_ge(land_s["values_past"], 16 * DEC_BATCH * N_PAGES)
                pe.wait_ge(MM.free, MM.turn(at, "fo"))
                bank = MM.ap(at, "fo")
                for b in range(DEC_BATCH):
                    for h in range(H_FOX):
                        o = bank[0:DH, h * rows + b * DEC_SEQ:h * rows + (b + 1) * DEC_SEQ]
                        for page in range(N_PAGES):
                            nc.tensor.matmul(o, past_values[:, b * N_PAGES + page, h * DH:(h + 1) * DH],
                                             past_p_t[:, page * H_FOX + h, seq[b]], start=(page == 0), stop=False)
                        ins = nc.tensor.matmul(o, v_new[:, h * DH:(h + 1) * DH], new_p_t[:, h, seq[b]], start=False, stop=True)
                ins.then_inc(MM.full, 1)
                pe.wait_ge(MM.free, MM.taken(at, "fo"))
                pe.wait_ge(TP.free, TP.turn(at, "fot"))
                transposes(at, "fot", lambda j: fo_t[:, j, :], DH, rows, 8, pitch=DH).then_inc(TP.full, 1)
                pe.wait_ge(done["merged"], t + 1)
                pe.wait_ge(TP.free, TP.turn(at, "m0"))
                transposes(at, "m0", lambda j: hb[0:rows, (0 + j) * P:(0 + j + 1) * P], rows, P, 4).then_inc(TP.full, 1)
                pe.wait_ge(TP.free, TP.turn(at, "m1"))
                transposes(at, "m1", lambda j: hb[0:rows, (4 + j) * P:(4 + j + 1) * P], rows, P, 4).then_inc(TP.full, 1)
                pe.wait_ge(TP.free, TP.taken(at, "m1"))
                pe.wait_ge(SC.free, SC.turn(at, "wout"))
                pe.wait_ge(w_land[c_out % WB], loads(t, c_out))
                rows_times(SC.ap(at, "wout")[0:rows, 0:W], h_t, c_out, rows)
                pe.wait_ge(w_land[(c_out + 1) % WB], loads(t, c_out + 1))
                rows_times(SC.ap(at, "wout")[0:rows, W:D], h_t, c_out + 1, rows).then_inc(SC.full, 1)
                pe.wait_ge(done["xs_2"], t + 1)
                pe.wait_ge(TP.free, TP.turn(at, "h0"))
                transposes(at, "h0", lambda j: xs[0:rows, (0 + j) * P:(0 + j + 1) * P], rows, P, 4).then_inc(TP.full, 1)
                pe.wait_ge(TP.free, TP.turn(at, "h1"))
                transposes(at, "h1", lambda j: xs[0:rows, (4 + j) * P:(4 + j + 1) * P], rows, P, 4).then_inc(TP.full, 1)
                pe.wait_ge(TP.free, TP.taken(at, "h1"))
                pe.wait_ge(MM.free, MM.turn(at, "cq0"))
                pe.wait_ge(w_land[(c_cq) % WB], loads(t, c_cq))
                chunk_times(MM.ap(at, "cq0"), h_t, c_cq, rows).then_inc(MM.full, 1)
                pe.wait_ge(MM.free, MM.turn(at, "cq1"))
                pe.wait_ge(w_land[(c_cq + 1) % WB], loads(t, c_cq + 1))
                chunk_times(MM.ap(at, "cq1"), h_t, c_cq + 1, rows).then_inc(MM.full, 1)
                pe.wait_ge(MM.free, MM.taken(at, "cq1"))
                pe.wait_ge(MM.free, MM.turn(at, "cs"))
                bank = MM.ap(at, "cs")
                for b in range(DEC_BATCH):
                    pe.wait_ge(smk_land[b % 2], 16 * (b // 2 + 1))
                    for h in range(H_MEM):
                        for m in range(MC):
                            o = (m * H_MEM + h) * rows + b * DEC_SEQ
                            for c in range(2):
                                ins = nc.tensor.matmul(bank[:, o:o + DEC_SEQ], s_mem_k[b % 2][:, 2 * h + c, m * P:(m + 1) * P],
                                                       c_qt[:, 2 * h + c, seq[b]], start=(c == 0), stop=(c == 1))
                    if b < DEC_BATCH - 1:
                        ins.then_inc(done["smk_used"], 1)
                ins.then_inc(MM.full, 1)
                pe.wait_ge(MM.free, MM.taken(at, "cs"))
                for m in range(MC):
                    pe.wait_ge(TP.free, TP.turn(at, f"c{m}"))
                    transposes(at, f"c{m}", lambda j: cs_t[:, m * H_MEM + j, :], P, rows, 4).then_inc(TP.full, 1)
                pe.wait_ge(done["p_norm"], t + 1)
                pe.wait_ge(TP.free, TP.turn(at, "p0"))
                transposes(at, "p0", lambda j: probs[0][0:rows, (0 + j) * P:(0 + j + 1) * P], rows, P, 4).then_inc(TP.full, 1)
                pe.wait_ge(TP.free, TP.turn(at, "p1"))
                transposes(at, "p1", lambda j: probs[0][0:rows, (4 + j) * P:(4 + j + 1) * P], rows, P, 4).then_inc(TP.full, 1)
                pe.wait_ge(TP.free, TP.taken(at, "p1"))
                pe.wait_ge(MM.free, MM.turn(at, "cu1"))
                banks = [MM.ap(at, f"cu{i}") for i in range(2)]
                for b in range(DEC_BATCH):
                    pe.wait_ge(smv_land[b % 2], 16 * (b // 2 + 1))
                    for d in range(KC):
                        o = (d % 4) * P + b * DEC_SEQ
                        for m in range(MC):
                            ins = nc.tensor.matmul(banks[d // 4][:, o:o + DEC_SEQ], s_mem_v[b % 2][:, m, d * P:(d + 1) * P],
                                                   p_t[:, 2 * (d // 2) + m, seq[b]], start=(m == 0), stop=(m == MC - 1))
                        if b == DEC_BATCH - 1 and d % 4 == 3:
                            ins.then_inc(MM.full, 1)
                    if b < DEC_BATCH - 1:
                        ins.then_inc(done["smv_used"], 1)
                pe.wait_ge(MM.free, MM.taken(at, "cu1"))
                pe.wait_ge(SC.free, SC.turn(at, "wo"))
                pe.wait_ge(w_land[c_co % WB], loads(t, c_co))
                rows_times(SC.ap(at, "wo")[0:rows, 0:W], h_t, c_co, rows)
                pe.wait_ge(w_land[(c_co + 1) % WB], loads(t, c_co + 1))
                rows_times(SC.ap(at, "wo")[0:rows, W:D], h_t, c_co + 1, rows).then_inc(SC.full, 1)
                peer_scores(at, t, rows)
                peer_sum(t, rows)

            sample_tile(TILES)

        @block.scalar
        def _(act):
            A = nc.scalar.activation

            def root(rows, n=D, inp=SSQ, out=STD, w=1):
                act.drain()
                return A(stats[0:rows, out:out + w], stats[0:rows, inp:inp + w], ACT.Sqrt, scale=1.0 / n, bias=eps_col[0:rows, :])

            def rms(src, rows):
                A(xs[0:rows, :], src[0:rows, :], ACT.Square, accum_out=stats[0:rows, SSQ:SSQ + 1])
                return root(rows)

            def take(at, name, out, shape, func=ACT.Copy, **kw):
                return A(out, shape(MM.ap(at, name)), func, **kw)

            act.sem_inc(MM.free, MM.depth)
            act.wait_ge(done["consts"], 1)
            act.wait_ge(done["preset"], 1)
            at = ("setup", 0)
            act.wait_ge(land["mem"], 32)
            for m, src in enumerate(mem_rows):
                if m == 1:
                    act.wait_ge(done["mem_xs"], 1)
                A(xs[:, :], src, ACT.Square, accum_out=stats[:, SSQ:SSQ + 1])
                root(P).then_inc(done["mem_ss"], 1)
            for k, wv in enumerate("kkvv"):
                for m in range(MC):
                    name = f"mem{m}{wv}{k % 2}"
                    dst = mem_k_rows[:, m, k % 2, :] if wv == "k" else mem_v[:, m, (k % 2) * W:(k % 2 + 1) * W]
                    act.wait_ge(MM.full, MM.filled(at, name))
                    take(at, name, dst, lambda b: b[:, :]).then_inc(MM.free, 1)
            act.wait_ge(MM.free, MM.taken(at, "mem1v1"))
            for m in range(MC):
                act.dma_start(outs["mem_k"][m * P:(m + 1) * P, :].rearrange("p (c n) -> p c n", c=2), mem_k_rows[:, m, :, :]).then_inc(out_sem["mk0"], 16)
                act.dma_start(outs["mem_v"][m * P:(m + 1) * P, :], mem_v[:, m, :]).then_inc(out_sem["mk0"], 16)
            act.wait_ge(out_sem["mk0"], 64)

            def front(at, t, rows, v_dst, row0):
                act.wait_ge(land["x"], 16 * (t + 1))
                rms(xr, rows).then_inc(done["std_x"], 1)
                heads = lambda b: b[0:rows, :].rearrange("p (h d) -> p h d", h=H_FOX)
                act.wait_ge(MM.full, MM.filled(at, "fq"))
                take(at, "fq", q_aug[0:rows, :, 0:DH], heads, scale=DH ** -0.5).then_inc(MM.free, 1)
                act.wait_ge(MM.full, MM.filled(at, "fk"))
                take(at, "fk", k_aug[0:rows, :, 0:DH], heads).then_inc(MM.free, 1)
                act.wait_ge(MM.full, MM.filled(at, "fv"))
                take(at, "fv", v_dst, lambda b: b[0:rows, :]).then_inc(MM.free, 1)
                act.wait_ge(MM.full, MM.filled(at, "gqk"))
                take(at, "gqk", gqk[0:rows, :], lambda b: b[0:rows, :]).then_inc(MM.free, 1)
                act.wait_ge(MM.full, MM.filled(at, "gv"))
                take(at, "gv", gv[0:rows, :], lambda b: b[0:rows, :]).then_inc(MM.free, 1)
                act.wait_ge(MM.full, MM.filled(at, "gr"))
                take(at, "gr", silu_r[0:rows, :], lambda b: b[0:rows, :], ACT.Silu).then_inc(MM.free, 1)
                act.wait_ge(MM.full, MM.filled(at, "small"))
                bank = MM.ap(at, "small")
                A(zz[0:rows, 0:H_FOX], bank[0:rows, 0:H_FOX], ACT.Copy)
                A(gg[0:rows, :], bank[0:rows, H_FOX:H_FOX + RANK], ACT.Copy).then_inc(MM.free, 1)
                act.wait_ge(MM.free, MM.taken(at, "fv"))
                k_out, v_out, lf_out = row0
                act.dma_start(k_out, k_aug[0:rows, :, 0:DH]).then_inc(out_sem["fk"], 16)
                act.dma_start(v_out, v_dst).then_inc(out_sem["fv"], 16)
                act.wait_ge(MM.full, MM.filled(at, "gate"))
                take(at, "gate", zz[0:rows, H_FOX:], lambda b: b[0:rows, 0:GKW]).then_inc(MM.free, 1)
                act.wait_ge(done["zmin"], t + 1)
                A(zl[0:rows, :], zl[0:rows, :], ACT.Exp)
                act.drain()
                A(zl[0:rows, :], zl[0:rows, :], ACT.Ln, bias=1.0).then_inc(done["lnz"], 1)
                act.wait_ge(done["lf"], t + 1)
                act.dma_start(lf_out, lf[0:rows, 0:H_FOX]).then_inc(out_sem["lf"], 16)

            def gate_exps(at, t, rows):
                act.wait_ge(MM.full, MM.filled(at, "cum"))
                bank = MM.ap(at, "cum")
                A(cums[0:rows, :], bank[0:rows, 0:2 * H_FOX], ACT.Copy)
                b = bank[0:rows, 2 * H_FOX:2 * H_FOX + GKW]
                A(gb[0:rows, :], b, ACT.Copy)
                A(q_dec[0:rows, :], b, ACT.Exp)
                A(k_neg[0:rows, :], b, ACT.Exp, scale=-1.0).then_inc(MM.free, 1)

            def gla_squares(at, t, rows, src):
                for h in range(H_GLA):
                    A(xs[0:rows, h * DV:(h + 1) * DV], src[:, h * DV:(h + 1) * DV], ACT.Square,
                      accum_out=stats[0:rows, GSS + h:GSS + h + 1])

            def cross_exp(t, rows):
                for h in range(H_MEM):
                    p = probs[0][0:rows, h * N_MEM:(h + 1) * N_MEM]
                    ins = A(p, p, ACT.Exp, accum_out=stats[0:rows, CSUM + h:CSUM + h + 1])
                ins.then_inc(done["c_exp"], 1)

            def peer(at, t, rows):
                act.wait_ge(SC.free, SC.taken(at, "wo"))
                rms(xr, rows).then_inc(done["std_3"], 1)
                for i in range(4):
                    act.wait_ge(MM.full, MM.filled(at, f"pq{i}"))
                    take(at, f"pq{i}", pq_t[:, 4 * i:4 * i + 4, 0:rows], lambda b: b[:, :].rearrange("p (j q) -> p j q", j=4)[:, :, 0:rows]).then_inc(MM.free, 1)
                act.wait_ge(done["gate_sub"], t + 1)
                A(gates[0:rows, :], gates[0:rows, :], ACT.Exp).then_inc(done["gate_exp"], 1)
                with act.Fori(0, SLOTS // (2 * GROUP)) as it:
                    for g in range(2):
                        n = (t * 8 + it) * 2 + g
                        act.wait_ge(done["u_free"], n * GROUP + GROUP + UB)
                        A(gelu[0:rows, g, :], dots[0:rows, g, :], ACT.Gelu_apprx_tanh).then_inc(done["gelu"], 1)
                        act.wait_ge(done["wts"], n + 1)
                        act.wait_ge(done["v_free"], n * GROUP + VB)
                        for s in range(GROUP):
                            ins = A(diag[0:rows, s, :], ident[0:rows, :], ACT.Copy, scale=wts[0:rows, g, s:s + 1])
                        ins.then_inc(done["diag"], 1)
                act.wait_ge(done["v_free"], (t + 1) * SLOTS + VB)
                A(xs[0:rows, :], acc[0:rows, :], ACT.Square, accum_out=stats[0:rows, SSQ:SSQ + 1])
                root(rows).then_inc(done["std_y"], 1)
                act.wait_ge(done["y_rows"], t + 1)

            def prompt_tile(t):
                at = ("prompt", t)
                r = bass.ds(t * P, P)
                front(at, t, P, v_all[:, bass.ds(t, 1), :].rearrange("p a n -> p (a n)"),
                      (outs["fk"][r, :].rearrange("p (h d) -> p h d", h=H_FOX), outs["fv"][r, :], outs["lf"][r, :]))
                A(mask[:, :], causal[:, bass.ds((TILES - 1) * P - t * P, SEQ)], ACT.Copy).then_inc(done["mask"], 1)
                gate_exps(at, t, P)
                act.wait_ge(MM.full, MM.filled(at, "cumg"))
                bank = MM.ap(at, "cumg")
                A(k_dl[:, :], bank[:, 0:GKW], ACT.Copy)
                A(decay[:, :], bank[0:DK, GKW:GKW + H_GLA * NCH], ACT.Exp).then_inc(MM.free, 1)
                act.wait_ge(done["gdiff"], t + 1)
                A(k_dl[:, :], k_dl[:, :], ACT.Exp).then_inc(done["gexpl"], 1)
                for h in range(H_FOX):
                    act.wait_ge(done["fox_sub"], t * H_FOX + h + 1)
                    A(probs[h % 2], probs[h % 2], ACT.Exp, bias=stats[:, FMAX + h:FMAX + h + 1],
                           accum_out=stats[:, FSUM + h:FSUM + h + 1]).then_inc(done["fox_exp"], 1)
                for n in ("fk", "fv", "lf"):
                    act.wait_ge(out_sem[n], 16 * (t + 1))
                act.wait_ge(MM.full, MM.filled(at, "fo"))
                bank = MM.ap(at, "fo")
                act.wait_ge(done["finv"], t + 1)
                for h in range(H_FOX):
                    ins = A(hb[:, h * DH:(h + 1) * DH], bank[:, h * DH:(h + 1) * DH], ACT.Copy, scale=stats[:, FINV + h:FINV + h + 1])
                ins.then_inc(MM.free, 1)
                act.wait_ge(MM.full, MM.filled(at, "go"))
                bank = MM.ap(at, "go")
                gla_squares(at, t, P, bank)
                A(gqk[:, :], bank[:, :], ACT.Copy).then_inc(MM.free, 1)
                root(P, n=DV, inp=GSS, out=GSTD, w=H_GLA).then_inc(done["gstd"], 1)
                act.wait_ge(SC.free, SC.taken(at, "wout"))
                rms(xr, P).then_inc(done["std_2"], 1)
                for i in range(2):
                    act.wait_ge(MM.full, MM.filled(at, f"cq{i}"))
                    take(at, f"cq{i}", c_qt[:, 4 * i:4 * i + 4, :], lambda b: b[:, :].rearrange("p (j q) -> p j q", j=4), scale=DH_MEM ** -0.5).then_inc(MM.free, 1)
                act.wait_ge(SC.free, SC.taken(at, "xs"))
                cross_exp(t, P)
                for i in range(2):
                    act.wait_ge(MM.full, MM.filled(at, f"cu{i}"))
                    take(at, f"cu{i}", h_t[:, 4 * i:4 * i + 4, :], lambda b: b[:, :].rearrange("p (j q) -> p j q", j=4)).then_inc(MM.free, 1)
                peer(at, t, P)
                act.dma_start(outs["y"][r, :], xs[:, :]).then_inc(out_sem["y"], 16)
                act.wait_ge(out_sem["y"], 16 * (t + 1))

            def sample_tile(t):
                at = ("sample", t)
                rows = RS
                front(at, t, rows, v_new, (outs["fk"][SEQ:, :].rearrange("p (h d) -> p h d", h=H_FOX), outs["fv"][SEQ:, :], outs["lf"][SEQ:, :]))
                act.wait_ge(MM.full, MM.filled(at, "cpast"))
                bank = MM.ap(at, "cpast")
                n = DEC_BATCH * H_FOX
                A(c_past[:].rearrange("p a b h -> p (a b h)"), bank[:, 0:2 * n], ACT.Copy)
                A(c_last[:].rearrange("p b h -> p (b h)"), bank[0:rows, 2 * n:3 * n], ACT.Copy).then_inc(MM.free, 1)
                act.wait_ge(MM.full, MM.filled(at, "cum"))
                bank = MM.ap(at, "cum")
                A(cums[0:rows, 0:H_FOX], bank[0:rows, 0:H_FOX], ACT.Copy)
                b = bank[0:rows, 2 * H_FOX:2 * H_FOX + GKW]
                A(gb[0:rows, :], b, ACT.Copy)
                A(q_dec[0:rows, :], b, ACT.Exp)
                A(k_neg[0:rows, :], b, ACT.Exp, scale=-1.0).then_inc(MM.free, 1)
                act.wait_ge(MM.full, MM.filled(at, "cumg"))
                bank = MM.ap(at, "cumg")
                A(k_dl[0:rows, :], bank[0:rows, 0:GKW], ACT.Copy)
                A(decay_s[:, :], bank[0:DK, GKW:GKW + H_GLA * DEC_BATCH], ACT.Exp).then_inc(MM.free, 1)
                act.wait_ge(done["gdiff"], t + 1)
                A(k_dl[0:rows, :], k_dl[0:rows, :], ACT.Exp).then_inc(done["gexpl"], 1)
                act.wait_ge(MM.full, MM.filled(at, "go"))
                take(at, "go", go_t, lambda b: b[:, 0:H_GLA * rows].rearrange("p (h q) -> p h q", q=rows)).then_inc(MM.free, 1)
                act.wait_ge(TP.free, TP.taken(at, "got"))
                gla_squares(at, t, rows, gqk[0:rows, :])
                root(rows, n=DV, inp=GSS, out=GSTD, w=H_GLA).then_inc(done["gstd"], 1)
                for n in ("fk", "fv", "lf"):
                    act.wait_ge(out_sem[n], 16 * (t + 1))
                act.wait_ge(done["s_sub"], 1)
                A(s_rows, s_rows, ACT.Exp).then_inc(done["s_exp"], 1)
                act.wait_ge(MM.full, MM.filled(at, "fo"))
                take(at, "fo", fo_t, lambda b: b[0:DH, :].rearrange("p (h q) -> p h q", q=rows)).then_inc(MM.free, 1)
                act.wait_ge(SC.free, SC.taken(at, "wout"))
                rms(xr, rows).then_inc(done["std_2"], 1)
                for i in range(2):
                    act.wait_ge(MM.full, MM.filled(at, f"cq{i}"))
                    take(at, f"cq{i}", c_qt[:, 4 * i:4 * i + 4, 0:rows], lambda b: b[:, :].rearrange("p (j q) -> p j q", j=4)[:, :, 0:rows],
                         scale=DH_MEM ** -0.5).then_inc(MM.free, 1)
                act.wait_ge(MM.full, MM.filled(at, "cs"))
                take(at, "cs", cs_t, lambda b: b[:, :].rearrange("p (s q) -> p s q", q=rows)).then_inc(MM.free, 1)
                act.wait_ge(done["c_sub"], 1)
                cross_exp(t, rows)
                for i in range(2):
                    act.wait_ge(MM.full, MM.filled(at, f"cu{i}"))
                    take(at, f"cu{i}", h_t[:, 4 * i:4 * i + 4, 0:rows], lambda b: b[:, :].rearrange("p (j q) -> p j q", j=4)[:, :, 0:rows]).then_inc(MM.free, 1)
                peer(at, t, rows)
                act.dma_start(outs["y"][SEQ:, :], xs[0:rows, :]).then_inc(out_sem["y"], 16)
                act.dma_start(outs["gs_s"].rearrange("(s d) v -> d s v", d=DK), states_s).then_inc(out_sem["gs"], 16)
                act.wait_ge(out_sem["y"], 16 * (t + 1))
                act.wait_ge(out_sem["gs"], 32)

            with act.Fori(0, TILES) as t:
                prompt_tile(t)
            act.wait_ge(done["merged"], TILES)
            act.dma_start(outs["gs"].rearrange("(h d) v -> d h v", h=H_GLA), state[:, :, :]).then_inc(out_sem["gs"], 16)
            act.wait_ge(out_sem["gs"], 16)
            sample_tile(TILES)

        @block.vector
        def _(dve):
            V = nc.vector

            def gained(at, name, gain, dst, rows, cols=P):
                bank = TP.ap(at, name)
                src = bank[0:cols, :].rearrange("p (j q) -> p j q", j=4)[:, :, 0:rows]
                if gain is None:
                    return V.tensor_copy(dst, src)
                return V.tensor_tensor(dst, src, gain.unsqueeze(2).to_broadcast([P, 4, rows]), ALU.mult)

            def scaled(rows):
                V.reciprocal(stats[0:rows, RSTD:RSTD + 1], stats[0:rows, STD:STD + 1])
                dve.drain()
                return V.tensor_scalar(xs[0:rows, :], xr[0:rows, :], stats[0:rows, RSTD:RSTD + 1], None, ALU.mult)

            V.memset(eps_col[:], EPS)
            V.memset(q_aug[:, :, DH:DH + 1], 1.0)
            V.memset(k_aug[:, :, DH + 1:DA], 1.0)
            V.memset(carry[:], 0.0)
            V.memset(state[:], 0.0)
            V.memset(kt_all[:], 0.0)
            V.memset(att_t[:], 0.0).then_inc(TP.free, TP.depth)
            dve.drain().then_inc(done["preset"], 1)
            dve.sem_inc(SC.free, SC.depth)
            dve.sem_inc(done["u_free"], UB)
            dve.sem_inc(done["acc_free"], 1)
            for n in ("gains", "sub", "ffn", "fin", "bias", "gate2"):
                dve.wait_ge(land[n], 16)
            dve.wait_ge(land["small"], 32)
            dve.wait_ge(done["consts"], 1)
            V.tensor_scalar(same_mask[:, :], same_low[:, :], 1.0, -NEG, ALU.subtract, ALU.mult)
            dve.wait_ge(land_s["pages"], 16)
            V.tensor_scalar(page_rows[:], pages[:], float(P), row_no[:, :], ALU.mult, ALU.add)
            V.tensor_scalar(page_cols[:], pages[:], float(DH), row_no[:, :], ALU.mult, ALU.add).then_inc(done["page_idx"], 1)
            at = ("setup", 0)
            for m, src in enumerate(mem_rows):
                dve.wait_ge(done["mem_ss"], m + 1)
                V.reciprocal(stats[:, RSTD:RSTD + 1], stats[:, STD:STD + 1])
                dve.drain()
                V.tensor_scalar(hb[:, :], src, stats[:, RSTD:RSTD + 1], None, ALU.mult).then_inc(done["mem_xs"], 1)
                for c in range(2):
                    dve.wait_ge(TP.full, TP.filled(at, f"mx{m}{c}"))
                    gained(at, f"mx{m}{c}", g_mem_c[:, 4 * c:4 * c + 4], mem_t[:, 4 * c:4 * c + 4, m * P:(m + 1) * P], P).then_inc(TP.free, 1)
            V.memset(v_all[:], 0.0)
            for c in range(2):
                for m in range(MC):
                    dve.wait_ge(TP.full, TP.filled(at, f"mk{m}{c}"))
                    gained(at, f"mk{m}{c}", None, mem_kt[:, 4 * c:4 * c + 4, m * P:(m + 1) * P], P).then_inc(TP.free, 1)

            def log_sigmoid(at, t, rows):
                dve.wait_ge(SC.full, SC.filled(at, "gg"))
                SCb = SC.ap(at, "gg")
                V.tensor_copy(gg_t[:, 0:rows], SCb[0:RANK, 0:rows]).then_inc(SC.free, 1)
                dve.wait_ge(MM.free, MM.taken(at, "gate"))
                z = zz[0:rows, :]
                V.tensor_tensor(z, z, bias_bc[0:rows, :], ALU.add)
                dve.drain()
                V.scalar_tensor_tensor(zl[0:rows, :], z, -1.0, z, ALU.mult, ALU.min).then_inc(done["zmin"], 1)
                dve.wait_ge(done["lnz"], t + 1)
                V.scalar_tensor_tensor(lf[0:rows, :], z, 0.0, zl[0:rows, :], ALU.min, ALU.subtract)
                dve.drain()
                V.tensor_scalar(lf[0:rows, H_FOX:], lf[0:rows, H_FOX:], 1.0 / TAU, None, ALU.mult).then_inc(done["lf"], 1)

            def gla_operands(t, rows):
                q, k = gqk[0:rows, 0:GKW], gqk[0:rows, GKW:]
                V.scalar_tensor_tensor(q_dec[0:rows, :], q, DK ** -0.5, q_dec[0:rows, :], ALU.mult, ALU.mult)
                V.tensor_tensor(k_neg[0:rows, :], k, k_neg[0:rows, :], ALU.mult).then_inc(done["q_dec"], 1)
                dve.wait_ge(done["gexpl"], t + 1)
                V.tensor_tensor(k_dl[0:rows, :], k, k_dl[0:rows, :], ALU.mult).then_inc(done["k_dl"], 1)

            def softmax_cross(rows, t):
                dve.wait_ge(done["c_exp"], t + 1)
                V.reciprocal(stats[0:rows, CINV:CINV + 4], stats[0:rows, CSUM:CSUM + 4])
                dve.drain()
                p = probs[0][0:rows, :].rearrange("p (h m) -> p h m", h=H_MEM)
                V.tensor_tensor(p, p, stats[0:rows, CINV:CINV + 4].unsqueeze(2).to_broadcast([rows, H_MEM, N_MEM]), ALU.mult).then_inc(done["p_norm"], 1)

            def choose(at, t, rows):
                R = slice(0, rows)
                for i in range(2):
                    dve.wait_ge(SC.full, SC.filled(at, f"ps{i}"))
                    bank = SC.ap(at, f"ps{i}")
                    apart(dve)
                    s = [bank[R, j * P:(j + 1) * P] for j in range(8)]
                    v = [vals[R, 8 * i + j, :] for j in range(8)]
                    x = [inds[R, 8 * i + j, :] for j in range(8)]
                    for j in range(8):
                        V.max(v[j][:, 0:8], s[j])
                    dve.drain()
                    for j in range(8):
                        V.match_replace(rest[R, j, :], v[j][:, 0:8], s[j], LOWEST)
                    dve.drain()
                    for j in range(8):
                        V.max(v[j][:, 8:16], rest[R, j, :])
                        ins = V.max_index(x[j][:, 0:8], v[j][:, 0:8], s[j])
                    ins.then_inc(SC.free, 1)
                    dve.drain()
                    for j in range(8):
                        V.max_index(x[j][:, 8:16], v[j][:, 8:16], rest[R, j, :])
                    dve.drain()
                V.tensor_copy(indf[R], inds[R])
                c4 = cand[R, :].rearrange("p (h i j) -> p h i j", h=H_PEER, i=TOPK)
                v4 = vals[R].rearrange("p (h s) k -> p h s k", s=2)
                V.tensor_tensor(c4, v4[:, :, 0, :].unsqueeze(3).to_broadcast([rows, H_PEER, TOPK, TOPK]),
                                v4[:, :, 1, :].unsqueeze(2).to_broadcast([rows, H_PEER, TOPK, TOPK]), ALU.add)
                dve.drain()
                c = [cand[R, h * 256:(h + 1) * 256] for h in range(H_PEER)]
                c2 = [cand2[R, h * 256:(h + 1) * 256] for h in range(H_PEER)]
                for h in range(H_PEER):
                    V.max(best[R, h, 0:8], c[h])
                dve.drain()
                for h in range(H_PEER):
                    V.match_replace(c2[h], best[R, h, 0:8], c[h], LOWEST)
                dve.drain()
                for h in range(H_PEER):
                    V.max(best[R, h, 8:16], c2[h])
                    V.max_index(besti[R, h, 0:8], best[R, h, 0:8], c[h])
                dve.drain()
                for h in range(H_PEER):
                    V.max_index(besti[R, h, 8:16], best[R, h, 8:16], c2[h])
                g3 = gates[R, :].rearrange("p (h k) -> p h k", h=H_PEER)
                V.tensor_tensor(g3, best[R], best[R, :, 0:1].to_broadcast([rows, H_PEER, TOPK]), ALU.subtract).then_inc(done["gate_sub"], 1)
                dve.drain()
                bi = besti[R].rearrange("p h k -> p (h k)")
                V.tensor_scalar(half_i[R, 0, :], bi, 4, None, ALU.logical_shift_right)
                V.tensor_scalar(half_i[R, 1, :], bi, TOPK - 1, None, ALU.bitwise_and)
                dve.drain()
                V.tensor_copy(half_f[R], half_i[R])
                dve.drain()
                eq = [a[R, :].rearrange("p (n j) -> p n j", j=TOPK) for a in (cand, cand2)]
                i4 = indf[R].rearrange("p (h s) k -> p h s k", s=2)
                for s in range(2):
                    V.tensor_tensor(eq[s], half_f[R, s, :].unsqueeze(2).to_broadcast([rows, SLOTS, TOPK]),
                                    iota_k[R, :].unsqueeze(1).to_broadcast([rows, SLOTS, TOPK]), ALU.is_equal)
                dve.drain()
                for s in range(2):
                    e4 = eq[s].rearrange("p (h k) j -> p h k j", h=H_PEER)
                    V.tensor_tensor(e4, e4, i4[:, :, s, :].unsqueeze(2).to_broadcast([rows, H_PEER, TOPK, TOPK]), ALU.mult)
                dve.drain()
                for s in range(2):
                    V.tensor_reduce(picked[R, s, :], eq[s], AX.X, ALU.add)
                dve.drain()
                V.scalar_tensor_tensor(experts[R, :], picked[R, 0, :], float(N_KEYS), picked[R, 1, :], ALU.mult, ALU.add).then_inc(done["experts"], 1)
                dve.wait_ge(done["gate_exp"], t + 1)
                V.tensor_reduce(gsum[R, :], g3, AX.X, ALU.add)
                dve.drain()
                V.reciprocal(ginv[R, :], gsum[R, :])
                dve.drain()
                V.tensor_tensor(g3, g3, ginv[R, :].unsqueeze(2).to_broadcast([rows, H_PEER, TOPK]), ALU.mult)
                dve.drain()

            def peer(at, t, rows):
                R = slice(0, rows)
                dve.wait_ge(SC.full, SC.filled(at, "wo"))
                bank = SC.ap(at, "wo")
                V.tensor_tensor(xr[R, :], xr[R, :], bank[R, :], ALU.add).then_inc(SC.free, 1)
                dve.wait_ge(done["std_3"], t + 1)
                V.reciprocal(stats[R, RSTD:RSTD + 1], stats[R, STD:STD + 1])
                dve.drain()
                V.scalar_tensor_tensor(hb[R, :], xr[R, :], stats[R, RSTD:RSTD + 1], g_ffn_bc[R, :], ALU.mult, ALU.mult).then_inc(done["hb_rows"], 1)
                for c in range(2):
                    dve.wait_ge(TP.full, TP.filled(at, f"f{c}"))
                    gained(at, f"f{c}", None, h_t[:, 4 * c:4 * c + 4, 0:rows], rows).then_inc(TP.free, 1)
                choose(at, t, rows)
                with dve.Fori(0, SLOTS // (2 * GROUP)) as it:
                    for g in range(2):
                        m = (t * 8 + it) * 2 + g
                        for s in range(GROUP):
                            n = g * GROUP + s
                            dve.wait_ge(u_land[n % UB], ((t * 8 + it) * (2 * GROUP // UB) + n // UB + 1) * 16)
                            u = u_ring[R, n % UB, :]
                            V.tensor_tensor_reduce(u, u, hb[R, :], 1.0, 0.0, ALU.mult, ALU.add, dots[R, g, s:s + 1]).then_inc(done["u_free"], 1)
                        dve.wait_ge(done["gelu"], m + 1)
                        V.tensor_tensor(wts[R, g, :], gelu[R, g, :], gates[R, bass.ds((it * 2 + g) * GROUP, GROUP)], ALU.mult).then_inc(done["wts"], 1)
                dve.wait_ge(done["std_y"], t + 1)
                V.reciprocal(stats[R, RSTD:RSTD + 1], stats[R, STD:STD + 1])
                dve.drain()
                V.scalar_tensor_tensor(xs[R, :], acc[R, :], stats[R, RSTD:RSTD + 1], g_fin_bc[R, :], ALU.mult, ALU.mult).then_inc(done["y_rows"], 1)
                dve.wait_ge(done["y_rows"], t + 1)
                dve.sem_inc(done["acc_free"], 1)

            def prompt_tile(t):
                at = ("prompt", t)
                dve.wait_ge(done["std_x"], t + 1)
                scaled(P).then_inc(done["xs_x"], 1)
                for c in range(2):
                    dve.wait_ge(TP.full, TP.filled(at, f"x{c}"))
                    gained(at, f"x{c}", g_mix_c[:, 4 * c:4 * c + 4], h_t[:, 4 * c:4 * c + 4, :], P).then_inc(TP.free, 1)
                log_sigmoid(at, t, P)
                dve.wait_ge(MM.free, MM.taken(at, "cumg"))
                V.tensor_tensor(k_dl[:, :], k_dl[:, :], gb[:, :], ALU.subtract).then_inc(done["gdiff"], 1)
                V.tensor_tensor(cums[:, 0:H_FOX], cums[:, 0:H_FOX], carry[:, :], ALU.add)
                dve.drain()
                V.tensor_tensor(carry[:, :], carry[:, :], cums[:, H_FOX:], ALU.add)
                V.tensor_copy(q_aug[:, :, DH + 1], cums[:, 0:H_FOX])
                V.tensor_scalar(k_aug[:, :, DH], cums[:, 0:H_FOX], -1.0, None, ALU.mult).then_inc(done["aug_cols"], 1)
                gla_operands(t, P)
                for c in range(2):
                    dve.wait_ge(TP.full, TP.filled(at, f"q{c}"))
                    gained(at, f"q{c}", None, q_t[:, 4 * c:4 * c + 4, :], P, DA).then_inc(TP.free, 1)
                for c in range(2):
                    dve.wait_ge(TP.full, TP.filled(at, f"k{c}"))
                    gained(at, f"k{c}", None, kt_all[0:DA, 4 * c:4 * c + 4, bass.ds(t * P, P)], P, DA).then_inc(TP.free, 1)
                dve.wait_ge(TP.full, TP.filled(at, "gq"))
                gained(at, "gq", None, qd_t[:, :, :], P, DK).then_inc(TP.free, 1)
                dve.wait_ge(TP.full, TP.filled(at, "gk"))
                gained(at, "gk", None, kn_t[:, :, :], P, DK).then_inc(TP.free, 1)

                def masked(h):
                    dve.wait_ge(SC.full, SC.filled(at, f"s{h}"))
                    bank = SC.ap(at, f"s{h}")
                    if h == 0:
                        dve.wait_ge(done["mask"], t + 1)
                    apart(dve)
                    mx = stats[:, FMAX + h:FMAX + h + 1]
                    V.tensor_tensor_reduce(probs[h % 2], bank[:, :], mask[:, :], 1.0, LOWEST,
                                           ALU.add, ALU.max, mx).then_inc(SC.free, 1)
                    dve.drain()
                    V.tensor_scalar(mx, mx, -1.0, None, ALU.mult).then_inc(done["fox_sub"], 1)

                masked(0)
                for h in range(H_FOX):
                    if h + 1 < H_FOX:
                        masked(h + 1)
                    for c in range(2):
                        dve.wait_ge(TP.full, TP.filled(at, f"P{h}{c}"))
                        gained(at, f"P{h}{c}", None, p_t[:, 4 * c:4 * c + 4, :], P).then_inc(TP.free, 1)
                dve.wait_ge(done["fox_exp"], (t + 1) * H_FOX)
                V.reciprocal(stats[:, FINV:FINV + 8], stats[:, FSUM:FSUM + 8]).then_inc(done["finv"], 1)
                dve.wait_ge(SC.full, SC.filled(at, "gatt"))
                bank = SC.ap(at, "gatt")
                apart(dve)
                V.copy_predicated(att_t[:, :, :], blk_up[:, :].bitcast(U32).unsqueeze(1).to_broadcast([P, H_GLA, P]),
                                  bank[:, 0:H_GLA * P].rearrange("p (h c) -> p h c", h=H_GLA)).then_inc(SC.free, 1)
                dve.wait_ge(SC.full, SC.filled(at, "gkv"))
                bank = SC.ap(at, "gkv")
                for ch, (new, old) in enumerate(((state1, state), (state, state1))):
                    if ch == 1:
                        dve.wait_ge(done["gstd"], t + 1)
                    for h in range(H_GLA):
                        ins = V.scalar_tensor_tensor(new[:, h, :], old[:, h, :], decay[:, NCH * h + ch:NCH * h + ch + 1],
                                                     bank[0:DK, (ch * H_GLA + h) * DV:(ch * H_GLA + h + 1) * DV], ALU.mult, ALU.add)
                    if ch == 0:
                        ins.then_inc(done["state1"], 1)
                ins.then_inc(SC.free, 1)
                V.reciprocal(stats[:, GINV:GINV + 4], stats[:, GSTD:GSTD + 4])
                dve.drain()
                for h in range(H_GLA):
                    r = slice(h * DV, (h + 1) * DV)
                    ins = V.scalar_tensor_tensor(hb[:, W + h * DV:W + (h + 1) * DV], gqk[:, r], stats[:, GINV + h:GINV + h + 1],
                                                 silu_r[:, r], ALU.mult, ALU.mult)
                ins.then_inc(done["merged"], 1)
                dve.wait_ge(TP.full, TP.filled(at, "m0"))
                gained(at, "m0", None, h_t[:, 0:4, :], P).then_inc(TP.free, 1)
                dve.wait_ge(TP.full, TP.filled(at, "m1"))
                gained(at, "m1", g_gla_c, h_t[:, 4:8, :], P).then_inc(TP.free, 1)
                dve.wait_ge(SC.full, SC.filled(at, "wout"))
                bank = SC.ap(at, "wout")
                V.tensor_tensor(xr[:, :], xr[:, :], bank[:, :], ALU.add).then_inc(SC.free, 1)
                dve.wait_ge(done["std_2"], t + 1)
                scaled(P).then_inc(done["xs_2"], 1)
                for c in range(2):
                    dve.wait_ge(TP.full, TP.filled(at, f"h{c}"))
                    gained(at, f"h{c}", g_cross_c[:, 4 * c:4 * c + 4], h_t[:, 4 * c:4 * c + 4, :], P).then_inc(TP.free, 1)
                dve.wait_ge(SC.full, SC.filled(at, "xs"))
                bank = SC.ap(at, "xs")
                b3 = bank[:, :].rearrange("p (h m) -> p h m", h=H_MEM)
                V.tensor_reduce(stats[:, CMAX:CMAX + 4], b3, AX.X, ALU.max)
                dve.drain()
                V.tensor_tensor(probs[0].rearrange("p (h m) -> p h m", h=H_MEM), b3,
                                stats[:, CMAX:CMAX + 4].unsqueeze(2).to_broadcast([P, H_MEM, N_MEM]), ALU.subtract).then_inc(SC.free, 1)
                softmax_cross(P, t)
                for c in range(2):
                    dve.wait_ge(TP.full, TP.filled(at, f"p{c}"))
                    gained(at, f"p{c}", None, p_t[:, 4 * c:4 * c + 4, :], P).then_inc(TP.free, 1)
                peer(at, t, P)

            def sample_tile(t):
                at = ("sample", t)
                rows = RS
                R = slice(0, rows)
                V.memset(att_t[:], 0.0)
                dve.wait_ge(done["std_x"], t + 1)
                scaled(rows).then_inc(done["xs_x"], 1)
                for c in range(2):
                    dve.wait_ge(TP.full, TP.filled(at, f"x{c}"))
                    gained(at, f"x{c}", g_mix_c[:, 4 * c:4 * c + 4], h_t[:, 4 * c:4 * c + 4, 0:rows], rows).then_inc(TP.free, 1)
                log_sigmoid(at, t, rows)
                dve.wait_ge(MM.free, MM.taken(at, "cumg"))
                V.tensor_tensor(k_dl[R, :], k_dl[R, :], gb[R, :], ALU.subtract).then_inc(done["gdiff"], 1)
                V.tensor_tensor(c_last[:], c_last[:], same_ind[:, :].unsqueeze(2).to_broadcast([rows, DEC_BATCH, H_FOX]), ALU.mult)
                dve.drain()
                V.tensor_reduce(c_rows[:, :], c_last[:].rearrange("p b h -> p h b"), AX.X, ALU.add)
                dve.drain()
                V.tensor_tensor(c_rows[:, :], c_rows[:, :], cums[R, 0:H_FOX], ALU.add)
                dve.drain()
                V.tensor_copy(q_aug[R, :, DH + 1], c_rows[:, :])
                V.tensor_scalar(k_aug[R, :, DH], c_rows[:, :], -1.0, None, ALU.mult).then_inc(done["aug_cols"], 1)
                gla_operands(t, rows)
                for c in range(2):
                    dve.wait_ge(TP.full, TP.filled(at, f"q{c}"))
                    gained(at, f"q{c}", None, q_t[:, 4 * c:4 * c + 4, 0:rows], rows, DA).then_inc(TP.free, 1)
                for c in range(2):
                    dve.wait_ge(TP.full, TP.filled(at, f"k{c}"))
                    gained(at, f"k{c}", None, k_new_t[:, 4 * c:4 * c + 4, 0:rows], rows, DA).then_inc(TP.free, 1)
                dve.wait_ge(TP.full, TP.filled(at, "gq"))
                gained(at, "gq", None, qd_t[:, :, 0:rows], rows, DK).then_inc(TP.free, 1)
                dve.wait_ge(TP.full, TP.filled(at, "gk"))
                gained(at, "gk", None, kn_t[:, :, 0:rows], rows, DK).then_inc(TP.free, 1)
                dve.wait_ge(done["k_dl"], t + 1)
                V.tensor_tensor(k_masked, k_dl[R, :].unsqueeze(1).to_broadcast([rows, DEC_BATCH, GKW]),
                                     same_ind[:, :].unsqueeze(2).to_broadcast([rows, DEC_BATCH, GKW]), ALU.mult).then_inc(done["k_masked"], 1)
                dve.wait_ge(SC.full, SC.filled(at, "gatt"))
                bank = SC.ap(at, "gatt")
                V.copy_predicated(att_t[R, :, 0:rows], same_up[:, :].bitcast(U32).unsqueeze(1).to_broadcast([rows, H_GLA, rows]),
                                  bank[R, 0:H_GLA * P].rearrange("p (h c) -> p h c", h=H_GLA)[:, :, 0:rows]).then_inc(SC.free, 1)
                dve.wait_ge(MM.free, MM.taken(at, "go"))
                for b in range(DEC_BATCH):
                    dve.wait_ge(SC.full, SC.filled(at, f"kv{b}"))
                    bank = SC.ap(at, f"kv{b}")
                    for h in range(H_GLA):
                        st = states_s[:, b * H_GLA + h, :]
                        ins = V.scalar_tensor_tensor(st, st, decay_s[:, DEC_BATCH * h + b:DEC_BATCH * h + b + 1],
                                                     bank[0:DK, h * DV:(h + 1) * DV], ALU.mult, ALU.add)
                    ins.then_inc(SC.free, 1)
                dve.wait_ge(TP.full, TP.filled(at, "got"))
                gained(at, "got", None, gqk[R, :].rearrange("p (h v) -> p h v", h=H_GLA), P, rows).then_inc(TP.free, 1)
                dve.wait_ge(SC.full, SC.filled(at, "past"))
                bank = SC.ap(at, "past")
                for page in range(N_PAGES):
                    r = slice(page * D // 2, (page + 1) * D // 2)
                    v4 = lambda a: a.rearrange("p (h b q) -> p h b q", h=H_FOX, b=DEC_BATCH)
                    ins = V.tensor_tensor(v4(work[:, r]), v4(bank[:, r]),
                                          c_past[:, page].rearrange("p b h -> p h b").unsqueeze(3).to_broadcast([P, H_FOX, DEC_BATCH, DEC_SEQ]),
                                          ALU.subtract)
                ins.then_inc(SC.free, 1)
                dve.wait_ge(SC.full, SC.filled(at, "new"))
                bank = SC.ap(at, "new")
                V.tensor_tensor(s_rows[:, :, N_PAGES * P:], bank[R, 0:H_FOX * rows].rearrange("p (h k) -> p h k", h=H_FOX),
                                same_mask[:, :].unsqueeze(1).to_broadcast([rows, H_FOX, rows]), ALU.add).then_inc(SC.free, 1)
                for i in range(4):
                    dve.wait_ge(TP.full, TP.filled(at, f"S{i}"))
                    bank = TP.ap(at, f"S{i}")
                    hs = slice(4 * (i % 2), 4 * (i % 2) + 4)
                    V.tensor_tensor(s_rows[:, hs, (i // 2) * P:(i // 2 + 1) * P], bank[R, :].rearrange("p (j k) -> p j k", j=4),
                                    c_rows[:, hs].unsqueeze(2).to_broadcast([rows, 4, P]), ALU.add).then_inc(TP.free, 1)
                dve.drain()
                V.tensor_reduce(stats[R, FMAX:FMAX + 8], s_rows, AX.X, ALU.max)
                dve.drain()
                V.tensor_tensor(s_rows, s_rows, stats[R, FMAX:FMAX + 8].unsqueeze(2).to_broadcast([rows, H_FOX, NK_S]), ALU.subtract).then_inc(done["s_sub"], 1)
                dve.wait_ge(done["s_exp"], 1)
                V.tensor_reduce(stats[R, FSUM:FSUM + 8], s_rows, AX.X, ALU.add)
                dve.drain()
                V.reciprocal(stats[R, FINV:FINV + 8], stats[R, FSUM:FSUM + 8])
                for i in range(4):
                    dve.wait_ge(TP.full, TP.filled(at, f"P{i}"))
                    gained(at, f"P{i}", None, past_p_t[:, 4 * i:4 * i + 4, :], rows).then_inc(TP.free, 1)
                dve.wait_ge(TP.full, TP.filled(at, "Pn"))
                bank = TP.ap(at, "Pn")
                V.tensor_copy(new_p_t, bank[R, 0:H_FOX * rows].rearrange("p (h q) -> p h q", q=rows)).then_inc(TP.free, 1)
                dve.wait_ge(TP.full, TP.filled(at, "fot"))
                bank = TP.ap(at, "fot")
                V.tensor_tensor(hb[R, 0:W].rearrange("p (h d) -> p h d", h=H_FOX), bank[R, :].rearrange("p (h d) -> p h d", h=H_FOX),
                                stats[R, FINV:FINV + 8].unsqueeze(2).to_broadcast([rows, H_FOX, DH]), ALU.mult).then_inc(TP.free, 1)
                dve.wait_ge(done["gstd"], t + 1)
                V.reciprocal(stats[R, GINV:GINV + 4], stats[R, GSTD:GSTD + 4])
                dve.drain()
                for h in range(H_GLA):
                    r = slice(h * DV, (h + 1) * DV)
                    ins = V.scalar_tensor_tensor(hb[R, W + h * DV:W + (h + 1) * DV], gqk[R, r], stats[R, GINV + h:GINV + h + 1],
                                                 silu_r[R, r], ALU.mult, ALU.mult)
                ins.then_inc(done["merged"], 1)
                dve.wait_ge(TP.full, TP.filled(at, "m0"))
                gained(at, "m0", None, h_t[:, 0:4, 0:rows], rows).then_inc(TP.free, 1)
                dve.wait_ge(TP.full, TP.filled(at, "m1"))
                gained(at, "m1", g_gla_c, h_t[:, 4:8, 0:rows], rows).then_inc(TP.free, 1)
                dve.wait_ge(SC.full, SC.filled(at, "wout"))
                bank = SC.ap(at, "wout")
                V.tensor_tensor(xr[R, :], xr[R, :], bank[R, :], ALU.add).then_inc(SC.free, 1)
                dve.wait_ge(done["std_2"], t + 1)
                scaled(rows).then_inc(done["xs_2"], 1)
                for c in range(2):
                    dve.wait_ge(TP.full, TP.filled(at, f"h{c}"))
                    gained(at, f"h{c}", g_cross_c[:, 4 * c:4 * c + 4], h_t[:, 4 * c:4 * c + 4, 0:rows], rows).then_inc(TP.free, 1)
                p3 = probs[0][R, :].rearrange("p (h m) -> p h m", h=H_MEM)
                for m in range(MC):
                    dve.wait_ge(TP.full, TP.filled(at, f"c{m}"))
                    bank = TP.ap(at, f"c{m}")
                    V.tensor_copy(p3[:, :, m * P:(m + 1) * P], bank[R, :].rearrange("p (h m) -> p h m", h=H_MEM)).then_inc(TP.free, 1)
                dve.drain()
                V.tensor_reduce(stats[R, CMAX:CMAX + 4], p3, AX.X, ALU.max)
                dve.drain()
                V.tensor_tensor(p3, p3, stats[R, CMAX:CMAX + 4].unsqueeze(2).to_broadcast([rows, H_MEM, N_MEM]), ALU.subtract).then_inc(done["c_sub"], 1)
                softmax_cross(rows, t)
                for c in range(2):
                    dve.wait_ge(TP.full, TP.filled(at, f"p{c}"))
                    gained(at, f"p{c}", None, p_t[:, 4 * c:4 * c + 4, 0:rows], rows).then_inc(TP.free, 1)
                peer(at, t, rows)

            with dve.Fori(0, TILES) as t:
                prompt_tile(t)
            sample_tile(TILES)

        @block.gpsimd
        def _(pool):
            G = nc.gpsimd
            made = [0]

            def step(ins):
                made[0] += 1
                ins.then_inc(done["made"], 1)
                pool.wait_ge(done["made"], made[0])

            def keep(ap, pattern, base, mult, fill=0.0):
                step(G.affine_select(out=ap, in_=ap, compare_op=ALU.is_ge, fill=fill, base=base, pattern=pattern, channel_multiplier=mult))

            step(G.memset(ones[:], 1.0))
            step(G.memset(upper[:], 1.0))
            keep(upper[:], [[1, P]], 0, -1)
            step(G.memset(ident[:], 1.0))
            keep(ident[:], [[1, P]], 0, -1)
            keep(ident[:], [[-1, P]], 0, 1)
            step(G.memset(causal[:], 0.0))
            keep(causal[:], [[-1, 2 * SEQ - P]], SEQ - P, 1, NEG)
            for tile_ in (blk_up, blk_one):
                step(G.memset(tile_[:], 1.0))
                v = tile_[:].rearrange("p (b c) -> p b c", b=NCH)
                keep(v, [[-CHUNK, NCH], [0, CHUNK]], 0, 1)
                keep(v, [[CHUNK, NCH], [0, CHUNK]], CHUNK - 1, -1)
            keep(blk_up[:], [[1, P]], 0, -1)
            step(G.memset(blk_ind[:], 1.0))
            keep(blk_ind[:], [[-CHUNK, NCH]], 0, 1)
            keep(blk_ind[:], [[CHUNK, NCH]], CHUNK - 1, -1)
            for tile_ in (same_up, same_one, same_low):
                step(G.memset(tile_[:], 1.0))
                v = tile_[:].rearrange("p (b c) -> p b c", b=DEC_BATCH)
                keep(v, [[-DEC_SEQ, DEC_BATCH], [0, DEC_SEQ]], 0, 1)
                keep(v, [[DEC_SEQ, DEC_BATCH], [0, DEC_SEQ]], DEC_SEQ - 1, -1)
            keep(same_up[:], [[1, RS]], 0, -1)
            keep(same_low[:], [[-1, RS]], 0, 1)
            step(G.memset(same_ind[:], 1.0))
            keep(same_ind[:], [[-DEC_SEQ, DEC_BATCH]], 0, 1)
            keep(same_ind[:], [[DEC_SEQ, DEC_BATCH]], DEC_SEQ - 1, -1)
            step(G.iota(row_no[:], pattern=[[0, 1]], base=0, channel_multiplier=1, allow_small_or_imprecise_dtypes=True))
            G.iota(iota_k[:], pattern=[[1, TOPK]], base=0, channel_multiplier=0, allow_small_or_imprecise_dtypes=True).then_inc(done["consts"], 1)

            def gathers(t, rows):
                pool.wait_ge(done["experts"], t + 1)
                apart(pool)
                with pool.Fori(0, SLOTS // (2 * GROUP)) as it:
                    for g in range(2):
                        m = (t * 8 + it) * 2 + g
                        G.tensor_copy(stage[0:rows, g, :], experts[0:rows, bass.ds((it * 2 + g) * GROUP, GROUP)]).then_inc(done["staged"], 1)
                        pool.wait_ge(done["staged"], m + 1)
                        for ring, land_, free, depth, table in ((u_ring, u_land, done["u_free"], UB, peer_u), (v_ring, v_land, done["v_free"], VB, peer_v)):
                            for s in range(GROUP):
                                n = g * GROUP + s
                                pool.wait_ge(free, (t * 8 + it) * 2 * GROUP + n + 1)
                                apart(pool)
                                G.indirect_dma_start(ring[0:rows, n % depth, :], None, table,
                                                     bass.IndirectOffsetOnAxis(ap=stage[0:rows, g, s:s + 1], axis=0)).then_inc(land_[n % depth], 16)

            pool.wait_ge(done["page_idx"], 1)
            for n in range(DEC_BATCH * N_PAGES):
                G.indirect_dma_start(lf_past[:, n // N_PAGES, n % N_PAGES, :], None, past_lf,
                                     bass.IndirectOffsetOnAxis(ap=page_rows[:, n:n + 1], axis=0)).then_inc(land_s["lf_past"], 16)
            with pool.Fori(0, TILES) as t:
                gathers(t, P)
                apart(pool)
            for n in range(DEC_BATCH * N_PAGES):
                G.indirect_dma_start(past_values[:, n, :], None, past_v,
                                     bass.IndirectOffsetOnAxis(ap=page_rows[:, n:n + 1], axis=0)).then_inc(land_s["values_past"], 16)
                if n == 0:
                    pool.wait_ge(done["u_free"], TILES * SLOTS + UB)
                if n >= UB:
                    pool.wait_ge(done["past_kept"], n - UB + 1)
                G.indirect_dma_start(past_keys[n % UB].rearrange("p h k -> p (h k)"), None, past_kt,
                                     bass.IndirectOffsetOnAxis(ap=page_cols[0:DH, n:n + 1], axis=0)).then_inc(key_land[n % UB], 16)
            gathers(TILES, RS)


def kernel(**inputs):
    import concourse.bacc as bacc
    from concourse.bass_utils import run_bass_kernel_spmd

    a = {k: np.asarray(v) for k, v in inputs.items()}
    c = np.ascontiguousarray
    cols = lambda g: g.reshape(-1, P).T
    arrays = {
        "x_all": np.concatenate([a["x_prompt"][0], a["x_sample"].reshape(RS, D), np.zeros((P - RS, D), np.float32)]),
        "page_table": c(a["page_table"].reshape(1, -1)),
        "past_kt": c(a["cache_fox_k"][0].transpose(0, 3, 2, 1).reshape(-1, H_FOX * P)),
        "past_v": a["cache_fox_v"][0].reshape(-1, H_FOX * DH),
        "past_lf": a["cache_fox_logf"][0].reshape(-1, H_FOX),
        "state_in": a["state_gla"][0].reshape(-1, DV),
        "smem_kt": c(a["cache_mem_k"][0].reshape(DEC_BATCH, N_MEM, D).transpose(0, 2, 1).reshape(-1, N_MEM)),
        "smem_v": a["cache_mem_v"][0].reshape(-1, D),
        "mem_prompt": a["mem_prompt"][0],
        "g_cols": c(np.concatenate([cols(a["g_mix"][0]), cols(a["g_cross"][0]), cols(a["g_mem"][0]), cols(a["g_gla_out"][0])], axis=1)),
        "w_in": a["w_in"][0],
        "bias_ls": np.concatenate([a["b_fox_f"][0], a["b_gla_gate"][0]]),
        "w_gate2": a["w_gla_gate2"][0],
        "w_out": a["w_out"][0],
        "w_mem_k": a["w_mem_k"][0], "w_mem_v": a["w_mem_v"][0],
        "w_cross_q": a["w_cross_q"][0], "w_cross_o": a["w_cross_o"][0],
        "g_ffn": a["g_ffn"][0],
        "peer_w_q": a["peer_w_q"][0],
        "subkeys_t": c(a["peer_subkeys"][0].transpose(2, 0, 1)),
        "peer_u": a["peer_u"][0], "peer_v": a["peer_v"][0],
        "g_final": a["g_final"],
    }
    results = {"y": (SEQ + RS, D), "fk": (SEQ + RS, H_FOX * DH), "fv": (SEQ + RS, H_FOX * DH), "lf": (SEQ + RS, H_FOX),
               "gs": (H_GLA * DK, DV), "mem_k": (N_MEM, D), "mem_v": (N_MEM, D), "gs_s": (DEC_BATCH * H_GLA * DK, DV)}
    nc = bacc.Bacc("TRN2", target_bir_lowering=False, num_devices=1)
    ins = {k: nc.dram_tensor(k, v.shape, mybir.dt.from_np(v.dtype), kind="ExternalInput").ap() for k, v in arrays.items()}
    outs = {k: nc.dram_tensor("out_" + k, s, F32, kind="ExternalOutput").ap() for k, s in results.items()}
    build(nc, ins, outs)
    r = run_bass_kernel_spmd(nc, [arrays], core_ids=[0]).results[0]
    o = {k: np.asarray(r["out_" + k]) for k in results}
    return (o["y"][:SEQ].reshape(1, SEQ, D), o["y"][SEQ:].reshape(DEC_BATCH, DEC_SEQ, D),
            o["fk"][:SEQ].reshape(1, 1, SEQ, H_FOX, DH), o["fv"][:SEQ].reshape(1, 1, SEQ, H_FOX, DH),
            o["lf"][:SEQ].reshape(1, 1, SEQ, H_FOX), o["gs"].reshape(1, 1, H_GLA, DK, DV),
            o["mem_k"].reshape(1, 1, N_MEM, H_MEM, DH_MEM), o["mem_v"].reshape(1, 1, N_MEM, H_MEM, DH_MEM),
            o["fk"][SEQ:].reshape(1, DEC_BATCH, DEC_SEQ, H_FOX, DH), o["fv"][SEQ:].reshape(1, DEC_BATCH, DEC_SEQ, H_FOX, DH),
            o["lf"][SEQ:].reshape(1, DEC_BATCH, DEC_SEQ, H_FOX), o["gs_s"].reshape(1, DEC_BATCH, H_GLA, DK, DV))
```

```python
from contextlib import ExitStack

import numpy as np

import concourse.bass as bass
from concourse import mybir

F32 = mybir.dt.float32
I32 = mybir.dt.int32
U32 = mybir.dt.uint32
BF16 = mybir.dt.bfloat16
ACT = mybir.ActivationFunctionType
ALU = mybir.AluOpType
AX = mybir.AxisListType

P = 128
D = 1024
KC = D // P
SEQ = 1024
TILES = SEQ // P
DEC_BATCH, DEC_SEQ = 8, 8
RS = DEC_BATCH * DEC_SEQ
N_PAGES = 2
H_FOX, DH = 8, 64
DA = DH + 2
H_GLA, DK, DV = 4, 64, 128
CHUNK = 64
NCH = P // CHUNK
RANK = 16
TAU = 16.0
N_MEM = 256
MC = N_MEM // P
H_MEM, DH_MEM = 4, 256
N_KEYS = 128
H_PEER = 8
TOPK = 16
SLOTS = H_PEER * TOPK
EPS = 1e-6
NEG = -1e30
LOWEST = -3.0e38
GKW = H_GLA * DK
NLS = H_FOX + GKW
OFF_FQ, OFF_FK, OFF_FV, OFF_FF = 0, 512, 1024, 1536
OFF_GQK, OFF_GV, OFF_GG, OFF_GR, D_IN = 1544, 2056, 2568, 2584, 3096
W = 512
GROUP = 8
HALF = GROUP // 2
HALVES = SLOTS // HALF
LAG = 8
UB = 4
VB = 4
WB = 2
KB = 4
V_FIRST = 10
KEY_STEP = 16

MM_SETUP = [f"mem{m}{w}{c}" for w in "kv" for c in range(2) for m in range(MC)]
MM_PROMPT = ["fq", "fk", "fv", "gqk", "gv", "gr", "small", "gate", "cum", "cumg", "fo", "go",
             "cq0", "cq1", "cu0", "cu1", "pq0", "pq1", "pq2", "pq3"]
TP_SETUP = [f"mx{m}{c}" for m in range(MC) for c in range(2)] + [f"mk{m}{c}" for c in range(2) for m in range(MC)]
TP_PROMPT = (["x0", "x1", "q0", "q1", "k0", "k1", "gq", "gk"] + [f"P{h}{c}" for h in range(H_FOX) for c in range(2)]
             + ["m0", "m1", "h0", "h1", "p0", "p1", "f0", "f1"])
SC_PROMPT = ["gg"] + [f"s{h}" for h in range(H_FOX)] + ["gatt", "gkv", "wout", "xs", "wo", "ps0", "ps1"]
MM_SAMPLE = ["fq", "fk", "fv", "gqk", "gv", "gr", "small", "gate", "cpast", "cum", "cumg", "go", "fo",
             "cq0", "cq1", "cs", "cu0", "cu1", "pq0", "pq1", "pq2", "pq3"]
TP_SAMPLE = (["x0", "x1", "q0", "q1", "k0", "k1", "gq", "gk", "got"] + [f"S{i}" for i in range(4)]
             + [f"P{i}" for i in range(4)] + ["Pn", "fot", "m0", "m1", "h0", "h1", "c0", "c1", "p0", "p1", "f0", "f1"])
SC_SAMPLE = ["gg", "gatt"] + [f"kv{b}" for b in range(DEC_BATCH)] + ["past", "new", "wout", "wo", "ps0", "ps1"]


CUTS = ([("x", 1)] + [(f"in{k}", 1) for k in range(6)] + [("small", 1), ("gate", 0), ("lf", 1), ("cum", 1), ("turn", 1)]
        + [(f"h{h}", 1) for h in range(H_FOX)] + [("gla", 1), ("kv", 1), ("merge", 1), ("wout", 1), ("cq0", 1), ("cq1", 1),
        ("cross", 2), ("cu", 1), ("wo", 1)] + [(f"pq{i}", 1) for i in range(4)] + [("half0", 1), ("half1", 2), ("sums", 2), ("best", 2)])
SAMPLE_CUTS = ([("x", 2)] + [(f"in{k}", 1) for k in range(6)] + [("small", 1), ("gate", 1), ("lf", 1), ("cum", 1), ("turn", 1),
               ("kv1", 1), ("kv3", 1), ("kv5", 1), ("soft", 2), ("fo1", 1), ("fo3", 1), ("fo5", 1), ("merge", 1), ("wout", 1),
               ("cq0", 1), ("cq1", 1), ("cs1", 1), ("cs3", 1), ("cs5", 1), ("cu1", 1), ("cu3", 1), ("cu5", 1)]
               + [(f"pq{i}", 1) for i in range(4)] + [("half0", 1), ("half1", 1), ("sums", 1), ("best", 2)])


def numbered(cuts):
    count = [n for _, n in cuts]
    assert sum(count) == HALVES + LAG
    return {name: range(sum(count[:i]), sum(count[:i + 1])) for i, (name, _) in enumerate(cuts)}


STEPS_AT = {"prompt": numbered(CUTS), "sample": numbered(SAMPLE_CUTS)}
assert STEPS_AT["sample"]["soft"].start == KEY_STEP and (KEY_STEP - LAG) % 4 == 0


def mixed(at):
    return not (isinstance(at[1], int) and at[1] == 0)


class Banks:

    def __init__(self, nc, ctx, name, depth, width, setup, prompt, sample):
        self.full = ctx.enter_context(nc.semaphore(f"{name}_full"))
        self.free = ctx.enter_context(nc.semaphore(f"{name}_free"))
        self.bank = [ctx.enter_context(nc.psum_tensor(f"{name}{i}", [P, width], F32)) for i in range(depth)]
        self.depth = depth
        self.plans = {"setup": setup, "prompt": prompt, "sample": sample}
        assert len(setup) % depth == 0 and len(prompt) % depth == 0

    def number(self, at, name):
        plan, t = at
        k = self.plans[plan].index(name)
        if plan == "setup":
            return k
        return len(self.plans["setup"]) + t * len(self.plans["prompt"]) + k

    def ap(self, at, name):
        return self.bank[self.plans[at[0]].index(name) % self.depth]

    def turn(self, at, name):
        return self.number(at, name) + 1

    def filled(self, at, name):
        return self.number(at, name) + 1

    def taken(self, at, name):
        return self.number(at, name) + 1 + self.depth


def build(nc, ins, outs):
    (x_all, page_table, past_kt, past_v, past_lf, state_in, smem_kt, smem_v, mem_prompt, g_cols, w_in, bias_ls, w_gate2,
     w_out, w_mem_k, w_mem_v, w_cross_q, w_cross_o, g_ffn, peer_w_q, subkeys_t, peer_u, peer_v, g_final) = (
        ins[n] for n in ("x_all page_table past_kt past_v past_lf state_in smem_kt smem_v mem_prompt g_cols w_in bias_ls "
                         "w_gate2 w_out w_mem_k w_mem_v w_cross_q w_cross_o g_ffn peer_w_q subkeys_t peer_u peer_v "
                         "g_final").split())
    with ExitStack() as ctx:
        def sb(name, shape, dt=F32):
            return ctx.enter_context(nc.sbuf_tensor(name, shape, dt))

        def sem(name):
            return ctx.enter_context(nc.semaphore(name))

        MM = Banks(nc, ctx, "mm", 2, 512, MM_SETUP, MM_PROMPT, MM_SAMPLE)
        TP = Banks(nc, ctx, "tp", 2, 512, TP_SETUP, TP_PROMPT, TP_SAMPLE)
        SC = Banks(nc, ctx, "sc", 1, 1024, [], SC_PROMPT, SC_SAMPLE)
        acc = ctx.enter_context(nc.psum_tensor("acc", [P, D], F32))

        kt_all = sb("kt_all", [P, H_FOX, SEQ])
        v_all = sb("v_all", [P, TILES, H_FOX * DH])
        mem_kt = sb("mem_kt", [P, KC, N_MEM])
        mem_v = sb("mem_v", [P, MC, D])
        state = sb("state", [DK, H_GLA, DV])
        carry = sb("carry", [P, H_FOX])
        ident = sb("ident", [P, P])
        causal = sb("causal", [P, 2 * SEQ - P], BF16)
        upper = sb("upper", [P, P])
        ones = sb("ones", [P, P])
        blk_up = sb("blk_up", [P, P])
        blk_one = sb("blk_one", [P, P])
        blk_ind = sb("blk_ind", [P, NCH])
        iota_k = sb("iota_k", [P, TOPK])
        eps_col = sb("eps_col", [P, 1])
        gains_t = sb("gains_t", [P, 3 * KC + H_GLA])
        g_ffn_bc = sb("g_ffn_bc", [P, D])
        bias_bc = sb("bias_bc", [P, NLS])
        gate2 = sb("gate2", [RANK, GKW])
        w_small = sb("w_small", [P, KC, H_FOX + RANK])
        same_ind = sb("same_ind", [RS, DEC_BATCH])
        row_no = sb("row_no", [P, 1])
        pages = sb("pages", [P, DEC_BATCH * N_PAGES], I32)
        page_rows = sb("page_rows", [P, DEC_BATCH * N_PAGES], I32)
        page_cols = sb("page_cols", [P, DEC_BATCH * N_PAGES], I32)
        c_rows = sb("c_rows", [RS, H_FOX])
        decay_s = sb("decay_s", [DK, H_GLA * DEC_BATCH])
        sub_t = sb("sub_t", [P, 2, N_KEYS])
        w_ring = sb("w_ring", [P, WB, KC, W])
        u_ring = sb("u_ring", [P, UB, D])
        v_ring = sb("v_ring", [P, VB, D])
        xr = sb("xr", [P, D])
        xs = sb("xs", [P, D])
        h_t = sb("h_t", [P, KC, P])
        hb = sb("hb", [P, D])
        rows_p = sb("rows_p", [P, D])
        diag = sb("diag", [P, GROUP, P])
        q_aug = sb("q_aug", [P, H_FOX, DA])
        k_aug = sb("k_aug", [P, H_FOX, DA])
        gqk = sb("gqk", [P, 2 * GKW])
        gv = sb("gv", [P, H_GLA * DV])
        silu_r = sb("silu_r", [P, H_GLA * DV])
        gg = sb("gg", [P, RANK])
        lf = sb("lf", [P, NLS])
        cums = sb("cums", [P, 2 * H_FOX])
        gb = sb("gb", [P, GKW])
        q_dec = sb("q_dec", [P, GKW])
        k_neg = sb("k_neg", [P, GKW])
        k_dl = sb("k_dl", [P, GKW])
        decay = sb("decay", [DK, H_GLA * NCH])
        att_t = sb("att_t", [P, H_GLA, P])
        stats = sb("stats", [P, 64])
        work = sb("work", [P, 5120])
        gates = sb("gates", [P, SLOTS])
        experts = sb("experts", [P, SLOTS], I32)
        stage = sb("stage", [P, 2, 2, GROUP], I32)
        dots = sb("dots", [P, 2, GROUP])
        gelu = sb("gelu", [P, 2, GROUP])
        wts = sb("wts", [P, 2, GROUP])
        gsum = sb("gsum", [P, H_PEER])
        ginv = sb("ginv", [P, H_PEER])

        g_mix_c, g_cross_c, g_mem_c = (gains_t[:, i * KC:(i + 1) * KC] for i in range(3))
        g_gla_c = gains_t[:, 3 * KC:3 * KC + H_GLA]
        SSQ, STD, RSTD, FMAX, FSUM, FINV, GSS, GSTD, GINV, CMAX, CSUM, CINV, YSQ, YSTD, YINV = (
            0, 1, 2, 8, 16, 24, 32, 36, 40, 44, 48, 52, 56, 57, 58)
        probs = [work[:, i * D:(i + 1) * D] for i in range(2)]
        p_t = work[:, 2 * D:3 * D].rearrange("p (j q) -> p j q", j=KC)
        c_qt = work[:, 3 * D:4 * D].rearrange("p (j q) -> p j q", j=KC)
        pq_t = work[:, 3 * D:5 * D].rearrange("p (j q) -> p j q", j=2 * H_PEER)
        mem_t = work[:, 0:2 * D].rearrange("p (j m) -> p j m", j=KC)
        mem_k_rows = work[:, 2 * D:4 * D].rearrange("p (m c n) -> p m c n", m=MC, c=2)
        zz, zl = xs[:, 0:NLS], xs[:, NLS:2 * NLS]
        gg_t = xs[0:RANK, 2 * NLS:2 * NLS + P]
        state1 = work[0:DK, D:D + W].rearrange("p (h v) -> p h v", h=H_GLA)
        junk = diag[:].rearrange("p s q -> p (s q)")
        mask = h_t[:, 0:4, :].rearrange("p a b -> p (a b)").bitcast(BF16)
        q_t = work[0:DA, 3 * D:4 * D].rearrange("p (h q) -> p h q", h=H_FOX)
        qd_t = work[0:DK, 4 * D:4 * D + W].rearrange("p (h q) -> p h q", h=H_GLA)
        kn_t = work[0:DK, 4 * D + W:5 * D].rearrange("p (h q) -> p h q", h=H_GLA)
        lists = lambda a, shape: a.rearrange("p (a b) -> p a b", a=shape[0])
        vals = lists(gqk[:, 0:256], (2 * H_PEER, TOPK))
        indf = lists(gqk[:, 256:512], (2 * H_PEER, TOPK))
        half_f = lists(gv[:, 0:256], (2, SLOTS))
        picked = lists(gv[:, 256:512], (2, SLOTS))
        inds = lists(silu_r[:, 0:256].bitcast(U32), (2 * H_PEER, TOPK))
        best = lists(silu_r[:, 256:384], (H_PEER, TOPK))
        besti = lists(silu_r[:, 384:512].bitcast(U32), (H_PEER, TOPK))
        half_i = lists(gb[:, :].bitcast(U32), (2, SLOTS))
        mem_rows = [v_all[:, 2 * m:2 * m + 2, :].rearrange("p c n -> p (c n)") for m in range(MC)]
        states_s = v_all[0:DK].rearrange("p t n -> p (t n)").rearrange("p (s v) -> p s v", v=DV)
        big = kt_all[:].rearrange("p h k -> p (h k)")
        mem_area = [mem_kt[:].rearrange("p c m -> p (c m)"), mem_v[:].rearrange("p m n -> p (m n)")]
        past_keys = [mem_area[i // 2][0:DH, i % 2 * D:(i % 2 + 1) * D].rearrange("p (h k) -> p h k", h=H_FOX) for i in range(KB)]
        past_values = ([big[:, n * W:(n + 1) * W] for n in range(V_FIRST)]
                       + [mem_area[n // 4][:, n % 4 * W:(n % 4 + 1) * W] for n in range(DEC_BATCH * N_PAGES - V_FIRST)])
        s_mem_k = [big[:, i * 2 * D:(i + 1) * 2 * D].rearrange("p (j m) -> p j m", j=KC) for i in range(2)]
        s_mem_v = [big[:, (2 + i) * 2 * D:(3 + i) * 2 * D].rearrange("p (m n) -> p m n", m=MC) for i in range(2)]
        beside = big[:, V_FIRST * W:]
        k_masked = beside[0:RS, 0:DEC_BATCH * GKW].rearrange("p (b n) -> p b n", b=DEC_BATCH)
        NK_S = N_PAGES * P + RS
        s_rows = beside[0:RS, 0:H_FOX * NK_S].rearrange("p (h k) -> p h k", h=H_FOX)
        small = beside[:, H_FOX * NK_S:]
        lf_past = small[:, 0:P].rearrange("p (b n h) -> p b n h", b=DEC_BATCH, n=N_PAGES)
        c_past = small[:, P:2 * P].rearrange("p (n b h) -> p n b h", b=DEC_BATCH, n=N_PAGES)
        c_last = small[0:RS, 2 * P:2 * P + RS].rearrange("p (b h) -> p b h", b=DEC_BATCH)
        same_up, same_one, same_mask = (small[0:RS, 2 * P + i * RS:2 * P + (i + 1) * RS] for i in range(1, 4))
        past_scores = work[:, 0:D].rearrange("p (s q) -> p s q", q=RS)
        past_p_t = past_scores
        k_new_t = work[0:DA, D:2 * D].rearrange("p (h q) -> p h q", h=H_FOX)
        go_t = work[:, 2 * D:2 * D + H_GLA * RS].rearrange("p (h q) -> p h q", q=RS)
        new_p_t = work[0:RS, 2 * D:2 * D + W].rearrange("p (h q) -> p h q", q=RS)
        cs_t = work[:, 2 * D:2 * D + W].rearrange("p (s q) -> p s q", q=RS)
        v_new = work[0:RS, 2 * D + W:3 * D]
        fo_t = work[0:DH, 3 * D:3 * D + W].rearrange("p (h q) -> p h q", q=RS)
        rest = work[:, 0:D].rearrange("p (j q) -> p j q", j=KC)
        cand = work[:, D:3 * D]
        cand2 = work[:, 3 * D:5 * D]

        names = ("page_idx c_sub s_sub s_exp fo_norm k_masked past_q new_kt smk_used smv_used past_kept mask preset made copied consts same mem_ss mem_xs std_x xs_x zmin lnz lf gdiff aug_cols q_dec gexpl k_dl fox_sub fox_exp "
                 "finv gstd merged std_2 xs_2 c_exp p_norm std_3 hb_rows gate_sub gate_exp experts staged gelu "
                 "wts diag acc_set state1 u_free v_free acc_free std_y y_rows").split()
        done = {n: sem(n) for n in names}
        land = {n: sem("landed_" + n) for n in "x mem page gains ffn fin bias gate2 small sub past_kt0 past_kt1 past_v past_lf s_state smk0 smk1 smv0 smv1".split()}
        w_land = [sem(f"w_land{i}") for i in range(WB)]
        u_land = [sem(f"u_land{i}") for i in range(UB)]
        v_land = [sem(f"v_land{i}") for i in range(VB)]
        land_s = {n: sem("landed_" + n) for n in ("state_s", "lf_past", "pages", "values_past")}
        key_land = [sem(f"key_land{i}") for i in range(KB)]
        smk_land = [sem(f"smk_land{i}") for i in range(2)]
        smv_land = [sem(f"smv_land{i}") for i in range(2)]
        out_sem = {n: sem("stored_" + n) for n in "fk fv lf y gs mk0 mk1 mv0 mv1".split()}

        def all_steps(eng, step, t):
            for k in range(LAG):
                step(t, k, k)
            with eng.Fori(0, (HALVES - LAG) // GROUP * 2) as it:
                for j in range(GROUP // 2):
                    step(t, it * (GROUP // 2) + (LAG + j), LAG + j)
            for k in range(HALVES, HALVES + LAG):
                step(t, k, k)

        def apart(eng):
            eng.sem_inc(done["copied"], 1)

        block = ctx.enter_context(nc.Block())

        chunks = ([(w_in, o) for o in (OFF_FQ, OFF_FK, OFF_FV, OFF_GQK, OFF_GV, OFF_GR)]
                  + [(w, o) for w in (w_out, w_cross_q, w_cross_o) for o in (0, W)]
                  + [(peer_w_q, i * W) for i in range(4)])
        NCHUNK = len(chunks)
        mem_chunks = [(w_mem_k, 0), (w_mem_k, W), (w_mem_v, 0), (w_mem_v, W)]
        NMEMC = len(mem_chunks)
        chunk_user = ([(MM, n) for n in ("fq", "fk", "fv", "gqk", "gv", "gr")] + [(SC, "wout")] * 2
                      + [(MM, "cq0"), (MM, "cq1")] + [(SC, "wo")] * 2 + [(MM, f"pq{i}") for i in range(4)])
        c_in, c_out, c_cq, c_co, c_pq = 0, 6, 8, 10, 12
        assert NCHUNK % WB == 0 and NMEMC % WB == 0

        @block.sync
        def _(sp):
            def load_chunk(which, n):
                src, off = which
                sp.dma_start(w_ring[:, n % WB], src.rearrange("(c p) n -> p c n", p=P)[:, :, off:off + W]
                             ).then_inc(w_land[n % WB], 16)

            def mem_load(b, which):
                if b >= 2:
                    sp.wait_ge(done["smk_used"] if which == "k" else done["smv_used"], b - 1)
                if which == "k":
                    sp.dma_start(s_mem_k[b % 2], smem_kt[b * D:(b + 1) * D, :].rearrange("(c p) m -> p c m", p=P)).then_inc(smk_land[b % 2], 16)
                else:
                    sp.dma_start(s_mem_v[b % 2], smem_v[b * N_MEM:(b + 1) * N_MEM, :].rearrange("(m p) n -> p m n", p=P)).then_inc(smv_land[b % 2], 16)

            def tile_loads(at):
                for k in range(NCHUNK - WB):
                    if at[0] == "sample" and k == c_out:
                        sp.wait_ge(MM.full, MM.number(at, "fo") + 1)
                        for b in range(2):
                            mem_load(b, "k")
                            mem_load(b, "v")
                    if at[0] == "sample" and k == c_co:
                        for which in "kv":
                            for b in range(2, DEC_BATCH):
                                mem_load(b, which)
                    bank, name = chunk_user[k]
                    sp.wait_ge(bank.full, bank.number(at, name) + 1)
                    load_chunk(chunks[k + WB], k + WB)

            sp.dma_start(v_all[:, 0:2, :], mem_prompt[0:P, :].rearrange("p (c n) -> p c n", c=2)).then_inc(land["mem"], 16)
            load_chunk(mem_chunks[0], 0)
            load_chunk(mem_chunks[1], 1)
            sp.dma_start(gains_t[:], g_cols).then_inc(land["gains"], 16)
            sp.dma_start(sub_t[:], subkeys_t).then_inc(land["sub"], 16)
            sp.dma_start(g_ffn_bc[:], g_ffn.partition_broadcast(P)).then_inc(land["ffn"], 16)
            sp.dma_start(bias_bc[:], bias_ls.partition_broadcast(P)).then_inc(land["bias"], 16)
            sp.dma_start(pages[:], page_table.partition_broadcast(P)).then_inc(land_s["pages"], 16)
            sp.dma_start(gate2[:], w_gate2).then_inc(land["gate2"], 16)
            w_rows = w_in.rearrange("(c p) n -> p c n", p=P)
            sp.dma_start(w_small[:, :, 0:H_FOX], w_rows[:, :, OFF_FF:OFF_FF + H_FOX]).then_inc(land["small"], 16)
            sp.dma_start(w_small[:, :, H_FOX:], w_rows[:, :, OFF_GG:OFF_GG + RANK]).then_inc(land["small"], 16)
            sp.dma_start(xr[:], x_all[0:P, :]).then_inc(land["x"], 16)
            sp.dma_start(v_all[:, 2:4, :], mem_prompt[P:2 * P, :].rearrange("p (c n) -> p c n", c=2)).then_inc(land["mem"], 16)
            for k in range(NMEMC):
                sp.wait_ge(MM.full, MC * (k + 1))
                load_chunk((mem_chunks + chunks)[k + WB], k + WB)
            def first_loads(t):
                for k in range(WB):
                    sp.wait_ge(MM.full, MM.number(("prompt", t - 1), f"pq{4 - WB + k}") + 1)
                    load_chunk(chunks[k], k)
                sp.wait_ge(done["acc_set"], t)
                sp.dma_start(xr[:], x_all[bass.ds(t * P, P), :]).then_inc(land["x"], 16)

            tile_loads(("prompt", 0))
            with sp.Fori(1, TILES) as t:
                first_loads(t)
                tile_loads(("prompt", t))
                apart(sp)
            sp.dma_start(states_s, state_in.rearrange("(s d) v -> d s v", d=DK)).then_inc(land_s["state_s"], 16)
            first_loads(TILES)
            tile_loads(("sample", TILES))

        @block.tensor
        def _(pe):
            def transposes(at, name, src, rows, cols, n, pitch=P):
                bank = TP.ap(at, name)
                if cols == DK:
                    apart(pe)
                for j in range(n):
                    ins = nc.tensor.transpose(bank[0:cols, j * pitch:j * pitch + rows], src(j), ident[0:rows, 0:rows])
                return ins

            def rows_times(bank, lhs, k, rows):
                for c in range(KC):
                    ins = nc.tensor.matmul(bank, lhs[:, c, 0:rows], w_ring[:, k % WB, c, :], start=(c == 0), stop=(c == KC - 1))
                return ins

            def chunk_times(bank, rhs, k, rows):
                for f in range(W // P):
                    for c in range(KC):
                        ins = nc.tensor.matmul(bank[:, f * P:f * P + rows], w_ring[:, k % WB, c, f * P:(f + 1) * P],
                                               rhs[:, c, 0:rows], start=(c == 0), stop=(c == KC - 1))
                return ins

            at = ("setup", 0)
            pe.wait_ge(done["consts"], 1)
            pe.sem_inc(done["v_free"], VB)
            for m in range(MC):
                pe.wait_ge(done["mem_xs"], m + 1)
                for c in range(2):
                    pe.wait_ge(TP.free, TP.turn(at, f"mx{m}{c}"))
                    transposes(at, f"mx{m}{c}", lambda j: hb[:, (4 * c + j) * P:(4 * c + j + 1) * P], P, P, 4).then_inc(TP.full, 1)
            pe.wait_ge(TP.free, TP.taken(at, "mx11"))
            for k, wv in enumerate("kkvv"):
                pe.wait_ge(w_land[k % WB], 16 * (k // WB + 1))
                for m in range(MC):
                    name = f"mem{m}{wv}{k % 2}"
                    pe.wait_ge(MM.free, MM.turn(at, name))
                    bank = MM.ap(at, name)
                    for c in range(KC):
                        ins = nc.tensor.matmul(bank[:, :], mem_t[:, c, m * P:(m + 1) * P], w_ring[:, k % WB, c, :],
                                               start=(c == 0), stop=(c == KC - 1))
                    ins.then_inc(MM.full, 1)
                    if wv == "k":
                        pe.wait_ge(MM.free, MM.taken(at, name))
                        pe.wait_ge(TP.free, TP.turn(at, f"mk{m}{k % 2}"))
                        transposes(at, f"mk{m}{k % 2}", lambda j: mem_k_rows[:, m, k % 2, j * P:(j + 1) * P], P, P, 4).then_inc(TP.full, 1)

            def loads(t, k):
                return (NMEMC // WB + t * (NCHUNK // WB) + k // WB + 1) * 16

            def peer_step(t, k, like):
                if like < LAG:
                    return
                pe.wait_ge(done["diag"], t * HALVES + k - LAG + 1)
                for s in range(HALF):
                    pe.wait_ge(v_land[s], (t * HALVES + k - LAG + 1) * 16)
                    for c in range(2):
                        ins = nc.tensor.matmul(acc[:, c * W:(c + 1) * W], diag[:, (like % 2) * HALF + s, :],
                                               v_ring[:, s, c * W:(c + 1) * W], start=False, stop=True, skip_group_check=True)
                    ins.then_inc(done["v_free"], 1)

            def cut(at, name):
                if mixed(at):
                    for k in STEPS_AT[at[0]].get(name, ()):
                        peer_step(at[1] - 1, k, k)

            def front(at, t, rows):
                cut(at, "x")
                pe.wait_ge(done["xs_x"], t + 1)
                for c in range(2):
                    pe.wait_ge(TP.free, TP.turn(at, f"x{c}"))
                    transposes(at, f"x{c}", lambda j: xs[0:rows, (4 * c + j) * P:(4 * c + j + 1) * P], rows, P, 4).then_inc(TP.full, 1)
                pe.wait_ge(TP.free, TP.taken(at, "x1"))
                for k, name in enumerate(MM_PROMPT[:6]):
                    pe.wait_ge(MM.free, MM.turn(at, name))
                    pe.wait_ge(w_land[k % WB], loads(t, k))
                    rows_times(MM.ap(at, name)[0:rows, :], h_t, k, rows).then_inc(MM.full, 1)
                    cut(at, f"in{k}")
                pe.wait_ge(MM.free, MM.turn(at, "small"))
                bank = MM.ap(at, "small")
                for c in range(KC):
                    ins = nc.tensor.matmul(bank[0:rows, 0:H_FOX + RANK], h_t[:, c, 0:rows], w_small[:, c, :],
                                           start=(c == 0), stop=(c == KC - 1))
                ins.then_inc(MM.full, 1)
                cut(at, "small")
                pe.wait_ge(MM.free, MM.taken(at, "small"))
                pe.wait_ge(SC.free, SC.turn(at, "gg"))
                bank = SC.ap(at, "gg")
                nc.tensor.transpose(bank[0:RANK, 0:rows], gg[0:rows, :], ident[0:rows, 0:rows]).then_inc(SC.full, 1)
                pe.wait_ge(SC.free, SC.taken(at, "gg"))
                pe.wait_ge(MM.free, MM.turn(at, "gate"))
                bank = MM.ap(at, "gate")
                nc.tensor.matmul(bank[0:rows, 0:GKW], gg_t[:, 0:rows], gate2[:, :], start=True, stop=True).then_inc(MM.full, 1)
                cut(at, "gate")
                cut(at, "lf")

            def turn_heads(at, t, rows):
                pe.wait_ge(done["aug_cols"], t + 1)
                for name, src in (("q", q_aug), ("k", k_aug)):
                    for c in range(2):
                        pe.wait_ge(TP.free, TP.turn(at, f"{name}{c}"))
                        transposes(at, f"{name}{c}", lambda j: src[0:rows, 4 * c + j, :], rows, DA, 4).then_inc(TP.full, 1)
                pe.wait_ge(done["q_dec"], t + 1)
                for name, src in (("gq", q_dec), ("gk", k_neg)):
                    pe.wait_ge(TP.free, TP.turn(at, name))
                    transposes(at, name, lambda j: src[0:rows, j * DK:(j + 1) * DK], rows, DK, 4).then_inc(TP.full, 1)

            def peer_scores(at, t, rows):
                pe.wait_ge(done["hb_rows"], t + 1)
                pe.wait_ge(TP.free, TP.turn(at, "f0"))
                transposes(at, "f0", lambda j: hb[0:rows, (0 + j) * P:(0 + j + 1) * P], rows, P, 4).then_inc(TP.full, 1)
                pe.wait_ge(TP.free, TP.turn(at, "f1"))
                transposes(at, "f1", lambda j: hb[0:rows, (4 + j) * P:(4 + j + 1) * P], rows, P, 4).then_inc(TP.full, 1)
                pe.wait_ge(TP.free, TP.taken(at, "f1"))
                for i in range(4):
                    pe.wait_ge(MM.free, MM.turn(at, f"pq{i}"))
                    pe.wait_ge(w_land[(c_pq + i) % WB], loads(t, c_pq + i))
                    chunk_times(MM.ap(at, f"pq{i}"), h_t, c_pq + i, rows).then_inc(MM.full, 1)
                    cut(at, f"pq{i}")
                pe.wait_ge(MM.free, MM.taken(at, "pq3"))
                for i in range(2):
                    pe.wait_ge(SC.free, SC.turn(at, f"ps{i}"))
                    bank = SC.ap(at, f"ps{i}")
                    for j in range(8):
                        hh = 8 * i + j
                        ins = nc.tensor.matmul(bank[0:rows, j * P:(j + 1) * P], pq_t[:, hh, 0:rows], sub_t[:, hh % 2, :],
                                               start=True, stop=True)
                    ins.then_inc(SC.full, 1)
                    cut(at, f"half{i}")
                cut(at, "sums")
                cut(at, "best")
                pe.wait_ge(done["acc_free"], t + 1)
                for c in range(2):
                    ins = nc.tensor.matmul(acc[:, c * W:(c + 1) * W], ident[:, :], xr[:, c * W:(c + 1) * W],
                                           start=True, stop=True, skip_group_check=True)
                ins.then_inc(done["acc_set"], 1)

            def prompt_tile(t, seen):
                at = ("prompt", t)
                front(at, t, P)
                pe.wait_ge(done["lf"], t + 1)
                pe.wait_ge(MM.free, MM.turn(at, "cum"))
                bank = MM.ap(at, "cum")
                nc.tensor.matmul(bank[:, 0:H_FOX], upper[:, :], lf[:, 0:H_FOX], start=True, stop=True)
                nc.tensor.matmul(bank[:, H_FOX:2 * H_FOX], ones[:, :], lf[:, 0:H_FOX], start=True, stop=True)
                nc.tensor.matmul(bank[:, 2 * H_FOX:2 * H_FOX + GKW], blk_up[:, :], lf[:, H_FOX:NLS],
                                 start=True, stop=True).then_inc(MM.full, 1)
                pe.wait_ge(MM.free, MM.turn(at, "cumg"))
                bank = MM.ap(at, "cumg")
                nc.tensor.matmul(bank[:, 0:GKW], blk_one[:, :], lf[:, H_FOX:NLS], start=True, stop=True)
                for h in range(H_GLA):
                    ins = nc.tensor.matmul(bank[0:DK, GKW + NCH * h:GKW + NCH * (h + 1)],
                                           lf[:, H_FOX + h * DK:H_FOX + (h + 1) * DK], blk_ind[:, :], start=True, stop=True)
                ins.then_inc(MM.full, 1)
                cut(at, "cum")
                turn_heads(at, t, P)
                cut(at, "turn")
                pe.wait_ge(TP.free, TP.taken(at, "gk"))

                def scores(h):
                    pe.wait_ge(SC.free, SC.turn(at, f"s{h}"))
                    bank = SC.ap(at, f"s{h}")
                    for c in range(seen * P // W):
                        ins = nc.tensor.matmul(bank[:, c * W:(c + 1) * W], q_t[:, h, :], kt_all[0:DA, h, c * W:(c + 1) * W],
                                               start=True, stop=True)
                    ins.then_inc(SC.full, 1)

                scores(0)
                pe.wait_ge(MM.free, MM.turn(at, "fo"))
                fo = MM.ap(at, "fo")
                for h in range(H_FOX):
                    if h + 1 < H_FOX:
                        scores(h + 1)
                    cut(at, f"h{h}")
                    pe.wait_ge(done["fox_exp"], t * H_FOX + h + 1)
                    for c in range(seen * P // W):
                        pe.wait_ge(TP.free, TP.turn(at, f"P{h}{c}"))
                        transposes(at, f"P{h}{c}", lambda j: probs[h % 2][:, (4 * c + j) * P:(4 * c + j + 1) * P], P, P, 4).then_inc(TP.full, TILES // seen)
                    pe.wait_ge(TP.free, TP.taken(at, f"P{h}1"))
                    for j in range(seen):
                        ins = nc.tensor.matmul(fo[:, h * DH:(h + 1) * DH], p_t[:, j, :], v_all[:, j, h * DH:(h + 1) * DH],
                                               start=(j == 0), stop=(j == seen - 1))
                ins.then_inc(MM.full, 1)
                cut(at, "gla")
                pe.wait_ge(SC.free, SC.turn(at, "gatt"))
                bank = SC.ap(at, "gatt")
                for h in range(H_GLA):
                    ins = nc.tensor.matmul(bank[:, h * P:(h + 1) * P], kn_t[:, h, :], qd_t[:, h, :], start=True, stop=True)
                ins.then_inc(SC.full, 1)
                pe.wait_ge(SC.free, SC.turn(at, "gkv"))
                bank = SC.ap(at, "gkv")
                pe.wait_ge(done["k_dl"], t + 1)
                apart(pe)
                for ch in range(NCH):
                    r = slice(ch * CHUNK, (ch + 1) * CHUNK)
                    for h in range(H_GLA):
                        ins = nc.tensor.matmul(bank[0:DK, (ch * H_GLA + h) * DV:(ch * H_GLA + h + 1) * DV],
                                               k_dl[r, h * DK:(h + 1) * DK], gv[r, h * DV:(h + 1) * DV], start=True, stop=True)
                ins.then_inc(SC.full, 1)
                cut(at, "kv")
                pe.wait_ge(MM.free, MM.turn(at, "go"))
                bank = MM.ap(at, "go")
                pe.wait_ge(done["state1"], t + 1)
                for h in range(H_GLA):
                    o = bank[:, h * DV:(h + 1) * DV]
                    nc.tensor.matmul(o, att_t[:, h, :], gv[:, h * DV:(h + 1) * DV], start=True, stop=False, skip_group_check=True)
                    for ch in range(NCH):
                        r = slice(ch * CHUNK, (ch + 1) * CHUNK)
                        ins = nc.tensor.matmul(bank[r, h * DV:(h + 1) * DV], qd_t[:, h, r], (state, state1)[ch][:, h, :],
                                               start=False, stop=True, skip_group_check=True)
                ins.then_inc(MM.full, 1)
                cut(at, "merge")
                pe.wait_ge(done["merged"], t + 1)
                pe.wait_ge(TP.free, TP.turn(at, "m0"))
                transposes(at, "m0", lambda j: hb[0:P, (0 + j) * P:(0 + j + 1) * P], P, P, 4).then_inc(TP.full, 1)
                pe.wait_ge(TP.free, TP.turn(at, "m1"))
                transposes(at, "m1", lambda j: hb[0:P, (4 + j) * P:(4 + j + 1) * P], P, P, 4).then_inc(TP.full, 1)
                pe.wait_ge(TP.free, TP.taken(at, "m1"))
                pe.wait_ge(SC.free, SC.turn(at, "wout"))
                pe.wait_ge(w_land[c_out % WB], loads(t, c_out))
                rows_times(SC.ap(at, "wout")[0:P, 0:W], h_t, c_out, P)
                pe.wait_ge(w_land[(c_out + 1) % WB], loads(t, c_out + 1))
                rows_times(SC.ap(at, "wout")[0:P, W:D], h_t, c_out + 1, P).then_inc(SC.full, 1)
                cut(at, "wout")
                pe.wait_ge(done["xs_2"], t + 1)
                pe.wait_ge(TP.free, TP.turn(at, "h0"))
                transposes(at, "h0", lambda j: xs[0:P, (0 + j) * P:(0 + j + 1) * P], P, P, 4).then_inc(TP.full, 1)
                pe.wait_ge(TP.free, TP.turn(at, "h1"))
                transposes(at, "h1", lambda j: xs[0:P, (4 + j) * P:(4 + j + 1) * P], P, P, 4).then_inc(TP.full, 1)
                pe.wait_ge(TP.free, TP.taken(at, "h1"))
                pe.wait_ge(MM.free, MM.turn(at, "cq0"))
                pe.wait_ge(w_land[(c_cq) % WB], loads(t, c_cq))
                chunk_times(MM.ap(at, "cq0"), h_t, c_cq, P).then_inc(MM.full, 1)
                cut(at, "cq0")
                pe.wait_ge(MM.free, MM.turn(at, "cq1"))
                pe.wait_ge(w_land[(c_cq + 1) % WB], loads(t, c_cq + 1))
                chunk_times(MM.ap(at, "cq1"), h_t, c_cq + 1, P).then_inc(MM.full, 1)
                cut(at, "cq1")
                pe.wait_ge(MM.free, MM.taken(at, "cq1"))
                pe.wait_ge(SC.free, SC.turn(at, "xs"))
                bank = SC.ap(at, "xs")
                for h in range(H_MEM):
                    for c in range(2):
                        ins = nc.tensor.matmul(bank[:, h * N_MEM:(h + 1) * N_MEM], c_qt[:, 2 * h + c, :], mem_kt[:, 2 * h + c, :],
                                               start=(c == 0), stop=(c == 1))
                ins.then_inc(SC.full, 1)
                cut(at, "cross")
                pe.wait_ge(done["p_norm"], t + 1)
                pe.wait_ge(TP.free, TP.turn(at, "p0"))
                transposes(at, "p0", lambda j: probs[0][0:P, (0 + j) * P:(0 + j + 1) * P], P, P, 4).then_inc(TP.full, 1)
                pe.wait_ge(TP.free, TP.turn(at, "p1"))
                transposes(at, "p1", lambda j: probs[0][0:P, (4 + j) * P:(4 + j + 1) * P], P, P, 4).then_inc(TP.full, 1)
                pe.wait_ge(TP.free, TP.taken(at, "p1"))
                for i in range(2):
                    pe.wait_ge(MM.free, MM.turn(at, f"cu{i}"))
                    bank = MM.ap(at, f"cu{i}")
                    for j in range(4):
                        d = 4 * i + j
                        for m in range(MC):
                            ins = nc.tensor.matmul(bank[:, j * P:(j + 1) * P], mem_v[:, m, d * P:(d + 1) * P],
                                                   p_t[:, 2 * (d // 2) + m, :], start=(m == 0), stop=(m == MC - 1))
                    ins.then_inc(MM.full, 1)
                cut(at, "cu")
                pe.wait_ge(MM.free, MM.taken(at, "cu1"))
                pe.wait_ge(SC.free, SC.turn(at, "wo"))
                pe.wait_ge(w_land[c_co % WB], loads(t, c_co))
                rows_times(SC.ap(at, "wo")[0:P, 0:W], h_t, c_co, P)
                pe.wait_ge(w_land[(c_co + 1) % WB], loads(t, c_co + 1))
                rows_times(SC.ap(at, "wo")[0:P, W:D], h_t, c_co + 1, P).then_inc(SC.full, 1)
                cut(at, "wo")
                peer_scores(at, t, P)

            def sample_tile(t):
                at = ("sample", t)
                rows = RS
                seq = [slice(b * DEC_SEQ, (b + 1) * DEC_SEQ) for b in range(DEC_BATCH)]
                front(at, t, rows)
                pe.wait_ge(land_s["lf_past"], 16 * DEC_BATCH * N_PAGES)
                pe.wait_ge(MM.free, MM.turn(at, "cpast"))
                bank = MM.ap(at, "cpast")
                n = DEC_BATCH * H_FOX
                first, second = lf_past[:, :, 0, :], lf_past[:, :, 1, :]
                nc.tensor.matmul(bank[:, 0:n], upper[:, :], first, start=True, stop=True)
                nc.tensor.matmul(bank[:, n:2 * n], upper[:, :], second, start=True, stop=False)
                nc.tensor.matmul(bank[:, n:2 * n], ones[:, :], first, start=False, stop=True)
                nc.tensor.matmul(bank[0:rows, 2 * n:3 * n], ones[:, 0:rows], first, start=True, stop=False)
                nc.tensor.matmul(bank[0:rows, 2 * n:3 * n], ones[:, 0:rows], second, start=False, stop=True).then_inc(MM.full, 1)
                pe.wait_ge(done["lf"], t + 1)
                pe.wait_ge(done["same"], 1)
                pe.wait_ge(MM.free, MM.turn(at, "cum"))
                bank = MM.ap(at, "cum")
                nc.tensor.matmul(bank[0:rows, 0:H_FOX], same_up[:, :], lf[0:rows, 0:H_FOX], start=True, stop=True)
                nc.tensor.matmul(bank[0:rows, 2 * H_FOX:2 * H_FOX + GKW], same_up[:, :], lf[0:rows, H_FOX:NLS],
                                 start=True, stop=True).then_inc(MM.full, 1)
                pe.wait_ge(MM.free, MM.turn(at, "cumg"))
                bank = MM.ap(at, "cumg")
                nc.tensor.matmul(bank[0:rows, 0:GKW], same_one[:, :], lf[0:rows, H_FOX:NLS], start=True, stop=True)
                for h in range(H_GLA):
                    ins = nc.tensor.matmul(bank[0:DK, GKW + DEC_BATCH * h:GKW + DEC_BATCH * (h + 1)],
                                           lf[0:rows, H_FOX + h * DK:H_FOX + (h + 1) * DK], same_ind[:, :], start=True, stop=True)
                ins.then_inc(MM.full, 1)
                cut(at, "cum")
                turn_heads(at, t, rows)
                cut(at, "turn")
                pe.wait_ge(TP.free, TP.taken(at, "gk"))
                pe.wait_ge(SC.free, SC.turn(at, "gatt"))
                bank = SC.ap(at, "gatt")
                for h in range(H_GLA):
                    ins = nc.tensor.matmul(bank[0:rows, h * P:h * P + rows], kn_t[:, h, 0:rows], qd_t[:, h, 0:rows], start=True, stop=True)
                ins.then_inc(SC.full, 1)
                pe.wait_ge(MM.free, MM.turn(at, "go"))
                bank = MM.ap(at, "go")
                pe.wait_ge(SC.free, SC.taken(at, "gatt"))
                pe.wait_ge(land_s["state_s"], 16)
                for h in range(H_GLA):
                    nc.tensor.matmul(bank[:, h * rows:(h + 1) * rows], gv[0:rows, h * DV:(h + 1) * DV], att_t[0:rows, h, 0:rows],
                                     start=True, stop=False, skip_group_check=True)
                    for b in range(DEC_BATCH):
                        ins = nc.tensor.matmul(bank[:, h * rows + b * DEC_SEQ:h * rows + (b + 1) * DEC_SEQ], states_s[:, b * H_GLA + h, :],
                                               qd_t[:, h, seq[b]], start=False, stop=True, skip_group_check=True)
                ins.then_inc(MM.full, 1)
                pe.wait_ge(done["k_masked"], 1)
                for b in range(DEC_BATCH):
                    pe.wait_ge(SC.free, SC.turn(at, f"kv{b}"))
                    bank = SC.ap(at, f"kv{b}")
                    for h in range(H_GLA):
                        ins = nc.tensor.matmul(bank[0:DK, h * DV:(h + 1) * DV], k_masked[:, b, h * DK:(h + 1) * DK],
                                               gv[0:rows, h * DV:(h + 1) * DV], start=True, stop=True)
                    ins.then_inc(SC.full, 1)
                    cut(at, f"kv{b}")
                pe.wait_ge(MM.free, MM.taken(at, "go"))
                pe.wait_ge(TP.free, TP.turn(at, "got"))
                transposes(at, "got", lambda j: go_t[:, j, :], P, rows, 4).then_inc(TP.full, 1)
                pe.wait_ge(SC.free, SC.turn(at, "past"))
                bank = SC.ap(at, "past")
                for b in range(DEC_BATCH):
                    for page in range(N_PAGES):
                        n = b * N_PAGES + page
                        pe.wait_ge(key_land[n % KB], 16 * (n // KB + 1))
                        for h in range(H_FOX):
                            c = (page * H_FOX + h) * rows + b * DEC_SEQ
                            ins = nc.tensor.matmul(bank[:, c:c + DEC_SEQ], past_keys[n % KB][:, h, :], q_t[0:DH, h, seq[b]],
                                                   start=True, stop=True)
                        if n == DEC_BATCH * N_PAGES - 1:
                            ins.then_inc(SC.full, 1)
                        else:
                            ins.then_inc(done["past_kept"], 1)
                pe.wait_ge(SC.free, SC.turn(at, "new"))
                bank = SC.ap(at, "new")
                for h in range(H_FOX):
                    ins = nc.tensor.matmul(bank[0:rows, h * rows:(h + 1) * rows], q_t[:, h, 0:rows], k_new_t[:, h, 0:rows], start=True, stop=True)
                ins.then_inc(SC.full, 1)
                for i in range(4):
                    pe.wait_ge(TP.free, TP.turn(at, f"S{i}"))
                    transposes(at, f"S{i}", lambda j: past_scores[:, 4 * i + j, :], P, rows, 4).then_inc(TP.full, 1)
                cut(at, "soft")
                pe.wait_ge(done["s_exp"], 1)
                for i in range(4):
                    pe.wait_ge(TP.free, TP.turn(at, f"P{i}"))
                    transposes(at, f"P{i}", lambda j: s_rows[:, 4 * (i % 2) + j, (i // 2) * P:(i // 2 + 1) * P], rows, P, 4).then_inc(TP.full, 1)
                pe.wait_ge(TP.free, TP.turn(at, "Pn"))
                transposes(at, "Pn", lambda j: s_rows[:, j, N_PAGES * P:], rows, rows, 8, pitch=rows).then_inc(TP.full, 1)
                pe.wait_ge(TP.free, TP.taken(at, "Pn"))
                pe.wait_ge(land_s["values_past"], 16 * DEC_BATCH * N_PAGES)
                pe.wait_ge(MM.free, MM.turn(at, "fo"))
                bank = MM.ap(at, "fo")
                for b in range(DEC_BATCH):
                    for h in range(H_FOX):
                        o = bank[0:DH, h * rows + b * DEC_SEQ:h * rows + (b + 1) * DEC_SEQ]
                        for page in range(N_PAGES):
                            nc.tensor.matmul(o, past_values[b * N_PAGES + page][:, h * DH:(h + 1) * DH],
                                             past_p_t[:, page * H_FOX + h, seq[b]], start=(page == 0), stop=False)
                        ins = nc.tensor.matmul(o, v_new[:, h * DH:(h + 1) * DH], new_p_t[:, h, seq[b]], start=False, stop=True)
                    if b == DEC_BATCH - 1:
                        ins.then_inc(MM.full, 1)
                    cut(at, f"fo{b}")
                pe.wait_ge(MM.free, MM.taken(at, "fo"))
                pe.wait_ge(TP.free, TP.turn(at, "fot"))
                transposes(at, "fot", lambda j: fo_t[:, j, :], DH, rows, 8, pitch=DH).then_inc(TP.full, 1)
                cut(at, "merge")
                pe.wait_ge(done["merged"], t + 1)
                pe.wait_ge(TP.free, TP.turn(at, "m0"))
                transposes(at, "m0", lambda j: hb[0:rows, (0 + j) * P:(0 + j + 1) * P], rows, P, 4).then_inc(TP.full, 1)
                pe.wait_ge(TP.free, TP.turn(at, "m1"))
                transposes(at, "m1", lambda j: hb[0:rows, (4 + j) * P:(4 + j + 1) * P], rows, P, 4).then_inc(TP.full, 1)
                pe.wait_ge(TP.free, TP.taken(at, "m1"))
                pe.wait_ge(SC.free, SC.turn(at, "wout"))
                pe.wait_ge(w_land[c_out % WB], loads(t, c_out))
                rows_times(SC.ap(at, "wout")[0:rows, 0:W], h_t, c_out, rows)
                pe.wait_ge(w_land[(c_out + 1) % WB], loads(t, c_out + 1))
                rows_times(SC.ap(at, "wout")[0:rows, W:D], h_t, c_out + 1, rows).then_inc(SC.full, 1)
                cut(at, "wout")
                pe.wait_ge(done["xs_2"], t + 1)
                pe.wait_ge(TP.free, TP.turn(at, "h0"))
                transposes(at, "h0", lambda j: xs[0:rows, (0 + j) * P:(0 + j + 1) * P], rows, P, 4).then_inc(TP.full, 1)
                pe.wait_ge(TP.free, TP.turn(at, "h1"))
                transposes(at, "h1", lambda j: xs[0:rows, (4 + j) * P:(4 + j + 1) * P], rows, P, 4).then_inc(TP.full, 1)
                pe.wait_ge(TP.free, TP.taken(at, "h1"))
                pe.wait_ge(MM.free, MM.turn(at, "cq0"))
                pe.wait_ge(w_land[(c_cq) % WB], loads(t, c_cq))
                chunk_times(MM.ap(at, "cq0"), h_t, c_cq, rows).then_inc(MM.full, 1)
                cut(at, "cq0")
                pe.wait_ge(MM.free, MM.turn(at, "cq1"))
                pe.wait_ge(w_land[(c_cq + 1) % WB], loads(t, c_cq + 1))
                chunk_times(MM.ap(at, "cq1"), h_t, c_cq + 1, rows).then_inc(MM.full, 1)
                cut(at, "cq1")
                pe.wait_ge(MM.free, MM.taken(at, "cq1"))
                pe.wait_ge(MM.free, MM.turn(at, "cs"))
                bank = MM.ap(at, "cs")
                for b in range(DEC_BATCH):
                    pe.wait_ge(smk_land[b % 2], 16 * (b // 2 + 1))
                    for h in range(H_MEM):
                        for m in range(MC):
                            o = (m * H_MEM + h) * rows + b * DEC_SEQ
                            for c in range(2):
                                ins = nc.tensor.matmul(bank[:, o:o + DEC_SEQ], s_mem_k[b % 2][:, 2 * h + c, m * P:(m + 1) * P],
                                                       c_qt[:, 2 * h + c, seq[b]], start=(c == 0), stop=(c == 1))
                    if b < DEC_BATCH - 1:
                        ins.then_inc(done["smk_used"], 1)
                    else:
                        ins.then_inc(MM.full, 1)
                    cut(at, f"cs{b}")
                pe.wait_ge(MM.free, MM.taken(at, "cs"))
                for m in range(MC):
                    pe.wait_ge(TP.free, TP.turn(at, f"c{m}"))
                    transposes(at, f"c{m}", lambda j: cs_t[:, m * H_MEM + j, :], P, rows, 4).then_inc(TP.full, 1)
                pe.wait_ge(done["p_norm"], t + 1)
                pe.wait_ge(TP.free, TP.turn(at, "p0"))
                transposes(at, "p0", lambda j: probs[0][0:rows, (0 + j) * P:(0 + j + 1) * P], rows, P, 4).then_inc(TP.full, 1)
                pe.wait_ge(TP.free, TP.turn(at, "p1"))
                transposes(at, "p1", lambda j: probs[0][0:rows, (4 + j) * P:(4 + j + 1) * P], rows, P, 4).then_inc(TP.full, 1)
                pe.wait_ge(TP.free, TP.taken(at, "p1"))
                pe.wait_ge(MM.free, MM.turn(at, "cu1"))
                banks = [MM.ap(at, f"cu{i}") for i in range(2)]
                for b in range(DEC_BATCH):
                    pe.wait_ge(smv_land[b % 2], 16 * (b // 2 + 1))
                    for d in range(KC):
                        o = (d % 4) * P + b * DEC_SEQ
                        for m in range(MC):
                            ins = nc.tensor.matmul(banks[d // 4][:, o:o + DEC_SEQ], s_mem_v[b % 2][:, m, d * P:(d + 1) * P],
                                                   p_t[:, 2 * (d // 2) + m, seq[b]], start=(m == 0), stop=(m == MC - 1))
                        if b == DEC_BATCH - 1 and d % 4 == 3:
                            ins.then_inc(MM.full, 1)
                    if b < DEC_BATCH - 1:
                        ins.then_inc(done["smv_used"], 1)
                    cut(at, f"cu{b}")
                pe.wait_ge(MM.free, MM.taken(at, "cu1"))
                pe.wait_ge(SC.free, SC.turn(at, "wo"))
                pe.wait_ge(w_land[c_co % WB], loads(t, c_co))
                rows_times(SC.ap(at, "wo")[0:rows, 0:W], h_t, c_co, rows)
                pe.wait_ge(w_land[(c_co + 1) % WB], loads(t, c_co + 1))
                rows_times(SC.ap(at, "wo")[0:rows, W:D], h_t, c_co + 1, rows).then_inc(SC.full, 1)
                peer_scores(at, t, rows)

            prompt_tile(0, TILES // 2)
            with pe.Fori(1, TILES // 2) as t:
                prompt_tile(t, TILES // 2)
            with pe.Fori(TILES // 2, TILES) as t:
                prompt_tile(t, TILES)
            sample_tile(TILES)
            all_steps(pe, peer_step, TILES)

        @block.scalar
        def _(act):
            A = nc.scalar.activation

            def root(rows, n=D, inp=SSQ, out=STD, w=1):
                act.drain()
                return A(stats[0:rows, out:out + w], stats[0:rows, inp:inp + w], ACT.Sqrt, scale=1.0 / n, bias=eps_col[0:rows, :])

            def rms(src, rows):
                A(xs[0:rows, :], src[0:rows, :], ACT.Square, accum_out=stats[0:rows, SSQ:SSQ + 1])
                return root(rows)

            def take(at, name, out, shape, func=ACT.Copy, **kw):
                return A(out, shape(MM.ap(at, name)), func, **kw)

            act.sem_inc(MM.free, MM.depth)
            act.wait_ge(done["consts"], 1)
            act.wait_ge(done["preset"], 1)
            at = ("setup", 0)
            act.wait_ge(land["mem"], 32)
            for m, src in enumerate(mem_rows):
                if m == 1:
                    act.wait_ge(done["mem_xs"], 1)
                A(xs[:, :], src, ACT.Square, accum_out=stats[:, SSQ:SSQ + 1])
                root(P).then_inc(done["mem_ss"], 1)
            for k, wv in enumerate("kkvv"):
                for m in range(MC):
                    name = f"mem{m}{wv}{k % 2}"
                    dst = mem_k_rows[:, m, k % 2, :] if wv == "k" else mem_v[:, m, (k % 2) * W:(k % 2 + 1) * W]
                    act.wait_ge(MM.full, MM.filled(at, name))
                    take(at, name, dst, lambda b: b[:, :]).then_inc(MM.free, 1)
            act.wait_ge(MM.free, MM.taken(at, "mem1v1"))
            for m in range(MC):
                act.dma_start(outs["mem_k"][m * P:(m + 1) * P, :].rearrange("p (c n) -> p c n", c=2), mem_k_rows[:, m, :, :]).then_inc(out_sem["mk0"], 16)
                act.dma_start(outs["mem_v"][m * P:(m + 1) * P, :], mem_v[:, m, :]).then_inc(out_sem["mk0"], 16)

            def peer_step(t, k, like):
                if LAG - 1 <= like < LAG - 1 + HALVES:
                    h = like - (LAG - 1)
                    if h % 2 == 0:
                        act.wait_ge(done["wts"], t * HALVES + k - LAG + 3)
                    if h >= 1:
                        act.wait_ge(done["v_free"], t * SLOTS + k * HALF - LAG * HALF + VB)
                    for s in range(h % 2 * HALF, (h % 2 + 1) * HALF):
                        ins = A(diag[:, s, :], ident[:, :], ACT.Copy, scale=wts[:, h // 2 % 2, s:s + 1])
                    ins.then_inc(done["diag"], 1)
                if like % 2 == 1 and 3 <= like < 3 + HALVES:
                    g = (like - 3) // 2 % 2
                    act.wait_ge(done["u_free"], t * SLOTS + k * HALF - HALF + UB)
                    A(gelu[:, g, :], dots[:, g, :], ACT.Gelu_apprx_tanh).then_inc(done["gelu"], 2)
                if like == HALVES + 1:
                    act.dma_start(rows_p[:], g_final.partition_broadcast(P)).then_inc(land["fin"], 16)

            def cut(at, name):
                if mixed(at):
                    for k in STEPS_AT[at[0]].get(name, ()):
                        peer_step(at[1] - 1, k, k)

            def cuts(at, stage):
                for b in range(DEC_BATCH):
                    cut(at, f"{stage}{b}")

            def final_squares(t):
                act.wait_ge(done["v_free"], (t + 1) * SLOTS + VB)
                A(junk, acc[:, :], ACT.Square, accum_out=stats[:, YSQ:YSQ + 1])
                root(P, inp=YSQ, out=YSTD).then_inc(done["std_y"], 1)

            def store_y(t):
                act.wait_ge(done["y_rows"], t + 1)
                act.dma_start(outs["y"][bass.ds(t * P, P), :], rows_p[:, :]).then_inc(out_sem["y"], 16)

            def front(at, t, rows, v_dst, row0):
                cut(at, "x")
                act.wait_ge(land["x"], 16 * (t + 1))
                rms(xr, rows).then_inc(done["std_x"], 1)
                heads = lambda b: b[0:rows, :].rearrange("p (h d) -> p h d", h=H_FOX)
                act.wait_ge(MM.full, MM.filled(at, "fq"))
                take(at, "fq", q_aug[0:rows, :, 0:DH], heads, scale=DH ** -0.5).then_inc(MM.free, 1)
                cut(at, "in0")
                act.wait_ge(MM.full, MM.filled(at, "fk"))
                take(at, "fk", k_aug[0:rows, :, 0:DH], heads).then_inc(MM.free, 1)
                cut(at, "in1")
                act.wait_ge(MM.full, MM.filled(at, "fv"))
                take(at, "fv", v_dst, lambda b: b[0:rows, :]).then_inc(MM.free, 1)
                cut(at, "in2")
                act.wait_ge(MM.full, MM.filled(at, "gqk"))
                take(at, "gqk", gqk[0:rows, :], lambda b: b[0:rows, :]).then_inc(MM.free, 1)
                cut(at, "in3")
                act.wait_ge(MM.full, MM.filled(at, "gv"))
                take(at, "gv", gv[0:rows, :], lambda b: b[0:rows, :]).then_inc(MM.free, 1)
                cut(at, "in4")
                act.wait_ge(MM.full, MM.filled(at, "gr"))
                take(at, "gr", silu_r[0:rows, :], lambda b: b[0:rows, :], ACT.Silu).then_inc(MM.free, 1)
                cut(at, "in5")
                act.wait_ge(MM.full, MM.filled(at, "small"))
                bank = MM.ap(at, "small")
                A(zz[0:rows, 0:H_FOX], bank[0:rows, 0:H_FOX], ACT.Copy)
                A(gg[0:rows, :], bank[0:rows, H_FOX:H_FOX + RANK], ACT.Copy).then_inc(MM.free, 1)
                cut(at, "small")
                if not mixed(at):
                    act.wait_ge(out_sem["mk0"], 64)
                act.wait_ge(MM.free, MM.taken(at, "fv"))
                k_out, v_out, lf_out = row0
                act.dma_start(k_out, k_aug[0:rows, :, 0:DH]).then_inc(out_sem["fk"], 16)
                act.dma_start(v_out, v_dst).then_inc(out_sem["fv"], 16)
                act.wait_ge(MM.full, MM.filled(at, "gate"))
                take(at, "gate", zz[0:rows, H_FOX:], lambda b: b[0:rows, 0:GKW]).then_inc(MM.free, 1)
                cut(at, "gate")
                act.wait_ge(done["zmin"], t + 1)
                A(zl[0:rows, :], zl[0:rows, :], ACT.Exp)
                act.drain()
                A(zl[0:rows, :], zl[0:rows, :], ACT.Ln, bias=1.0).then_inc(done["lnz"], 1)
                cut(at, "lf")
                act.wait_ge(done["lf"], t + 1)
                act.dma_start(lf_out, lf[0:rows, 0:H_FOX]).then_inc(out_sem["lf"], 16)

            def gate_exps(at, t, rows):
                act.wait_ge(MM.full, MM.filled(at, "cum"))
                bank = MM.ap(at, "cum")
                A(cums[0:rows, :], bank[0:rows, 0:2 * H_FOX], ACT.Copy)
                b = bank[0:rows, 2 * H_FOX:2 * H_FOX + GKW]
                A(gb[0:rows, :], b, ACT.Copy)
                A(q_dec[0:rows, :], b, ACT.Exp)
                A(k_neg[0:rows, :], b, ACT.Exp, scale=-1.0).then_inc(MM.free, 1)

            def gla_squares(at, t, rows, src):
                for h in range(H_GLA):
                    A(xs[0:rows, h * DV:(h + 1) * DV], src[:, h * DV:(h + 1) * DV], ACT.Square,
                      accum_out=stats[0:rows, GSS + h:GSS + h + 1])

            def cross_exp(t, rows):
                for h in range(H_MEM):
                    p = probs[0][0:rows, h * N_MEM:(h + 1) * N_MEM]
                    ins = A(p, p, ACT.Exp, accum_out=stats[0:rows, CSUM + h:CSUM + h + 1])
                ins.then_inc(done["c_exp"], 1)

            def peer(at, t, rows):
                act.wait_ge(SC.free, SC.taken(at, "wo"))
                rms(xr, rows).then_inc(done["std_3"], 1)
                for i in range(4):
                    act.wait_ge(MM.full, MM.filled(at, f"pq{i}"))
                    take(at, f"pq{i}", pq_t[:, 4 * i:4 * i + 4, 0:rows], lambda b: b[:, :].rearrange("p (j q) -> p j q", j=4)[:, :, 0:rows]).then_inc(MM.free, 1)
                    cut(at, f"pq{i}")
                for name in ("half0", "half1", "sums", "best"):
                    cut(at, name)
                act.wait_ge(done["gate_sub"], t + 1)
                A(gates[0:rows, :], gates[0:rows, :], ACT.Exp).then_inc(done["gate_exp"], 1)
                if mixed(at):
                    final_squares(t - 1)
                    store_y(t - 1)

            def prompt_tile(t, seen):
                at = ("prompt", t)
                r = bass.ds(t * P, P)
                front(at, t, P, v_all[:, bass.ds(t, 1), :].rearrange("p a n -> p (a n)"),
                      (outs["fk"][r, :].rearrange("p (h d) -> p h d", h=H_FOX), outs["fv"][r, :], outs["lf"][r, :]))
                A(mask[:, 0:seen * P], causal[:, bass.ds((TILES - 1) * P - t * P, seen * P)], ACT.Copy).then_inc(done["mask"], 1)
                gate_exps(at, t, P)
                act.wait_ge(MM.full, MM.filled(at, "cumg"))
                bank = MM.ap(at, "cumg")
                A(k_dl[:, :], bank[:, 0:GKW], ACT.Copy)
                A(decay[:, :], bank[0:DK, GKW:GKW + H_GLA * NCH], ACT.Exp).then_inc(MM.free, 1)
                cut(at, "cum")
                act.wait_ge(done["gdiff"], t + 1)
                A(k_dl[:, :], k_dl[:, :], ACT.Exp).then_inc(done["gexpl"], 1)
                cut(at, "turn")
                for h in range(H_FOX):
                    act.wait_ge(done["fox_sub"], t * H_FOX + h + 1)
                    p = probs[h % 2][:, 0:seen * P]
                    A(p, p, ACT.Exp, bias=stats[:, FMAX + h:FMAX + h + 1],
                           accum_out=stats[:, FSUM + h:FSUM + h + 1]).then_inc(done["fox_exp"], 1)
                    cut(at, f"h{h}")
                cut(at, "gla")
                for n in ("fk", "fv", "lf"):
                    act.wait_ge(out_sem[n], 16 * (t + 1))
                act.wait_ge(MM.full, MM.filled(at, "fo"))
                bank = MM.ap(at, "fo")
                act.wait_ge(done["finv"], t + 1)
                for h in range(H_FOX):
                    ins = A(hb[:, h * DH:(h + 1) * DH], bank[:, h * DH:(h + 1) * DH], ACT.Copy, scale=stats[:, FINV + h:FINV + h + 1])
                ins.then_inc(MM.free, 1)
                cut(at, "kv")
                act.wait_ge(MM.full, MM.filled(at, "go"))
                bank = MM.ap(at, "go")
                gla_squares(at, t, P, bank)
                A(gqk[:, :], bank[:, :], ACT.Copy).then_inc(MM.free, 1)
                root(P, n=DV, inp=GSS, out=GSTD, w=H_GLA).then_inc(done["gstd"], 1)
                cut(at, "merge")
                cut(at, "wout")
                act.wait_ge(SC.free, SC.taken(at, "wout"))
                rms(xr, P).then_inc(done["std_2"], 1)
                for i in range(2):
                    act.wait_ge(MM.full, MM.filled(at, f"cq{i}"))
                    take(at, f"cq{i}", c_qt[:, 4 * i:4 * i + 4, :], lambda b: b[:, :].rearrange("p (j q) -> p j q", j=4), scale=DH_MEM ** -0.5).then_inc(MM.free, 1)
                    cut(at, f"cq{i}")
                act.wait_ge(SC.free, SC.taken(at, "xs"))
                cross_exp(t, P)
                cut(at, "cross")
                for i in range(2):
                    act.wait_ge(MM.full, MM.filled(at, f"cu{i}"))
                    take(at, f"cu{i}", h_t[:, 4 * i:4 * i + 4, :], lambda b: b[:, :].rearrange("p (j q) -> p j q", j=4)).then_inc(MM.free, 1)
                cut(at, "cu")
                cut(at, "wo")
                peer(at, t, P)

            def sample_tile(t):
                at = ("sample", t)
                rows = RS
                front(at, t, rows, v_new, (outs["fk"][SEQ:, :].rearrange("p (h d) -> p h d", h=H_FOX), outs["fv"][SEQ:, :], outs["lf"][SEQ:, :]))
                act.wait_ge(MM.full, MM.filled(at, "cpast"))
                bank = MM.ap(at, "cpast")
                n = DEC_BATCH * H_FOX
                A(c_past[:].rearrange("p a b h -> p (a b h)"), bank[:, 0:2 * n], ACT.Copy)
                A(c_last[:].rearrange("p b h -> p (b h)"), bank[0:rows, 2 * n:3 * n], ACT.Copy).then_inc(MM.free, 1)
                act.wait_ge(MM.full, MM.filled(at, "cum"))
                bank = MM.ap(at, "cum")
                A(cums[0:rows, 0:H_FOX], bank[0:rows, 0:H_FOX], ACT.Copy)
                b = bank[0:rows, 2 * H_FOX:2 * H_FOX + GKW]
                A(gb[0:rows, :], b, ACT.Copy)
                A(q_dec[0:rows, :], b, ACT.Exp)
                A(k_neg[0:rows, :], b, ACT.Exp, scale=-1.0).then_inc(MM.free, 1)
                act.wait_ge(MM.full, MM.filled(at, "cumg"))
                bank = MM.ap(at, "cumg")
                A(k_dl[0:rows, :], bank[0:rows, 0:GKW], ACT.Copy)
                A(decay_s[:, :], bank[0:DK, GKW:GKW + H_GLA * DEC_BATCH], ACT.Exp).then_inc(MM.free, 1)
                act.wait_ge(done["gdiff"], t + 1)
                cut(at, "cum")
                A(k_dl[0:rows, :], k_dl[0:rows, :], ACT.Exp).then_inc(done["gexpl"], 1)
                cut(at, "turn")
                act.wait_ge(MM.full, MM.filled(at, "go"))
                take(at, "go", go_t, lambda b: b[:, 0:H_GLA * rows].rearrange("p (h q) -> p h q", q=rows)).then_inc(MM.free, 1)
                cuts(at, "kv")
                act.wait_ge(TP.free, TP.taken(at, "got"))
                gla_squares(at, t, rows, gqk[0:rows, :])
                root(rows, n=DV, inp=GSS, out=GSTD, w=H_GLA).then_inc(done["gstd"], 1)
                for n in ("fk", "fv", "lf"):
                    act.wait_ge(out_sem[n], 16 * (t + 1))
                act.wait_ge(done["s_sub"], 1)
                A(s_rows, s_rows, ACT.Exp).then_inc(done["s_exp"], 1)
                cut(at, "soft")
                cuts(at, "fo")
                act.wait_ge(MM.full, MM.filled(at, "fo"))
                take(at, "fo", fo_t, lambda b: b[0:DH, :].rearrange("p (h q) -> p h q", q=rows)).then_inc(MM.free, 1)
                cut(at, "merge")
                cut(at, "wout")
                act.wait_ge(SC.free, SC.taken(at, "wout"))
                rms(xr, rows).then_inc(done["std_2"], 1)
                for i in range(2):
                    act.wait_ge(MM.full, MM.filled(at, f"cq{i}"))
                    take(at, f"cq{i}", c_qt[:, 4 * i:4 * i + 4, 0:rows], lambda b: b[:, :].rearrange("p (j q) -> p j q", j=4)[:, :, 0:rows],
                         scale=DH_MEM ** -0.5).then_inc(MM.free, 1)
                    cut(at, f"cq{i}")
                cuts(at, "cs")
                act.wait_ge(MM.full, MM.filled(at, "cs"))
                take(at, "cs", cs_t, lambda b: b[:, :].rearrange("p (s q) -> p s q", q=rows)).then_inc(MM.free, 1)
                act.wait_ge(done["c_sub"], 1)
                cross_exp(t, rows)
                cuts(at, "cu")
                for i in range(2):
                    act.wait_ge(MM.full, MM.filled(at, f"cu{i}"))
                    take(at, f"cu{i}", h_t[:, 4 * i:4 * i + 4, 0:rows], lambda b: b[:, :].rearrange("p (j q) -> p j q", j=4)[:, :, 0:rows]).then_inc(MM.free, 1)
                act.dma_start(outs["gs_s"].rearrange("(s d) v -> d s v", d=DK), states_s).then_inc(out_sem["gs"], 16)
                peer(at, t, rows)

            prompt_tile(0, TILES // 2)
            with act.Fori(1, TILES // 2) as t:
                prompt_tile(t, TILES // 2)
            with act.Fori(TILES // 2, TILES) as t:
                prompt_tile(t, TILES)
            act.wait_ge(done["merged"], TILES)
            act.dma_start(outs["gs"].rearrange("(h d) v -> d h v", h=H_GLA), state[:, :, :]).then_inc(out_sem["gs"], 16)
            act.wait_ge(out_sem["gs"], 16)
            sample_tile(TILES)
            all_steps(act, peer_step, TILES)
            final_squares(TILES)
            store_y(TILES)
            act.wait_ge(out_sem["y"], 16 * (TILES + 1))
            act.wait_ge(out_sem["gs"], 32)

        @block.vector
        def _(dve):
            V = nc.vector

            def gained(at, name, gain, dst, rows, cols=P):
                bank = TP.ap(at, name)
                src = bank[0:cols, :].rearrange("p (j q) -> p j q", j=4)[:, :, 0:rows]
                if gain is None:
                    return V.tensor_copy(dst, src)
                return V.tensor_tensor(dst, src, gain.unsqueeze(2).to_broadcast([P, 4, rows]), ALU.mult)

            def scaled(rows):
                V.reciprocal(stats[0:rows, RSTD:RSTD + 1], stats[0:rows, STD:STD + 1])
                dve.drain()
                return V.tensor_scalar(xs[0:rows, :], xr[0:rows, :], stats[0:rows, RSTD:RSTD + 1], None, ALU.mult)

            V.memset(eps_col[:], EPS)
            V.memset(q_aug[:, :, DH:DH + 1], 1.0)
            V.memset(k_aug[:, :, DH + 1:DA], 1.0)
            V.memset(carry[:], 0.0)
            V.memset(state[:], 0.0)
            V.memset(att_t[:], 0.0).then_inc(TP.free, TP.depth)
            dve.drain().then_inc(done["preset"], 1)
            dve.sem_inc(SC.free, SC.depth)
            dve.sem_inc(done["u_free"], UB)
            dve.sem_inc(done["acc_free"], 1)
            for n in ("gains", "sub", "ffn", "bias", "gate2"):
                dve.wait_ge(land[n], 16)
            dve.wait_ge(land["small"], 32)
            dve.wait_ge(done["consts"], 1)
            dve.wait_ge(land_s["pages"], 16)
            V.tensor_scalar(page_rows[:], pages[:], float(P), row_no[:, :], ALU.mult, ALU.add)
            V.tensor_scalar(page_cols[:], pages[:], float(DH), row_no[:, :], ALU.mult, ALU.add).then_inc(done["page_idx"], 1)
            at = ("setup", 0)
            for m, src in enumerate(mem_rows):
                dve.wait_ge(done["mem_ss"], m + 1)
                V.reciprocal(stats[:, RSTD:RSTD + 1], stats[:, STD:STD + 1])
                dve.drain()
                V.tensor_scalar(hb[:, :], src, stats[:, RSTD:RSTD + 1], None, ALU.mult).then_inc(done["mem_xs"], 1)
                for c in range(2):
                    dve.wait_ge(TP.full, TP.filled(at, f"mx{m}{c}"))
                    gained(at, f"mx{m}{c}", g_mem_c[:, 4 * c:4 * c + 4], mem_t[:, 4 * c:4 * c + 4, m * P:(m + 1) * P], P).then_inc(TP.free, 1)
            V.memset(v_all[:], 0.0)
            V.memset(kt_all[:], 0.0)
            for c in range(2):
                for m in range(MC):
                    dve.wait_ge(TP.full, TP.filled(at, f"mk{m}{c}"))
                    gained(at, f"mk{m}{c}", None, mem_kt[:, 4 * c:4 * c + 4, m * P:(m + 1) * P], P).then_inc(TP.free, 1)

            def peer_step(t, k, like):
                rows = RS if isinstance(t, int) and t == TILES else P
                if like < HALVES:
                    g = like // 2 % 2
                    if like % 2 == 0 and like >= 4:
                        dve.wait_ge(done["gelu"], t * HALVES + k - 2)
                    for s in range(HALF):
                        n = like % 2 * HALF + s
                        dve.wait_ge(u_land[s], (t * HALVES + k + 1) * 16)
                        u = u_ring[0:rows, s, :]
                        V.tensor_tensor_reduce(u, u, rows_p[0:rows, :], 1.0, 0.0, ALU.mult, ALU.add, dots[0:rows, g, n:n + 1]).then_inc(done["u_free"], 1)
                if like % 2 == 1 and 5 <= like < 5 + HALVES:
                    g = (like - 5) // 2 % 2
                    dve.wait_ge(done["gelu"], t * HALVES + k - 3)
                    if like >= 9:
                        dve.wait_ge(done["diag"], t * HALVES + k - 7)
                    V.tensor_tensor(wts[:, g, :], gelu[:, g, :], gates[:, bass.ds(k * HALF - 5 * HALF, GROUP)], ALU.mult).then_inc(done["wts"], 2)

            def cut(at, name):
                if mixed(at):
                    for k in STEPS_AT[at[0]].get(name, ()):
                        peer_step(at[1] - 1, k, k)

            def cuts(at, stage):
                for b in range(DEC_BATCH):
                    cut(at, f"{stage}{b}")

            def final_rows(t):
                dve.wait_ge(done["std_y"], t + 1)
                V.reciprocal(stats[:, YINV:YINV + 1], stats[:, YSTD:YSTD + 1])
                dve.drain()
                dve.wait_ge(land["fin"], 16 * (t + 1))
                V.scalar_tensor_tensor(rows_p[:, :], acc[:, :], stats[:, YINV:YINV + 1], rows_p[:, :], ALU.mult, ALU.mult).then_inc(done["y_rows"], 1)
                dve.wait_ge(done["y_rows"], t + 1)
                dve.sem_inc(done["acc_free"], 1)

            def log_sigmoid(at, t, rows):
                dve.wait_ge(SC.full, SC.filled(at, "gg"))
                SCb = SC.ap(at, "gg")
                V.tensor_copy(gg_t[:, 0:rows], SCb[0:RANK, 0:rows]).then_inc(SC.free, 1)
                cut(at, "gate")
                dve.wait_ge(MM.free, MM.taken(at, "gate"))
                z = zz[0:rows, :]
                V.tensor_tensor(z, z, bias_bc[0:rows, :], ALU.add)
                dve.drain()
                V.scalar_tensor_tensor(zl[0:rows, :], z, -1.0, z, ALU.mult, ALU.min).then_inc(done["zmin"], 1)
                cut(at, "lf")
                dve.wait_ge(done["lnz"], t + 1)
                V.scalar_tensor_tensor(lf[0:rows, :], z, 0.0, zl[0:rows, :], ALU.min, ALU.subtract)
                dve.drain()
                V.tensor_scalar(lf[0:rows, H_FOX:], lf[0:rows, H_FOX:], 1.0 / TAU, None, ALU.mult).then_inc(done["lf"], 1)

            def gla_operands(t, rows):
                q, k = gqk[0:rows, 0:GKW], gqk[0:rows, GKW:]
                V.scalar_tensor_tensor(q_dec[0:rows, :], q, DK ** -0.5, q_dec[0:rows, :], ALU.mult, ALU.mult)
                V.tensor_tensor(k_neg[0:rows, :], k, k_neg[0:rows, :], ALU.mult).then_inc(done["q_dec"], 1)
                dve.wait_ge(done["gexpl"], t + 1)
                V.tensor_tensor(k_dl[0:rows, :], k, k_dl[0:rows, :], ALU.mult).then_inc(done["k_dl"], 1)

            def softmax_cross(rows, t):
                dve.wait_ge(done["c_exp"], t + 1)
                V.reciprocal(stats[0:rows, CINV:CINV + 4], stats[0:rows, CSUM:CSUM + 4])
                dve.drain()
                p = probs[0][0:rows, :].rearrange("p (h m) -> p h m", h=H_MEM)
                V.tensor_tensor(p, p, stats[0:rows, CINV:CINV + 4].unsqueeze(2).to_broadcast([rows, H_MEM, N_MEM]), ALU.mult).then_inc(done["p_norm"], 1)

            def choose(at, t, rows):
                R = slice(0, rows)
                for i in range(2):
                    dve.wait_ge(SC.full, SC.filled(at, f"ps{i}"))
                    bank = SC.ap(at, f"ps{i}")
                    apart(dve)
                    s = [bank[R, j * P:(j + 1) * P] for j in range(8)]
                    v = [vals[R, 8 * i + j, :] for j in range(8)]
                    x = [inds[R, 8 * i + j, :] for j in range(8)]
                    for j in range(8):
                        V.max(v[j][:, 0:8], s[j])
                    dve.drain()
                    for j in range(8):
                        V.match_replace(rest[R, j, :], v[j][:, 0:8], s[j], LOWEST)
                    dve.drain()
                    for j in range(8):
                        V.max(v[j][:, 8:16], rest[R, j, :])
                        ins = V.max_index(x[j][:, 0:8], v[j][:, 0:8], s[j])
                    ins.then_inc(SC.free, 1)
                    dve.drain()
                    for j in range(8):
                        V.max_index(x[j][:, 8:16], v[j][:, 8:16], rest[R, j, :])
                    dve.drain()
                    cut(at, f"half{i}")
                V.tensor_copy(indf[R], inds[R])
                c4 = cand[R, :].rearrange("p (h i j) -> p h i j", h=H_PEER, i=TOPK)
                v4 = vals[R].rearrange("p (h s) k -> p h s k", s=2)
                V.tensor_tensor(c4, v4[:, :, 0, :].unsqueeze(3).to_broadcast([rows, H_PEER, TOPK, TOPK]),
                                v4[:, :, 1, :].unsqueeze(2).to_broadcast([rows, H_PEER, TOPK, TOPK]), ALU.add)
                dve.drain()
                cut(at, "sums")
                c = [cand[R, h * 256:(h + 1) * 256] for h in range(H_PEER)]
                c2 = [cand2[R, h * 256:(h + 1) * 256] for h in range(H_PEER)]
                for h in range(H_PEER):
                    V.max(best[R, h, 0:8], c[h])
                dve.drain()
                for h in range(H_PEER):
                    V.match_replace(c2[h], best[R, h, 0:8], c[h], LOWEST)
                dve.drain()
                cut(at, "best")
                for h in range(H_PEER):
                    V.max(best[R, h, 8:16], c2[h])
                    V.max_index(besti[R, h, 0:8], best[R, h, 0:8], c[h])
                dve.drain()
                for h in range(H_PEER):
                    V.max_index(besti[R, h, 8:16], best[R, h, 8:16], c2[h])
                dve.drain()
                g3 = gates[R, :].rearrange("p (h k) -> p h k", h=H_PEER)
                V.tensor_tensor(g3, best[R], best[R, :, 0:1].to_broadcast([rows, H_PEER, TOPK]), ALU.subtract).then_inc(done["gate_sub"], 1)
                dve.drain()
                bi = besti[R].rearrange("p h k -> p (h k)")
                V.tensor_scalar(half_i[R, 0, :], bi, 4, None, ALU.logical_shift_right)
                V.tensor_scalar(half_i[R, 1, :], bi, TOPK - 1, None, ALU.bitwise_and)
                dve.drain()
                V.tensor_copy(half_f[R], half_i[R])
                dve.drain()
                eq = [a[R, :].rearrange("p (n j) -> p n j", j=TOPK) for a in (cand, cand2)]
                i4 = indf[R].rearrange("p (h s) k -> p h s k", s=2)
                for s in range(2):
                    V.tensor_tensor(eq[s], half_f[R, s, :].unsqueeze(2).to_broadcast([rows, SLOTS, TOPK]),
                                    iota_k[R, :].unsqueeze(1).to_broadcast([rows, SLOTS, TOPK]), ALU.is_equal)
                dve.drain()
                for s in range(2):
                    e4 = eq[s].rearrange("p (h k) j -> p h k j", h=H_PEER)
                    V.tensor_tensor(e4, e4, i4[:, :, s, :].unsqueeze(2).to_broadcast([rows, H_PEER, TOPK, TOPK]), ALU.mult)
                dve.drain()
                for s in range(2):
                    V.tensor_reduce(picked[R, s, :], eq[s], AX.X, ALU.add)
                dve.drain()
                if mixed(at):
                    dve.wait_ge(done["staged"], t * (2 * SLOTS // GROUP))
                    apart(dve)
                V.scalar_tensor_tensor(experts[R, :], picked[R, 0, :], float(N_KEYS), picked[R, 1, :], ALU.mult, ALU.add).then_inc(done["experts"], 1)
                dve.wait_ge(done["gate_exp"], t + 1)
                V.tensor_reduce(gsum[R, :], g3, AX.X, ALU.add)
                dve.drain()
                V.reciprocal(ginv[R, :], gsum[R, :])
                dve.drain()
                V.tensor_tensor(g3, g3, ginv[R, :].unsqueeze(2).to_broadcast([rows, H_PEER, TOPK]), ALU.mult)
                if mixed(at):
                    final_rows(t - 1)
                    dve.wait_ge(out_sem["y"], 16 * t)
                V.tensor_copy(rows_p[R, :], hb[R, :])
                dve.drain()

            def peer(at, t, rows):
                R = slice(0, rows)
                dve.wait_ge(SC.full, SC.filled(at, "wo"))
                bank = SC.ap(at, "wo")
                V.tensor_tensor(xr[R, :], xr[R, :], bank[R, :], ALU.add).then_inc(SC.free, 1)
                dve.wait_ge(done["std_3"], t + 1)
                V.reciprocal(stats[R, RSTD:RSTD + 1], stats[R, STD:STD + 1])
                dve.drain()
                V.scalar_tensor_tensor(hb[R, :], xr[R, :], stats[R, RSTD:RSTD + 1], g_ffn_bc[R, :], ALU.mult, ALU.mult).then_inc(done["hb_rows"], 1)
                for c in range(2):
                    dve.wait_ge(TP.full, TP.filled(at, f"f{c}"))
                    gained(at, f"f{c}", None, h_t[:, 4 * c:4 * c + 4, 0:rows], rows).then_inc(TP.free, 1)
                for i in range(4):
                    cut(at, f"pq{i}")
                choose(at, t, rows)

            def prompt_tile(t, seen):
                at = ("prompt", t)
                cut(at, "x")
                dve.wait_ge(done["std_x"], t + 1)
                scaled(P).then_inc(done["xs_x"], 1)
                for c in range(2):
                    dve.wait_ge(TP.full, TP.filled(at, f"x{c}"))
                    gained(at, f"x{c}", g_mix_c[:, 4 * c:4 * c + 4], h_t[:, 4 * c:4 * c + 4, :], P).then_inc(TP.free, 1)
                for k in range(6):
                    cut(at, f"in{k}")
                cut(at, "small")
                log_sigmoid(at, t, P)
                cut(at, "cum")
                dve.wait_ge(MM.free, MM.taken(at, "cumg"))
                V.tensor_tensor(k_dl[:, :], k_dl[:, :], gb[:, :], ALU.subtract).then_inc(done["gdiff"], 1)
                V.tensor_tensor(cums[:, 0:H_FOX], cums[:, 0:H_FOX], carry[:, :], ALU.add)
                dve.drain()
                V.tensor_tensor(carry[:, :], carry[:, :], cums[:, H_FOX:], ALU.add)
                V.tensor_copy(q_aug[:, :, DH + 1], cums[:, 0:H_FOX])
                V.tensor_scalar(k_aug[:, :, DH], cums[:, 0:H_FOX], -1.0, None, ALU.mult).then_inc(done["aug_cols"], 1)
                gla_operands(t, P)
                for c in range(2):
                    dve.wait_ge(TP.full, TP.filled(at, f"q{c}"))
                    gained(at, f"q{c}", None, q_t[:, 4 * c:4 * c + 4, :], P, DA).then_inc(TP.free, 1)
                for c in range(2):
                    dve.wait_ge(TP.full, TP.filled(at, f"k{c}"))
                    gained(at, f"k{c}", None, kt_all[0:DA, 4 * c:4 * c + 4, bass.ds(t * P, P)], P, DA).then_inc(TP.free, 1)
                dve.wait_ge(TP.full, TP.filled(at, "gq"))
                gained(at, "gq", None, qd_t[:, :, :], P, DK).then_inc(TP.free, 1)
                dve.wait_ge(TP.full, TP.filled(at, "gk"))
                gained(at, "gk", None, kn_t[:, :, :], P, DK).then_inc(TP.free, 1)
                cut(at, "turn")

                def masked(h):
                    dve.wait_ge(SC.full, SC.filled(at, f"s{h}"))
                    bank = SC.ap(at, f"s{h}")
                    if h == 0:
                        dve.wait_ge(done["mask"], t + 1)
                    apart(dve)
                    mx = stats[:, FMAX + h:FMAX + h + 1]
                    k = slice(0, seen * P)
                    V.tensor_tensor_reduce(probs[h % 2][:, k], bank[:, k], mask[:, k], 1.0, LOWEST,
                                           ALU.add, ALU.max, mx).then_inc(SC.free, 1)
                    dve.drain()
                    V.tensor_scalar(mx, mx, -1.0, None, ALU.mult).then_inc(done["fox_sub"], 1)

                masked(0)
                for h in range(H_FOX):
                    if h + 1 < H_FOX:
                        masked(h + 1)
                    cut(at, f"h{h}")
                    for c in range(seen * P // W):
                        dve.wait_ge(TP.full, TP.filled(at, f"P{h}{c}"))
                        gained(at, f"P{h}{c}", None, p_t[:, 4 * c:4 * c + 4, :], P).then_inc(TP.free, TILES // seen)
                cut(at, "gla")
                dve.wait_ge(done["fox_exp"], (t + 1) * H_FOX)
                V.reciprocal(stats[:, FINV:FINV + 8], stats[:, FSUM:FSUM + 8]).then_inc(done["finv"], 1)
                dve.wait_ge(SC.full, SC.filled(at, "gatt"))
                bank = SC.ap(at, "gatt")
                apart(dve)
                V.copy_predicated(att_t[:, :, :], blk_up[:, :].bitcast(U32).unsqueeze(1).to_broadcast([P, H_GLA, P]),
                                  bank[:, 0:H_GLA * P].rearrange("p (h c) -> p h c", h=H_GLA)).then_inc(SC.free, 1)
                dve.wait_ge(SC.full, SC.filled(at, "gkv"))
                bank = SC.ap(at, "gkv")
                for ch, (new, old) in enumerate(((state1, state), (state, state1))):
                    if ch == 1:
                        dve.wait_ge(done["gstd"], t + 1)
                    for h in range(H_GLA):
                        ins = V.scalar_tensor_tensor(new[:, h, :], old[:, h, :], decay[:, NCH * h + ch:NCH * h + ch + 1],
                                                     bank[0:DK, (ch * H_GLA + h) * DV:(ch * H_GLA + h + 1) * DV], ALU.mult, ALU.add)
                    if ch == 0:
                        ins.then_inc(done["state1"], 1)
                        cut(at, "kv")
                ins.then_inc(SC.free, 1)
                V.reciprocal(stats[:, GINV:GINV + 4], stats[:, GSTD:GSTD + 4])
                dve.drain()
                for h in range(H_GLA):
                    r = slice(h * DV, (h + 1) * DV)
                    ins = V.scalar_tensor_tensor(hb[:, W + h * DV:W + (h + 1) * DV], gqk[:, r], stats[:, GINV + h:GINV + h + 1],
                                                 silu_r[:, r], ALU.mult, ALU.mult)
                ins.then_inc(done["merged"], 1)
                cut(at, "merge")
                dve.wait_ge(TP.full, TP.filled(at, "m0"))
                gained(at, "m0", None, h_t[:, 0:4, :], P).then_inc(TP.free, 1)
                dve.wait_ge(TP.full, TP.filled(at, "m1"))
                gained(at, "m1", g_gla_c, h_t[:, 4:8, :], P).then_inc(TP.free, 1)
                cut(at, "wout")
                dve.wait_ge(SC.full, SC.filled(at, "wout"))
                bank = SC.ap(at, "wout")
                V.tensor_tensor(xr[:, :], xr[:, :], bank[:, :], ALU.add).then_inc(SC.free, 1)
                dve.wait_ge(done["std_2"], t + 1)
                scaled(P).then_inc(done["xs_2"], 1)
                for c in range(2):
                    dve.wait_ge(TP.full, TP.filled(at, f"h{c}"))
                    gained(at, f"h{c}", g_cross_c[:, 4 * c:4 * c + 4], h_t[:, 4 * c:4 * c + 4, :], P).then_inc(TP.free, 1)
                cut(at, "cq0")
                cut(at, "cq1")
                dve.wait_ge(SC.full, SC.filled(at, "xs"))
                bank = SC.ap(at, "xs")
                b3 = bank[:, :].rearrange("p (h m) -> p h m", h=H_MEM)
                V.tensor_reduce(stats[:, CMAX:CMAX + 4], b3, AX.X, ALU.max)
                dve.drain()
                V.tensor_tensor(probs[0].rearrange("p (h m) -> p h m", h=H_MEM), b3,
                                stats[:, CMAX:CMAX + 4].unsqueeze(2).to_broadcast([P, H_MEM, N_MEM]), ALU.subtract).then_inc(SC.free, 1)
                cut(at, "cross")
                softmax_cross(P, t)
                for c in range(2):
                    dve.wait_ge(TP.full, TP.filled(at, f"p{c}"))
                    gained(at, f"p{c}", None, p_t[:, 4 * c:4 * c + 4, :], P).then_inc(TP.free, 1)
                cut(at, "cu")
                cut(at, "wo")
                peer(at, t, P)

            def sample_tile(t):
                at = ("sample", t)
                rows = RS
                R = slice(0, rows)
                V.memset(att_t[:], 0.0)
                cut(at, "x")
                dve.wait_ge(done["std_x"], t + 1)
                scaled(rows).then_inc(done["xs_x"], 1)
                for c in range(2):
                    dve.wait_ge(TP.full, TP.filled(at, f"x{c}"))
                    gained(at, f"x{c}", g_mix_c[:, 4 * c:4 * c + 4], h_t[:, 4 * c:4 * c + 4, 0:rows], rows).then_inc(TP.free, 1)
                for k in range(6):
                    cut(at, f"in{k}")
                cut(at, "small")
                log_sigmoid(at, t, rows)
                dve.wait_ge(MM.free, MM.taken(at, "cumg"))
                V.tensor_tensor(k_dl[R, :], k_dl[R, :], gb[R, :], ALU.subtract).then_inc(done["gdiff"], 1)
                V.tensor_tensor(c_last[:], c_last[:], same_ind[:, :].unsqueeze(2).to_broadcast([rows, DEC_BATCH, H_FOX]), ALU.mult)
                dve.drain()
                V.tensor_reduce(c_rows[:, :], c_last[:].rearrange("p b h -> p h b"), AX.X, ALU.add)
                dve.drain()
                V.tensor_tensor(c_rows[:, :], c_rows[:, :], cums[R, 0:H_FOX], ALU.add)
                dve.drain()
                V.tensor_copy(q_aug[R, :, DH + 1], c_rows[:, :])
                V.tensor_scalar(k_aug[R, :, DH], c_rows[:, :], -1.0, None, ALU.mult).then_inc(done["aug_cols"], 1)
                cut(at, "cum")
                gla_operands(t, rows)
                for c in range(2):
                    dve.wait_ge(TP.full, TP.filled(at, f"q{c}"))
                    gained(at, f"q{c}", None, q_t[:, 4 * c:4 * c + 4, 0:rows], rows, DA).then_inc(TP.free, 1)
                for c in range(2):
                    dve.wait_ge(TP.full, TP.filled(at, f"k{c}"))
                    gained(at, f"k{c}", None, k_new_t[:, 4 * c:4 * c + 4, 0:rows], rows, DA).then_inc(TP.free, 1)
                dve.wait_ge(TP.full, TP.filled(at, "gq"))
                gained(at, "gq", None, qd_t[:, :, 0:rows], rows, DK).then_inc(TP.free, 1)
                dve.wait_ge(TP.full, TP.filled(at, "gk"))
                gained(at, "gk", None, kn_t[:, :, 0:rows], rows, DK).then_inc(TP.free, 1)
                cut(at, "turn")
                dve.wait_ge(done["same"], 1)
                dve.wait_ge(done["k_dl"], t + 1)
                V.tensor_tensor(k_masked, k_dl[R, :].unsqueeze(1).to_broadcast([rows, DEC_BATCH, GKW]),
                                     same_ind[:, :].unsqueeze(2).to_broadcast([rows, DEC_BATCH, GKW]), ALU.mult).then_inc(done["k_masked"], 1)
                dve.wait_ge(SC.full, SC.filled(at, "gatt"))
                bank = SC.ap(at, "gatt")
                V.copy_predicated(att_t[R, :, 0:rows], same_up[:, :].bitcast(U32).unsqueeze(1).to_broadcast([rows, H_GLA, rows]),
                                  bank[R, 0:H_GLA * P].rearrange("p (h c) -> p h c", h=H_GLA)[:, :, 0:rows]).then_inc(SC.free, 1)
                dve.wait_ge(MM.free, MM.taken(at, "go"))
                for b in range(DEC_BATCH):
                    dve.wait_ge(SC.full, SC.filled(at, f"kv{b}"))
                    bank = SC.ap(at, f"kv{b}")
                    for h in range(H_GLA):
                        st = states_s[:, b * H_GLA + h, :]
                        ins = V.scalar_tensor_tensor(st, st, decay_s[:, DEC_BATCH * h + b:DEC_BATCH * h + b + 1],
                                                     bank[0:DK, h * DV:(h + 1) * DV], ALU.mult, ALU.add)
                    ins.then_inc(SC.free, 1)
                    cut(at, f"kv{b}")
                dve.wait_ge(TP.full, TP.filled(at, "got"))
                gained(at, "got", None, gqk[R, :].rearrange("p (h v) -> p h v", h=H_GLA), P, rows).then_inc(TP.free, 1)
                dve.wait_ge(SC.full, SC.filled(at, "past"))
                bank = SC.ap(at, "past")
                for page in range(N_PAGES):
                    r = slice(page * D // 2, (page + 1) * D // 2)
                    v4 = lambda a: a.rearrange("p (h b q) -> p h b q", h=H_FOX, b=DEC_BATCH)
                    ins = V.tensor_tensor(v4(work[:, r]), v4(bank[:, r]),
                                          c_past[:, page].rearrange("p b h -> p h b").unsqueeze(3).to_broadcast([P, H_FOX, DEC_BATCH, DEC_SEQ]),
                                          ALU.subtract)
                ins.then_inc(SC.free, 1)
                dve.wait_ge(SC.full, SC.filled(at, "new"))
                bank = SC.ap(at, "new")
                V.tensor_tensor(s_rows[:, :, N_PAGES * P:], bank[R, 0:H_FOX * rows].rearrange("p (h k) -> p h k", h=H_FOX),
                                same_mask[:, :].unsqueeze(1).to_broadcast([rows, H_FOX, rows]), ALU.add).then_inc(SC.free, 1)
                for i in range(4):
                    dve.wait_ge(TP.full, TP.filled(at, f"S{i}"))
                    bank = TP.ap(at, f"S{i}")
                    hs = slice(4 * (i % 2), 4 * (i % 2) + 4)
                    V.tensor_tensor(s_rows[:, hs, (i // 2) * P:(i // 2 + 1) * P], bank[R, :].rearrange("p (j k) -> p j k", j=4),
                                    c_rows[:, hs].unsqueeze(2).to_broadcast([rows, 4, P]), ALU.add).then_inc(TP.free, 1)
                dve.drain()
                V.tensor_reduce(stats[R, FMAX:FMAX + 8], s_rows, AX.X, ALU.max)
                dve.drain()
                V.tensor_tensor(s_rows, s_rows, stats[R, FMAX:FMAX + 8].unsqueeze(2).to_broadcast([rows, H_FOX, NK_S]), ALU.subtract).then_inc(done["s_sub"], 1)
                cut(at, "soft")
                dve.wait_ge(done["s_exp"], 1)
                V.tensor_reduce(stats[R, FSUM:FSUM + 8], s_rows, AX.X, ALU.add)
                dve.drain()
                V.reciprocal(stats[R, FINV:FINV + 8], stats[R, FSUM:FSUM + 8])
                for i in range(4):
                    dve.wait_ge(TP.full, TP.filled(at, f"P{i}"))
                    gained(at, f"P{i}", None, past_p_t[:, 4 * i:4 * i + 4, :], rows).then_inc(TP.free, 1)
                dve.wait_ge(TP.full, TP.filled(at, "Pn"))
                bank = TP.ap(at, "Pn")
                V.tensor_copy(new_p_t, bank[R, 0:H_FOX * rows].rearrange("p (h q) -> p h q", q=rows)).then_inc(TP.free, 1)
                cuts(at, "fo")
                dve.wait_ge(TP.full, TP.filled(at, "fot"))
                bank = TP.ap(at, "fot")
                V.tensor_tensor(hb[R, 0:W].rearrange("p (h d) -> p h d", h=H_FOX), bank[R, :].rearrange("p (h d) -> p h d", h=H_FOX),
                                stats[R, FINV:FINV + 8].unsqueeze(2).to_broadcast([rows, H_FOX, DH]), ALU.mult).then_inc(TP.free, 1)
                cut(at, "merge")
                dve.wait_ge(done["gstd"], t + 1)
                V.reciprocal(stats[R, GINV:GINV + 4], stats[R, GSTD:GSTD + 4])
                dve.drain()
                for h in range(H_GLA):
                    r = slice(h * DV, (h + 1) * DV)
                    ins = V.scalar_tensor_tensor(hb[R, W + h * DV:W + (h + 1) * DV], gqk[R, r], stats[R, GINV + h:GINV + h + 1],
                                                 silu_r[R, r], ALU.mult, ALU.mult)
                ins.then_inc(done["merged"], 1)
                dve.wait_ge(TP.full, TP.filled(at, "m0"))
                gained(at, "m0", None, h_t[:, 0:4, 0:rows], rows).then_inc(TP.free, 1)
                dve.wait_ge(TP.full, TP.filled(at, "m1"))
                gained(at, "m1", g_gla_c, h_t[:, 4:8, 0:rows], rows).then_inc(TP.free, 1)
                cut(at, "wout")
                dve.wait_ge(SC.full, SC.filled(at, "wout"))
                bank = SC.ap(at, "wout")
                V.tensor_tensor(xr[R, :], xr[R, :], bank[R, :], ALU.add).then_inc(SC.free, 1)
                dve.wait_ge(done["std_2"], t + 1)
                scaled(rows).then_inc(done["xs_2"], 1)
                for c in range(2):
                    dve.wait_ge(TP.full, TP.filled(at, f"h{c}"))
                    gained(at, f"h{c}", g_cross_c[:, 4 * c:4 * c + 4], h_t[:, 4 * c:4 * c + 4, 0:rows], rows).then_inc(TP.free, 1)
                cut(at, "cq0")
                cut(at, "cq1")
                cuts(at, "cs")
                p3 = probs[0][R, :].rearrange("p (h m) -> p h m", h=H_MEM)
                for m in range(MC):
                    dve.wait_ge(TP.full, TP.filled(at, f"c{m}"))
                    bank = TP.ap(at, f"c{m}")
                    V.tensor_copy(p3[:, :, m * P:(m + 1) * P], bank[R, :].rearrange("p (h m) -> p h m", h=H_MEM)).then_inc(TP.free, 1)
                dve.drain()
                V.tensor_reduce(stats[R, CMAX:CMAX + 4], p3, AX.X, ALU.max)
                dve.drain()
                V.tensor_tensor(p3, p3, stats[R, CMAX:CMAX + 4].unsqueeze(2).to_broadcast([rows, H_MEM, N_MEM]), ALU.subtract).then_inc(done["c_sub"], 1)
                softmax_cross(rows, t)
                for c in range(2):
                    dve.wait_ge(TP.full, TP.filled(at, f"p{c}"))
                    gained(at, f"p{c}", None, p_t[:, 4 * c:4 * c + 4, 0:rows], rows).then_inc(TP.free, 1)
                cuts(at, "cu")
                peer(at, t, rows)

            prompt_tile(0, TILES // 2)
            with dve.Fori(1, TILES // 2) as t:
                prompt_tile(t, TILES // 2)
            with dve.Fori(TILES // 2, TILES) as t:
                prompt_tile(t, TILES)
            sample_tile(TILES)
            all_steps(dve, peer_step, TILES)
            final_rows(TILES)

        @block.gpsimd
        def _(pool):
            G = nc.gpsimd
            made = [0]

            def step(ins):
                made[0] += 1
                ins.then_inc(done["made"], 1)
                pool.wait_ge(done["made"], made[0])

            def keep(ap, pattern, base, mult, fill=0.0):
                step(G.affine_select(out=ap, in_=ap, compare_op=ALU.is_ge, fill=fill, base=base, pattern=pattern, channel_multiplier=mult))

            step(G.memset(ones[:], 1.0))
            step(G.memset(upper[:], 1.0))
            keep(upper[:], [[1, P]], 0, -1)
            step(G.memset(ident[:], 1.0))
            keep(ident[:], [[1, P]], 0, -1)
            keep(ident[:], [[-1, P]], 0, 1)
            step(G.memset(causal[:], 0.0))
            keep(causal[:], [[-1, 2 * SEQ - P]], SEQ - P, 1, NEG)
            for tile_ in (blk_up, blk_one):
                step(G.memset(tile_[:], 1.0))
                v = tile_[:].rearrange("p (b c) -> p b c", b=NCH)
                keep(v, [[-CHUNK, NCH], [0, CHUNK]], 0, 1)
                keep(v, [[CHUNK, NCH], [0, CHUNK]], CHUNK - 1, -1)
            keep(blk_up[:], [[1, P]], 0, -1)
            step(G.memset(blk_ind[:], 1.0))
            keep(blk_ind[:], [[-CHUNK, NCH]], 0, 1)
            keep(blk_ind[:], [[CHUNK, NCH]], CHUNK - 1, -1)
            step(G.memset(same_ind[:], 1.0))
            keep(same_ind[:], [[-DEC_SEQ, DEC_BATCH]], 0, 1)
            keep(same_ind[:], [[DEC_SEQ, DEC_BATCH]], DEC_SEQ - 1, -1)
            step(G.iota(row_no[:], pattern=[[0, 1]], base=0, channel_multiplier=1, allow_small_or_imprecise_dtypes=True))
            G.iota(iota_k[:], pattern=[[1, TOPK]], base=0, channel_multiplier=0, allow_small_or_imprecise_dtypes=True).then_inc(done["consts"], 1)

            U, V = 0, 1
            PER_TILE = 2 * SLOTS // GROUP
            rings = ((u_ring, u_land, done["u_free"], peer_u), (v_ring, v_land, done["v_free"], peer_v))

            def stage_group(which, g, slot, count):
                G.tensor_copy(stage[:, which, slot, :], experts[:, bass.ds(g * GROUP, GROUP)]).then_inc(done["staged"], 1)
                pool.wait_ge(done["staged"], count)

            def gather(t, which, g, slot, n, rows):
                ring, land_, free, table = rings[which]
                pool.wait_ge(free, t * SLOTS + g * GROUP + n + 1)
                apart(pool)
                G.indirect_dma_start(ring[0:rows, n % HALF, :], None, table,
                                     bass.IndirectOffsetOnAxis(ap=stage[0:rows, which, slot, n:n + 1], axis=0)).then_inc(land_[n % HALF], 16)

            def gather_half(t, which, g, slot, half, rows):
                for s in range(HALF):
                    gather(t, which, g, slot, half * HALF + s, rows)

            def steady(t, first, last, rows):
                ahead = LAG // 2
                with pool.Fori(first, last) as it:
                    for slot in range(2):
                        g = it * 2 + slot
                        stage_group(U, g + ahead, slot, t * PER_TILE + it * 4 + (ahead + 2 * slot + 1))
                        stage_group(V, g, slot, t * PER_TILE + it * 4 + (ahead + 2 * slot + 2))
                        for half in range(2):
                            for s in range(HALF):
                                gather(t, U, g + ahead, slot, half * HALF + s, rows)
                                gather(t, V, g, slot, half * HALF + s, rows)

            def gathers(t, rows=P, between=None):
                ahead = LAG // 2
                pool.wait_ge(done["experts"], t + 1)
                apart(pool)
                for g in range(ahead):
                    stage_group(U, g, g % 2, t * PER_TILE + g + 1)
                    for half in range(2):
                        gather_half(t, U, g, g % 2, half, rows)
                if between is None:
                    steady(t, 0, (SLOTS // GROUP - ahead) // 2, rows)
                else:
                    steady(t, 0, (KEY_STEP - LAG) // 4, rows)
                    between()
                    steady(t, (KEY_STEP - LAG) // 4, (SLOTS // GROUP - ahead) // 2, rows)
                for g in range(SLOTS // GROUP - ahead, SLOTS // GROUP):
                    stage_group(V, g, g % 2, t * PER_TILE + SLOTS // GROUP + g + 1)
                    for half in range(2):
                        gather_half(t, V, g, g % 2, half, rows)

            def load_value(n):
                G.indirect_dma_start(past_values[n], None, past_v,
                                     bass.IndirectOffsetOnAxis(ap=page_rows[:, n:n + 1], axis=0)).then_inc(land_s["values_past"], 16)

            def load_key(n):
                G.indirect_dma_start(past_keys[n % KB].rearrange("p h k -> p (h k)"), None, past_kt,
                                     bass.IndirectOffsetOnAxis(ap=page_cols[0:DH, n:n + 1], axis=0)).then_inc(key_land[n % KB], 16)

            def sample_loads():
                pool.wait_ge(done["page_idx"], 1)
                pool.wait_ge(MM.full, MM.number(("prompt", TILES - 1), "cu1") + 1)
                for n in range(DEC_BATCH * N_PAGES):
                    G.indirect_dma_start(lf_past[:, n // N_PAGES, n % N_PAGES, :], None, past_lf,
                                         bass.IndirectOffsetOnAxis(ap=page_rows[:, n:n + 1], axis=0)).then_inc(land_s["lf_past"], 16)
                for n in range(KB):
                    load_key(n)
                for n in range(V_FIRST):
                    load_value(n)
                for mask_, value, fill in ((same_up, 1.0, 0.0), (same_one, 1.0, 0.0), (same_mask, 0.0, NEG)):
                    step(G.memset(mask_, value))
                    v = mask_.rearrange("p (b c) -> p b c", b=DEC_BATCH)
                    keep(v, [[-DEC_SEQ, DEC_BATCH], [0, DEC_SEQ]], 0, 1, fill)
                    keep(v, [[DEC_SEQ, DEC_BATCH], [0, DEC_SEQ]], DEC_SEQ - 1, -1, fill)
                keep(same_up, [[1, RS]], 0, -1)
                keep(same_mask, [[-1, RS]], 0, 1, NEG)
                pool.sem_inc(done["same"], 1)

            def rest_of_pages():
                for n in range(KB, DEC_BATCH * N_PAGES):
                    pool.wait_ge(done["past_kept"], n - KB + 1)
                    load_key(n)
                pool.wait_ge(SC.full, SC.number(("sample", TILES), "past") + 1)
                for n in range(V_FIRST, DEC_BATCH * N_PAGES):
                    load_value(n)

            with pool.Fori(0, TILES - 1) as t:
                gathers(t)
                apart(pool)
            sample_loads()
            gathers(TILES - 1, between=rest_of_pages)
            gathers(TILES, rows=RS)


def kernel(**inputs):
    import concourse.bacc as bacc
    from concourse.bass_utils import run_bass_kernel_spmd

    a = {k: np.asarray(v) for k, v in inputs.items()}
    c = np.ascontiguousarray
    cols = lambda g: g.reshape(-1, P).T
    arrays = {
        "x_all": np.concatenate([a["x_prompt"][0], a["x_sample"].reshape(RS, D), np.zeros((P - RS, D), np.float32)]),
        "page_table": c(a["page_table"].reshape(1, -1)),
        "past_kt": c(a["cache_fox_k"][0].transpose(0, 3, 2, 1).reshape(-1, H_FOX * P)),
        "past_v": a["cache_fox_v"][0].reshape(-1, H_FOX * DH),
        "past_lf": a["cache_fox_logf"][0].reshape(-1, H_FOX),
        "state_in": a["state_gla"][0].reshape(-1, DV),
        "smem_kt": c(a["cache_mem_k"][0].reshape(DEC_BATCH, N_MEM, D).transpose(0, 2, 1).reshape(-1, N_MEM)),
        "smem_v": a["cache_mem_v"][0].reshape(-1, D),
        "mem_prompt": a["mem_prompt"][0],
        "g_cols": c(np.concatenate([cols(a["g_mix"][0]), cols(a["g_cross"][0]), cols(a["g_mem"][0]), cols(a["g_gla_out"][0])], axis=1)),
        "w_in": a["w_in"][0],
        "bias_ls": np.concatenate([a["b_fox_f"][0], a["b_gla_gate"][0]]),
        "w_gate2": a["w_gla_gate2"][0],
        "w_out": a["w_out"][0],
        "w_mem_k": a["w_mem_k"][0], "w_mem_v": a["w_mem_v"][0],
        "w_cross_q": a["w_cross_q"][0], "w_cross_o": a["w_cross_o"][0],
        "g_ffn": a["g_ffn"][0],
        "peer_w_q": a["peer_w_q"][0],
        "subkeys_t": c(a["peer_subkeys"][0].transpose(2, 0, 1)),
        "peer_u": a["peer_u"][0], "peer_v": a["peer_v"][0],
        "g_final": a["g_final"],
    }
    results = {"y": (SEQ + P, D), "fk": (SEQ + RS, H_FOX * DH), "fv": (SEQ + RS, H_FOX * DH), "lf": (SEQ + RS, H_FOX),
               "gs": (H_GLA * DK, DV), "mem_k": (N_MEM, D), "mem_v": (N_MEM, D), "gs_s": (DEC_BATCH * H_GLA * DK, DV)}
    nc = bacc.Bacc("TRN2", target_bir_lowering=False, num_devices=1)
    ins = {k: nc.dram_tensor(k, v.shape, mybir.dt.from_np(v.dtype), kind="ExternalInput").ap() for k, v in arrays.items()}
    outs = {k: nc.dram_tensor("out_" + k, s, F32, kind="ExternalOutput").ap() for k, s in results.items()}
    build(nc, ins, outs)
    r = run_bass_kernel_spmd(nc, [arrays], core_ids=[0]).results[0]
    o = {k: np.asarray(r["out_" + k]) for k in results}
    return (o["y"][:SEQ].reshape(1, SEQ, D), o["y"][SEQ:SEQ + RS].reshape(DEC_BATCH, DEC_SEQ, D),
            o["fk"][:SEQ].reshape(1, 1, SEQ, H_FOX, DH), o["fv"][:SEQ].reshape(1, 1, SEQ, H_FOX, DH),
            o["lf"][:SEQ].reshape(1, 1, SEQ, H_FOX), o["gs"].reshape(1, 1, H_GLA, DK, DV),
            o["mem_k"].reshape(1, 1, N_MEM, H_MEM, DH_MEM), o["mem_v"].reshape(1, 1, N_MEM, H_MEM, DH_MEM),
            o["fk"][SEQ:].reshape(1, DEC_BATCH, DEC_SEQ, H_FOX, DH), o["fv"][SEQ:].reshape(1, DEC_BATCH, DEC_SEQ, H_FOX, DH),
            o["lf"][SEQ:].reshape(1, DEC_BATCH, DEC_SEQ, H_FOX), o["gs_s"].reshape(1, DEC_BATCH, H_GLA, DK, DV))
```
